# Optimizing a Trainium2 kernel written in Bass

```python
import math
import jax, jax.numpy as jnp
from jax import lax
import numpy as np

D_MODEL = 1024
BATCH = 1
SEQ = 1024
DEPTH = 2

GRID_W = 64
CTX_LEN = 256
HEAD_DIM = 64
A_HEADS = 6
A_KV_HEADS = 2
A_GROUP = A_HEADS // A_KV_HEADS
WINDOW = 128
B_HEADS = 4
B_QK_DIM = 32
B_V_DIM = 2 * B_QK_DIM
C_HEADS = 6
C_Q_RANK = 256
C_KV_RANK = 128
C_NOPE = 64
C_ROPE = 32
C_V = 64
MIX_WIDTH = A_HEADS * HEAD_DIM + B_HEADS * B_V_DIM + C_HEADS * C_V
D_FF = 2816
Q_BLOCK = 128
ROPE_BASE = 10000.0
NORM_EPS = 1e-6
NEG_INF = -1e30
A_SCALE = HEAD_DIM ** -0.5
B_SCALE = B_QK_DIM ** -0.5
C_SCALE = (C_NOPE + C_ROPE) ** -0.5
IN_SPLITS = (A_HEADS * HEAD_DIM, A_KV_HEADS * HEAD_DIM, A_KV_HEADS * HEAD_DIM,
             B_HEADS * 2 * B_QK_DIM, B_HEADS * 2 * B_QK_DIM, B_HEADS * B_V_DIM,
             C_Q_RANK, C_KV_RANK, C_ROPE)
D_IN = (A_HEADS * HEAD_DIM + 2 * A_KV_HEADS * HEAD_DIM + 2 * B_HEADS * 2 * B_QK_DIM
        + B_HEADS * B_V_DIM + C_Q_RANK + C_KV_RANK + C_ROPE)

kernel_name = "hybrid_dit_parallel_head_groups"

def rms_norm(x, g):
    xf = x.astype(jnp.float32)
    y = xf * lax.rsqrt(jnp.mean(xf * xf, axis=-1, keepdims=True) + NORM_EPS)
    return (y * g.astype(jnp.float32)).astype(x.dtype)

def modulate(h, shift, scale):
    return h * (1 + scale) + shift

def _rope_1d(x, pos):
    r = x.shape[-1]
    freqs = ROPE_BASE ** (-jnp.arange(0, r, 2, dtype=jnp.float32) / r)
    ang = pos[:, None] * freqs[None, :]
    shape = (1, x.shape[1]) + (1,) * (x.ndim - 3) + (r // 2,)
    cos = jnp.cos(ang).reshape(shape)
    sin = jnp.sin(ang).reshape(shape)
    xf = x.astype(jnp.float32)
    x1, x2 = jnp.split(xf, 2, axis=-1)
    return jnp.concatenate([x1 * cos - x2 * sin, x2 * cos + x1 * sin], axis=-1).astype(x.dtype)

def axial_rope(x, row, col):
    half = x.shape[-1] // 2
    return jnp.concatenate([_rope_1d(x[..., :half], row), _rope_1d(x[..., half:], col)], axis=-1)

def split_in(p):
    outs = []
    start = 0
    for size in IN_SPLITS:
        outs.append(p[..., start:start + size])
        start += size
    return outs

def sweep_query_blocks(fn, q):
    B, n = q.shape[0], q.shape[1]
    nb = n // Q_BLOCK
    qb = jnp.moveaxis(q.reshape((B, nb, Q_BLOCK) + q.shape[2:]), 1, 0)
    out = jnp.moveaxis(lax.map(fn, qb), 0, 1)
    return out.reshape((B, n) + out.shape[3:])

def dense_attend(q, k, v, scale):
    s = jnp.einsum("bqhd,bkhd->bhqk", q, k).astype(jnp.float32) * scale
    p = jax.nn.softmax(s, axis=-1)
    return jnp.einsum("bhqk,bkhd->bqhd", p.astype(v.dtype), v)

def diff_attend(q, k, v, lam):
    s = jnp.einsum("bqhmd,bkhmd->bhmqk", q, k).astype(jnp.float32) * B_SCALE
    p = jax.nn.softmax(s, axis=-1)
    a = p[:, :, 0] - lam * p[:, :, 1]
    return jnp.einsum("bhqk,bkhd->bqhd", a.astype(v.dtype), v)

def windowed_gqa_latent(q, k, v, k_ctx, v_ctx, sink):
    B, S = q.shape[0], q.shape[1]
    nb = S // WINDOW
    qb = q.reshape(B, nb, WINDOW, A_KV_HEADS, A_GROUP, HEAD_DIM)
    pad = ((0, 0), (WINDOW, WINDOW), (0, 0), (0, 0))
    kp = jnp.pad(k, pad).reshape(B, nb + 2, WINDOW, A_KV_HEADS, HEAD_DIM)
    vp = jnp.pad(v, pad).reshape(B, nb + 2, WINDOW, A_KV_HEADS, HEAD_DIM)
    k_band = jnp.concatenate([kp[:, :-2], kp[:, 1:-1], kp[:, 2:]], axis=2)
    v_band = jnp.concatenate([vp[:, :-2], vp[:, 1:-1], vp[:, 2:]], axis=2)
    s_loc = jnp.einsum("bnqkgd,bnjkd->bnkgqj", qb, k_band).astype(jnp.float32) * A_SCALE
    qi = jnp.arange(WINDOW)
    kj = jnp.arange(3 * WINDOW)
    blk = jnp.arange(nb)
    offset = kj[None, :] - WINDOW - qi[:, None]
    key_pos = blk[:, None] * WINDOW - WINDOW + kj[None, :]
    mask = (jnp.abs(offset) <= WINDOW)[None] & ((key_pos >= 0) & (key_pos < S))[:, None, :]
    s_loc = jnp.where(mask[None, :, None, None], s_loc, NEG_INF)
    s_ctx = jnp.einsum("bnqkgd,bckd->bnkgqc", qb, k_ctx).astype(jnp.float32) * A_SCALE
    sink_col = jnp.broadcast_to(sink.astype(jnp.float32).reshape(1, 1, A_KV_HEADS, A_GROUP, 1, 1),
                                s_loc.shape[:-1] + (1,))
    p = jax.nn.softmax(jnp.concatenate([s_loc, s_ctx, sink_col], axis=-1), axis=-1).astype(v.dtype)
    n_loc = 3 * WINDOW
    n_ctx = k_ctx.shape[1]
    o = (jnp.einsum("bnkgqj,bnjkd->bnqkgd", p[..., :n_loc], v_band)
         + jnp.einsum("bnkgqc,bckd->bnqkgd", p[..., n_loc:n_loc + n_ctx], v_ctx))
    return o.reshape(B, S, A_HEADS * HEAD_DIM)

def gqa_context(q, k, v, sink):
    B, C = q.shape[0], q.shape[1]
    qg = q.reshape(B, C, A_KV_HEADS, A_GROUP, HEAD_DIM)
    s = jnp.einsum("bqkgd,bckd->bkgqc", qg, k).astype(jnp.float32) * A_SCALE
    sink_col = jnp.broadcast_to(sink.astype(jnp.float32).reshape(1, A_KV_HEADS, A_GROUP, 1, 1),
                                s.shape[:-1] + (1,))
    p = jax.nn.softmax(jnp.concatenate([s, sink_col], axis=-1), axis=-1).astype(v.dtype)
    o = jnp.einsum("bkgqc,bckd->bqkgd", p[..., :C], v)
    return o.reshape(B, C, A_HEADS * HEAD_DIM)

def mla_qkv(c_q, c_kv, k_r, q_norm, w_q_up, kv_norm, w_kv_up, row, col, use_rope):
    B, n = c_q.shape[0], c_q.shape[1]
    q = (rms_norm(c_q, q_norm) @ w_q_up).reshape(B, n, C_HEADS, C_NOPE + C_ROPE)
    q_nope, q_rope = q[..., :C_NOPE], q[..., C_NOPE:]
    kv = (rms_norm(c_kv, kv_norm) @ w_kv_up).reshape(B, n, C_HEADS, C_NOPE + C_V)
    k_nope, v = kv[..., :C_NOPE], kv[..., C_NOPE:]
    if use_rope:
        q_rope = axial_rope(q_rope, row, col)
        k_r = axial_rope(k_r, row, col)
    k = jnp.concatenate([k_nope, jnp.broadcast_to(k_r[:, :, None, :], (B, n, C_HEADS, C_ROPE))], axis=-1)
    q = jnp.concatenate([q_nope, q_rope], axis=-1)
    return q, k, v

def swiglu(h, w_gate, w_up, w_down):
    return (jax.nn.silu(h @ w_gate) * (h @ w_up)) @ w_down

def hybrid_layer(l, update_ctx, x, ctx, mod_x, mod_c, row, col,
                 g_pre_mix, g_post_mix, w_in, win_sink,
                 diff_lambda_q1, diff_lambda_k1, diff_lambda_q2, diff_lambda_k2, diff_sub_norm,
                 mla_q_norm, mla_w_q_up, mla_kv_norm, mla_w_kv_up,
                 w_out, g_pre_ffn, g_post_ffn, w_gate, w_up, w_down):
    B, S = x.shape[0], x.shape[1]
    C = ctx.shape[1]
    sh_m, sc_m, gt_m, sh_f, sc_f, gt_f = jnp.split(mod_x, 6, axis=-1)
    csh_m, csc_m, cgt_m, csh_f, csc_f, cgt_f = jnp.split(mod_c, 6, axis=-1)

    h_x = modulate(rms_norm(x, g_pre_mix), sh_m, sc_m)
    h_c = modulate(rms_norm(ctx, g_pre_mix), csh_m, csc_m)
    ax_q, ax_k, ax_v, dx_q, dx_k, dx_v, mx_q, mx_kv, mx_kr = split_in(h_x @ w_in)
    ac_q, ac_k, ac_v, dc_q, dc_k, dc_v, mc_q, mc_kv, mc_kr = split_in(h_c @ w_in)

    qa_x = axial_rope(ax_q.reshape(B, S, A_HEADS, HEAD_DIM), row, col)
    ka_x = axial_rope(ax_k.reshape(B, S, A_KV_HEADS, HEAD_DIM), row, col)
    va_x = ax_v.reshape(B, S, A_KV_HEADS, HEAD_DIM)
    ka_c = ac_k.reshape(B, C, A_KV_HEADS, HEAD_DIM)
    va_c = ac_v.reshape(B, C, A_KV_HEADS, HEAD_DIM)
    o_a = windowed_gqa_latent(qa_x, ka_x, va_x, ka_c, va_c, win_sink)

    lam_init = 0.8 - 0.6 * math.exp(-0.3 * l)
    lam = (jnp.exp(jnp.sum(diff_lambda_q1.astype(jnp.float32) * diff_lambda_k1.astype(jnp.float32)))
           - jnp.exp(jnp.sum(diff_lambda_q2.astype(jnp.float32) * diff_lambda_k2.astype(jnp.float32)))
           + lam_init)
    qd_x = axial_rope(dx_q.reshape(B, S, B_HEADS, 2, B_QK_DIM), row, col)
    kd_x = axial_rope(dx_k.reshape(B, S, B_HEADS, 2, B_QK_DIM), row, col)
    vd_x = dx_v.reshape(B, S, B_HEADS, B_V_DIM)
    kd_c = dc_k.reshape(B, C, B_HEADS, 2, B_QK_DIM)
    vd_c = dc_v.reshape(B, C, B_HEADS, B_V_DIM)
    kd_all = jnp.concatenate([kd_x, kd_c], axis=1)
    vd_all = jnp.concatenate([vd_x, vd_c], axis=1)
    o_b = sweep_query_blocks(lambda qb: diff_attend(qb, kd_all, vd_all, lam), qd_x)
    o_b = (rms_norm(o_b, diff_sub_norm) * (1.0 - lam_init)).reshape(B, S, B_HEADS * B_V_DIM)

    qm_x, km_x, vm_x = mla_qkv(mx_q, mx_kv, mx_kr, mla_q_norm, mla_w_q_up, mla_kv_norm, mla_w_kv_up,
                               row, col, True)
    qm_c, km_c, vm_c = mla_qkv(mc_q, mc_kv, mc_kr, mla_q_norm, mla_w_q_up, mla_kv_norm, mla_w_kv_up,
                               None, None, False)
    km_all = jnp.concatenate([km_x, km_c], axis=1)
    vm_all = jnp.concatenate([vm_x, vm_c], axis=1)
    o_c = sweep_query_blocks(lambda qb: dense_attend(qb, km_all, vm_all, C_SCALE), qm_x)
    o_c = o_c.reshape(B, S, C_HEADS * C_V)

    mix_x = jnp.concatenate([o_a, o_b, o_c], axis=-1) @ w_out
    x = x + gt_m * rms_norm(mix_x, g_post_mix)
    h = modulate(rms_norm(x, g_pre_ffn), sh_f, sc_f)
    x = x + gt_f * rms_norm(swiglu(h, w_gate, w_up, w_down), g_post_ffn)

    if update_ctx:
        o_a_c = gqa_context(ac_q.reshape(B, C, A_HEADS, HEAD_DIM), ka_c, va_c, win_sink)
        o_b_c = diff_attend(dc_q.reshape(B, C, B_HEADS, 2, B_QK_DIM), kd_c, vd_c, lam)
        o_b_c = (rms_norm(o_b_c, diff_sub_norm) * (1.0 - lam_init)).reshape(B, C, B_HEADS * B_V_DIM)
        o_c_c = dense_attend(qm_c, km_c, vm_c, C_SCALE).reshape(B, C, C_HEADS * C_V)
        mix_c = jnp.concatenate([o_a_c, o_b_c, o_c_c], axis=-1) @ w_out
        ctx = ctx + cgt_m * rms_norm(mix_c, g_post_mix)
        hc = modulate(rms_norm(ctx, g_pre_ffn), csh_f, csc_f)
        ctx = ctx + cgt_f * rms_norm(swiglu(hc, w_gate, w_up, w_down), g_post_ffn)
    return x, ctx

def setup_inputs(seed: int = 0) -> dict:
    key = jax.random.key(seed)
    ks = jax.random.split(key, 26)

    def normal(k, shape, scale):
        return scale * jax.random.normal(k, shape, jnp.float32)

    def gain(k, shape):
        return 1.0 + 0.05 * jax.random.normal(k, shape, jnp.float32)

    return {
        "x": normal(ks[0], (BATCH, SEQ, D_MODEL), 1.0),
        "c": normal(ks[1], (BATCH, D_MODEL), 1.0),
        "ctx": normal(ks[2], (BATCH, CTX_LEN, D_MODEL), 1.0),
        "c_ctx": normal(ks[3], (D_MODEL,), 1.0),
        "w_ada": normal(ks[4], (DEPTH, D_MODEL, 6 * D_MODEL), 0.5 * D_MODEL ** -0.5),
        "b_ada": normal(ks[5], (DEPTH, 6 * D_MODEL), 0.02),
        "g_pre_mix": gain(ks[6], (DEPTH, D_MODEL)),
        "g_post_mix": gain(ks[7], (DEPTH, D_MODEL)),
        "w_in": normal(ks[8], (DEPTH, D_MODEL, D_IN), D_MODEL ** -0.5),
        "win_sink": normal(ks[9], (DEPTH, A_HEADS), 0.5),
        "diff_lambda_q1": normal(ks[10], (DEPTH, B_QK_DIM), 0.1),
        "diff_lambda_k1": normal(ks[11], (DEPTH, B_QK_DIM), 0.1),
        "diff_lambda_q2": normal(ks[12], (DEPTH, B_QK_DIM), 0.1),
        "diff_lambda_k2": normal(ks[13], (DEPTH, B_QK_DIM), 0.1),
        "diff_sub_norm": gain(ks[14], (DEPTH, B_V_DIM)),
        "mla_q_norm": gain(ks[15], (DEPTH, C_Q_RANK)),
        "mla_w_q_up": normal(ks[16], (DEPTH, C_Q_RANK, C_HEADS * (C_NOPE + C_ROPE)), C_Q_RANK ** -0.5),
        "mla_kv_norm": gain(ks[17], (DEPTH, C_KV_RANK)),
        "mla_w_kv_up": normal(ks[18], (DEPTH, C_KV_RANK, C_HEADS * (C_NOPE + C_V)), C_KV_RANK ** -0.5),
        "w_out": normal(ks[19], (DEPTH, MIX_WIDTH, D_MODEL), MIX_WIDTH ** -0.5),
        "g_pre_ffn": gain(ks[20], (DEPTH, D_MODEL)),
        "g_post_ffn": gain(ks[21], (DEPTH, D_MODEL)),
        "w_gate": normal(ks[22], (DEPTH, D_MODEL, D_FF), D_MODEL ** -0.5),
        "w_up": normal(ks[23], (DEPTH, D_MODEL, D_FF), D_MODEL ** -0.5),
        "w_down": normal(ks[24], (DEPTH, D_FF, D_MODEL), D_FF ** -0.5),
    }

def reference(x, c, ctx, c_ctx, w_ada, b_ada, g_pre_mix, g_post_mix, w_in, win_sink,
              diff_lambda_q1, diff_lambda_k1, diff_lambda_q2, diff_lambda_k2, diff_sub_norm,
              mla_q_norm, mla_w_q_up, mla_kv_norm, mla_w_kv_up, w_out,
              g_pre_ffn, g_post_ffn, w_gate, w_up, w_down):
    n = x.shape[1]
    rows = n // GRID_W
    row = jnp.repeat(jnp.arange(rows, dtype=jnp.float32), GRID_W)
    col = jnp.tile(jnp.arange(GRID_W, dtype=jnp.float32), rows)
    for l in range(DEPTH):
        mod_x = (jax.nn.silu(c) @ w_ada[l] + b_ada[l])[:, None, :]
        mod_c = (jax.nn.silu(c_ctx) @ w_ada[l] + b_ada[l])[None, None, :]
        x, ctx = hybrid_layer(l, l < DEPTH - 1, x, ctx, mod_x, mod_c, row, col,
                              g_pre_mix[l], g_post_mix[l], w_in[l], win_sink[l],
                              diff_lambda_q1[l], diff_lambda_k1[l], diff_lambda_q2[l], diff_lambda_k2[l],
                              diff_sub_norm[l], mla_q_norm[l], mla_w_q_up[l], mla_kv_norm[l],
                              mla_w_kv_up[l], w_out[l], g_pre_ffn[l], g_post_ffn[l],
                              w_gate[l], w_up[l], w_down[l])
    return x


_drawn_inputs = setup_inputs


def setup_inputs(seed=0):
    import zlib

    import numpy as np

    out = dict(_drawn_inputs(seed))
    spreads = {}
    factors = {'g_pre_mix': 3.56,
     'win_sink': 64.0,
     'diff_lambda_q1': 2.978,
     'diff_lambda_k1': 3.243,
     'diff_lambda_q2': 4.068,
     'diff_lambda_k2': 3.184,
     'diff_sub_norm': 14.914,
     'mla_q_norm': 8.0,
     'mla_kv_norm': 6.113,
     'g_post_ffn': 2.82}
    for name, (base, spread) in spreads.items():
        noise = np.random.default_rng([zlib.crc32(name.encode()), seed]).standard_normal(out[name].shape)
        drawn = base * np.exp(spread * noise) if base else spread * noise
        out[name] = __import__('jax').numpy.asarray(drawn.astype(out[name].dtype))
    for name, factor in factors.items():
        out[name] = (out[name] * factor).astype(out[name].dtype)
    return out
```

```python
from contextlib import ExitStack
import math

import numpy as np
import concourse.bass as bass
from concourse import mybir
from concourse.alu_op_type import AluOpType as ALU

F32 = mybir.dt.float32
F32R = mybir.dt.float32r
BF16 = mybir.dt.bfloat16
ACT = mybir.ActivationFunctionType
AX_X = mybir.AxisListType.X

P = 128
BANK = 512
D = 1024
KT = D // P
SEQ, CTX = 1024, 256
TX, TC = SEQ // P, CTX // P
TT = TX + TC
TOK = SEQ + CTX
DEPTH = 2
GRID_W = 64
EPS = 1e-6
NEG = -1e30
D_IN = 1824
QR, KVR = 256, 128
QUP, KVUP = 576, 768
VW = 768
DFF = 2816
FT = DFF // P
A_SCALE, B_SCALE, C_SCALE = 64 ** -0.5, 32 ** -0.5, 96 ** -0.5

IN_AQ, IN_AV, IN_BQ, IN_BV, IN_CQ, IN_CKV, IN_KR = 0, 512, 640, 1152, 1408, 1664, 1792
IN_BANKS = (0, 512, 1024, 1408, D_IN)
PJ_CQ, PJ_CKV, PJ_KR, PJ_END = (3 * BANK + c - IN_CQ for c in (IN_CQ, IN_CKV, IN_KR, D_IN))
R_AQ, R_AK, R_BQ, R_BK, R_CQ, R_CN, R_KR, R_ALL = 0, 384, 512, 768, 1024, 1600, 1984, 2048
V_A, V_B, V_C = 0, 128, 384


def lam_init(l):
    return 0.8 - 0.6 * math.exp(-0.3 * l)


def raw(ap):
    return ap.bitcast(F32)


def heads_of(ap, heads):
    return ap.rearrange("p (h e) -> p h e", h=heads)


class Scope:

    def __init__(self, nc, ctx, tag):
        self.nc, self.ctx, self.tag = nc, ctx, tag
        self.sems = []
        ctx.callback(self.close)

    def close(self):
        if self.sems:
            self.nc.clear_and_free_semaphores(self.sems)
            self.nc.all_engine_barrier()

    def sb(self, name, shape, dt=F32):
        return self.ctx.enter_context(self.nc.sbuf_tensor(f"{self.tag}_{name}", shape, dt))

    def ps(self, name, shape, dt=F32):
        return self.ctx.enter_context(self.nc.psum_tensor(f"{self.tag}_{name}", shape, dt))

    def sem(self, name):
        self.sems.append(self.nc.alloc_semaphore(f"{self.tag}_{name}"))
        return self.sems[-1]


def three_pass(pe, out, w_hi, w_lo, m_hi, m_lo, first, last):
    pe.matmul(out, w_hi, m_hi, start=first, stop=False)
    pe.matmul(out, w_hi, m_lo, start=False, stop=False)
    return pe.matmul(out, w_lo, m_hi, start=False, stop=last)


def modulation(nc, t, dr, keep):
    NCH = 6 * D // BANK
    RING = 4
    with ExitStack() as ctx:
        s = Scope(nc, ctx, "mod")
        cT = s.sb("cT", [P, 2, KT])
        sT = s.sb("sT", [P, 2, KT])
        bias = s.sb("bias", [2, DEPTH, 6 * D])
        rows = s.sb("rows", [2, DEPTH, 6 * D])
        gpost = s.sb("gpost", [2, DEPTH, 2, D])
        gpreT = s.sb("gpreT", [P, DEPTH, 2, KT])
        wring = s.sb("wring", [P, RING, KT, BANK])
        lamv = s.sb("lamv", [P, 4, DEPTH, 32])
        lamj = s.sb("lamj", [P, 2, DEPTH, 32])
        lamd = s.sb("lamd", [P, 2, DEPTH])
        lame = s.sb("lame", [P, 2, DEPTH])
        dsnr = s.sb("dsnr", [64, DEPTH])
        pm = s.ps("pm", [P, 2, BANK])
        pT = s.ps("pT", [P, BANK])
        cols_loaded, vecs_loaded = s.sem("cols_loaded"), keep["vecs_loaded"]
        w_loaded = [s.sem(f"w_loaded{i}") for i in range(RING)]
        silu_done, consts_done, chunk_summed, row_done = (
            s.sem("silu_done"), s.sem("consts_done"), s.sem("chunk_summed"), s.sem("row_done"))
        turned, lam_dots, lam_exp, own, stored = (
            s.sem("turned"), s.sem("lam_dots"), s.sem("lam_exp"), s.sem("own"), s.sem("stored"))
        ones = s.sb("ones", [1, TOK], F32R)
        ones_done = s.sem("ones_done")
        block = ctx.enter_context(nc.Block())
        NVEC = 13

        @block.sync
        def _(sp):
            sp.dma_start(cT[:, 0, :], t["c"].rearrange("o (k p) -> p (o k)", p=P),
                         allow_slow_non_contiguous=True).then_inc(cols_loaded, 16)
            sp.dma_start(cT[:, 1, :], t["c_ctx"].rearrange("(k p) -> p k", p=P),
                         allow_slow_non_contiguous=True).then_inc(cols_loaded, 16)
            for i in range(DEPTH * NCH):
                l, n = divmod(i, NCH)
                if i >= RING:
                    sp.wait_ge(chunk_summed, i - RING + 1)
                sp.dma_start(wring[:, i % RING, :, :],
                             t["w_ada"][l, :, n * BANK:(n + 1) * BANK].rearrange("(k p) n -> p k n", p=P)
                             ).then_inc(w_loaded[i % RING], 16)
            sp.wait_ge(own, 2 * DEPTH + 4)
            for l in range(DEPTH):
                for j in range(2):
                    sp.dma_start(dr["gate"][l, j], gpost[:, l, j, :]).then_inc(stored, 16)
            sp.wait_ge(ones_done, 1)
            sp.dma_start(dr["ones"], raw(ones[:])).then_inc(stored, 16)
            sp.wait_ge(stored, 16 * (2 * DEPTH + 1))

        @block.gpsimd
        def _(pool):
            pool.memset(raw(ones[:]), 1.0).then_inc(ones_done, 1)
            pool.memset(keep["ident"][:], 0.0).then_inc(consts_done, 1)
            pool.memset(keep["identb"][:], 0.0).then_inc(consts_done, 1)
            pool.memset(keep["above"][:], 0.0).then_inc(consts_done, 1)
            pool.memset(keep["below"][:], 0.0).then_inc(consts_done, 1)
            pool.wait_ge(consts_done, 4)
            for m in (keep["ident"], keep["identb"]):
                pool.affine_select(out=m[:], in_=m[:], compare_op=ALU.not_equal, fill=1.0, base=0,
                                   pattern=[[-1, P]], channel_multiplier=1).then_inc(consts_done, 1)
            pool.affine_select(out=keep["above"][:], in_=keep["above"][:], compare_op=ALU.is_ge, fill=NEG, base=0,
                               pattern=[[-1, P]], channel_multiplier=1).then_inc(consts_done, 1)
            pool.affine_select(out=keep["below"][:], in_=keep["below"][:], compare_op=ALU.is_ge, fill=NEG, base=0,
                               pattern=[[1, P]], channel_multiplier=-1).then_inc(consts_done, 1)
            pool.memset(keep["eps"][:], EPS).then_inc(consts_done, 1)
            pool.memset(keep["mhalf"][:], -0.5).then_inc(consts_done, 1)
            pool.dma_start(bias[:], t["b_ada"].partition_broadcast(2)).then_inc(vecs_loaded, 16)
            for j, name in enumerate(("g_post_mix", "g_post_ffn")):
                pool.dma_start(gpost[:, :, j, :], t[name].partition_broadcast(2)).then_inc(vecs_loaded, 16)
            for j, name in enumerate(("g_pre_mix", "g_pre_ffn")):
                for l in range(DEPTH):
                    pool.dma_start(gpreT[:, l, j, :], t[name][l].rearrange("(k p) -> p k", p=P),
                                   allow_slow_non_contiguous=True
                                   ).then_inc(vecs_loaded, 16)
            for j, name in enumerate(("diff_lambda_q1", "diff_lambda_k1", "diff_lambda_q2", "diff_lambda_k2")):
                pool.dma_start(lamv[:, j, :, :], t[name].partition_broadcast(P)).then_inc(vecs_loaded, 16)
            pool.dma_start(keep["sink"][:], t["win_sink"].partition_broadcast(P)).then_inc(vecs_loaded, 16)
            pool.dma_start(dsnr[:], t["diff_sub_norm"].rearrange("l v -> v l"),
                           allow_slow_non_contiguous=True).then_inc(vecs_loaded, 16)
            for l in range(DEPTH):
                pool.dma_start(keep["cnorm"][:, l, 0:2], t["mla_q_norm"][l].rearrange("(k p) -> p k", p=P),
                               allow_slow_non_contiguous=True
                               ).then_inc(vecs_loaded, 16)
                pool.dma_start(keep["cnorm"][:, l, 2:3], t["mla_kv_norm"][l].rearrange("(k p) -> p k", p=P),
                               allow_slow_non_contiguous=True
                               ).then_inc(vecs_loaded, 16)
            pool.wait_ge(vecs_loaded, 16 * (NVEC + 4))

        @block.scalar
        def _(act):
            act.wait_ge(cols_loaded, 32)
            act.activation(sT[:], cT[:], ACT.Silu).then_inc(silu_done, 1)
            act.wait_ge(lam_dots, 2 * DEPTH)
            act.activation(lame[:], lamd[:], ACT.Exp).then_inc(lam_exp, 1)

        @block.tensor
        def _(pe):
            pe.wait_ge(silu_done, 1)
            for i in range(DEPTH * NCH):
                pe.wait_ge(w_loaded[i % RING], 16 * (i // RING + 1))
                if i >= 2:
                    pe.wait_ge(row_done, i - 1)
                for k in range(KT):
                    mm = pe.matmul(pm[0:2, i % 2, :], sT[:, :, k], wring[:, i % RING, k, :],
                                   start=(k == 0), stop=(k == KT - 1))
                mm.then_inc(chunk_summed, 1)
            pe.wait_ge(row_done, DEPTH * NCH)
            pe.wait_ge(consts_done, 10)
            for l in range(DEPTH):
                for j, part in enumerate((0, 1, 3, 4)):
                    for k in range(KT):
                        at = ((l * 4 + j) * KT + k) * 2
                        mm = pe.transpose(pT[:, at:at + 2], rows[:, l, part * D + k * P:part * D + (k + 1) * P],
                                          keep["ident"][0:2, 0:2])
            mm.then_inc(turned, 1)

        @block.vector
        def _(dve):
            dve.wait_ge(vecs_loaded, 16 * (NVEC + 4))
            for l in range(DEPTH):
                for j in range(2):
                    dve.tensor_tensor_reduce(lamj[:, j, l, :], lamv[:, 2 * j, l, :], lamv[:, 2 * j + 1, l, :],
                                             1.0, 0.0, ALU.mult, ALU.add, lamd[:, j, l:l + 1]).then_inc(lam_dots, 1)
            for i in range(DEPTH * NCH):
                l, n = divmod(i, NCH)
                c = slice(n * BANK, (n + 1) * BANK)
                dve.wait_ge(chunk_summed, i + 1)
                dve.tensor_tensor(rows[:, l, c], pm[0:2, i % 2, :], bias[:, l, c], ALU.add).then_inc(row_done, 1)
            dve.wait_ge(row_done, DEPTH * NCH)
            for l in range(DEPTH):
                for j, part in enumerate((2, 5)):
                    dve.tensor_tensor(gpost[:, l, j, :], rows[:, l, part * D:(part + 1) * D], gpost[:, l, j, :],
                                      ALU.mult).then_inc(own, 1)
            dve.wait_ge(lam_exp, 1)
            for l in range(DEPTH):
                dve.scalar_tensor_tensor(out=keep["neglam"][:, l:l + 1], in0=lame[:, 1, l:l + 1], scalar=-lam_init(l),
                                         in1=lame[:, 0, l:l + 1], op0=ALU.add, op1=ALU.subtract).then_inc(own, 1)
                dve.tensor_scalar(keep["dsn"][:, l:l + 1], dsnr[:, l:l + 1], 1.0 - lam_init(l), None,
                                  ALU.mult).then_inc(own, 1)
            dve.tensor_scalar(keep["sinkdiv"][:], keep["sink"][:], 1.0 / A_SCALE, None, ALU.mult)
            dve.wait_ge(turned, 1)
            view = pT[:, 0:DEPTH * 4 * KT * 2].rearrange("p (l j k c) -> p l j k c", l=DEPTH, j=4, k=KT)
            for l in range(DEPTH):
                for j in range(2):
                    dve.tensor_copy(keep["modT"][:, l, 2 * j], view[:, l, 2 * j])
                    dve.scalar_tensor_tensor(out=keep["modT"][:, l, 2 * j + 1], in0=view[:, l, 2 * j + 1], scalar=1.0,
                                             in1=gpreT[:, l, j, :].unsqueeze(2).to_broadcast([P, KT, 2]),
                                             op0=ALU.add, op1=ALU.mult)


def split_weights(nc, tag, pieces, ring_cols):
    RING = 4
    with ExitStack() as ctx:
        s = Scope(nc, ctx, tag)
        ring = s.sb("ring", [P, RING, ring_cols])
        loaded = [s.sem(f"loaded{i}") for i in range(RING)]
        hi_done, lo_done = s.sem("hi_done"), s.sem("lo_done")
        block = ctx.enter_context(nc.Block())

        def slot(i, n):
            return ring[:, i % RING, 0:n]

        @block.sync
        def _(sp):
            for i, (src, hi, lo) in enumerate(pieces):
                if i >= RING:
                    sp.wait_ge(lo_done, i - RING + 1)
                sp.dma_start(slot(i, hi.shape[-1]), src).then_inc(loaded[i % RING], 16)

        @block.scalar
        def _(act):
            for i, (src, hi, lo) in enumerate(pieces):
                act.wait_ge(loaded[i % RING], 16 * (i // RING + 1))
                act.copy(hi, slot(i, hi.shape[-1])).then_inc(hi_done, 1)

        @block.vector
        def _(dve):
            for i, (src, hi, lo) in enumerate(pieces):
                dve.wait_ge(hi_done, i + 1)
                dve.wait_ge(loaded[i % RING], 16 * (i // RING + 1))
                dve.tensor_tensor(lo, slot(i, hi.shape[-1]), raw(hi), ALU.subtract).then_inc(lo_done, 1)


def project(nc, t, dr, keep, l):
    with ExitStack() as outer:
        w = Scope(nc, outer, f"pw{l}")
        win_hi, win_lo = w.sb("win_hi", [P, KT, D_IN], F32R), w.sb("win_lo", [P, KT, D_IN], F32R)
        wq_hi, wq_lo = w.sb("wq_hi", [P, 2, QUP], F32R), w.sb("wq_lo", [P, 2, QUP], F32R)
        wkv_hi, wkv_lo = w.sb("wkv_hi", [P, KVUP], F32R), w.sb("wkv_lo", [P, KVUP], F32R)
        pieces = [(t["w_in"][l, k * P:(k + 1) * P, :], win_hi[:, k, :], win_lo[:, k, :]) for k in range(KT)]
        pieces += [(t["mla_w_q_up"][l, k * P:(k + 1) * P, :], wq_hi[:, k, :], wq_lo[:, k, :]) for k in range(2)]
        pieces += [(t["mla_w_kv_up"][l], wkv_hi[:], wkv_lo[:])]
        split_weights(nc, f"ps{l}", pieces, D_IN)
        with ExitStack() as ctx:
            s = Scope(nc, ctx, f"pj{l}")
            xt = s.sb("xt", [P, 2, D])
            junk = s.sb("junk", [P, D], BF16)
            junk_c = s.sb("junk_c", [P, 384], BF16)
            hT_hi, hT_lo = s.sb("hT_hi", [P, 2, KT, P], F32R), s.sb("hT_lo", [P, 2, KT, P], F32R)
            R = s.sb("R", [P, R_ALL])
            T_hi, T_lo = s.sb("T_hi", [P, 16, P], F32R), s.sb("T_lo", [P, 16, P], F32R)
            V_hi, V_lo = s.sb("V_hi", [P, VW], F32R), s.sb("V_lo", [P, VW], F32R)
            cn = s.sb("cn", [P, 384])
            cT_hi, cT_lo = s.sb("cT_hi", [P, 3, P], F32R), s.sb("cT_lo", [P, 3, P], F32R)
            rot64, rot32 = s.sb("rot64", [P, 2, TX, 64]), s.sb("rot32", [P, 2, TX, 32])
            turn = s.sb("turn", [P, 512])
            ss, ms, rs = s.sb("ss", [P, 2, 4]), s.sb("ms", [P, 2, 4]), s.sb("rs", [P, 2, 4])
            pj = s.ps("pj", [P, 4 * BANK])
            pt = s.ps("pt", [P, 2 * BANK])
            pu = s.ps("pu", [P, 2 * BANK])
            x_loaded = [s.sem("x_loaded0"), s.sem("x_loaded1")]
            names = ("rot_loaded x_squared x_rms x_normed h_turned h_full h_hi h_lo proj_done c_squared "
                     " c_rms c_normed c_turned c_full c_hi c_lo q_up kv_up q_read_dve "
                     "q_read_act kv_read_dve kv_read_act r_turned t_hi t_lo v_hi v_lo pool_own dve_own t_stored v_stored "
                     "ropeA_done ropeB_done kr_done")
            S = {n: s.sem(n) for n in names.split()}
            block = ctx.enter_context(nc.Block())

            def src(i):
                if l == 0:
                    return t["x"][0, i * P:(i + 1) * P, :] if i < TX else t["ctx"][0, (i - TX) * P:(i - TX + 1) * P, :]
                return dr["x"][i * P:(i + 1) * P, :]

            def store(sp, i):
                sp.wait_ge(S["v_hi"], 3 * (i + 1))
                sp.wait_ge(S["v_lo"], 3 * (i + 1))
                for j, v in enumerate((V_hi, V_lo)):
                    sp.dma_start(dr["V"][j, i * P:(i + 1) * P, :], raw(v[:])).then_inc(S["v_stored"], 16)
                sp.wait_ge(S["t_hi"], 4 * (i + 1))
                sp.wait_ge(S["t_lo"], 4 * (i + 1))
                for j, v in enumerate((T_hi, T_lo)):
                    sp.dma_start(dr["T"][j, :, i * P:(i + 1) * P].rearrange("(b p) n -> p b n", p=P),
                                 raw(v[:])).then_inc(S["t_stored"], 16)

            @block.sync
            def _(sp):
                sp.dma_start(rot64[:], t["rot64"]).then_inc(S["rot_loaded"], 16)
                sp.dma_start(rot32[:], t["rot32"]).then_inc(S["rot_loaded"], 16)
                for i in range(TT):
                    if i >= 2:
                        sp.wait_ge(S["h_lo"], i - 1)
                    sp.dma_start(xt[:, i % 2, :], src(i)).then_inc(x_loaded[i % 2], 16)
                    if i >= 2:
                        store(sp, i - 2)
                store(sp, TT - 2)
                store(sp, TT - 1)
                sp.wait_ge(S["t_stored"], 32 * TT)
                sp.wait_ge(S["v_stored"], 32 * TT)

            @block.gpsimd
            def _(pool):
                own = 0

                def rsqrt(cols, i, divs):
                    nonlocal own
                    b = i % 2
                    for c, n in zip(cols, divs):
                        pool.tensor_scalar(ms[:, b, c:c + 1], ss[:, b, c:c + 1], 1.0 / n, EPS, ALU.mult, ALU.add
                                           ).then_inc(S["pool_own"], 1)
                        own += 1
                    pool.wait_ge(S["pool_own"], own)
                    lo, hi = cols[0], cols[-1] + 1
                    return pool.tensor_tensor(rs[:, b, lo:hi], ms[:, b, lo:hi],
                                              keep["mhalf"][:, 0:hi - lo], ALU.pow)

                def x_rms(i):
                    pool.wait_ge(S["x_squared"], i + 1)
                    if i >= 2:
                        pool.wait_ge(S["x_normed"], i - 1)
                    rsqrt([0], i, [D]).then_inc(S["x_rms"], 1)

                x_rms(0)
                for i in range(TT):
                    if i + 1 < TT:
                        x_rms(i + 1)
                    pool.wait_ge(S["c_squared"], 2 * (i + 1))
                    if i >= 2:
                        pool.wait_ge(S["c_normed"], i - 1)
                    rsqrt([1, 2], i, [QR, KVR]).then_inc(S["c_rms"], 1)

            @block.scalar
            def _(act):
                def x_norm(i):
                    b = i % 2
                    act.wait_ge(x_loaded[b], 16 * (i // 2 + 1))
                    if i >= 2:
                        act.wait_ge(S["x_rms"], i - 1)
                    act.activation(junk[:], xt[:, b, :], ACT.Square, accum_out=ss[:, b, 0:1]
                                   ).then_inc(S["x_squared"], 1)
                    act.wait_ge(S["x_rms"], i + 1)
                    act.activation(xt[:, b, :], xt[:, b, :], ACT.Copy, scale=rs[:, b, 0:1]
                                   ).then_inc(S["x_normed"], 1)

                def h_split(i):
                    act.wait_ge(S["h_full"], i + 1)
                    if i >= 2:
                        act.wait_ge(S["proj_done"], 4 * (i - 1))
                    act.copy(hT_hi[:, i % 2].rearrange("p k n -> p (k n)"), xt[:, i % 2, :]).then_inc(S["h_hi"], 1)

                def r_split(i, g, bank):
                    act.wait_ge(S["r_turned"], 4 * i + g + 1)
                    if g == 0 and i >= 1:
                        act.wait_ge(S["t_stored"], 32 * i)
                    act.copy(T_hi[:, 4 * g:4 * g + 4].rearrange("p b n -> p (b n)"), bank).then_inc(S["t_hi"], 1)

                def latent(i):
                    act.wait_ge(S["c_full"], i + 1)
                    if i >= 1:
                        act.wait_ge(S["kv_up"], i)
                    act.copy(cT_hi[:].rearrange("p k n -> p (k n)"), cn[:]).then_inc(S["c_hi"], 1)
                    r_split(i, 0, pt[:, BANK:2 * BANK])
                    r_split(i, 1, pu[:, 0:BANK])
                    act.wait_ge(S["q_up"], i + 1)
                    if i >= 1:
                        act.wait_ge(S["r_turned"], 4 * i)
                    act.copy(heads_of(R[:, R_CQ:R_CN], 6)[:, :, 0:64], heads_of(pu[:, 0:QUP], 6)[:, :, 0:64]
                             ).then_inc(S["q_read_act"], 1)
                    act.wait_ge(S["kv_up"], i + 1)
                    kv = heads_of(pt[:, 0:KVUP], 6)
                    act.copy(heads_of(R[:, R_CN:R_KR], 6), kv[:, :, 0:64]).then_inc(S["kv_read_act"], 1)
                    act.copy(heads_of(V_hi[:, V_C:VW], 6), kv[:, :, 64:128]).then_inc(S["v_hi"], 1)

                x_norm(0)
                h_split(0)
                for i in range(TT):
                    if i + 1 < TT:
                        x_norm(i + 1)
                    if i >= 1:
                        latent(i - 1)
                    if i + 1 < TT:
                        h_split(i + 1)
                    if i >= 1:
                        r_split(i - 1, 2, pu[:, 0:BANK])
                        r_split(i - 1, 3, pu[:, BANK:2 * BANK])
                    act.wait_ge(S["proj_done"], 4 * i + 2)
                    if i >= 1:
                        act.wait_ge(S["v_stored"], 32 * i)
                    act.copy(V_hi[:, V_A:V_B], pj[:, IN_AV:IN_BQ]).then_inc(S["v_hi"], 1)
                    act.wait_ge(S["proj_done"], 4 * i + 3)
                    act.copy(V_hi[:, V_B:V_C], pj[:, IN_BV:IN_CQ]).then_inc(S["v_hi"], 1)
                    act.wait_ge(S["proj_done"], 4 * i + 4)
                    if i >= 1:
                        act.wait_ge(S["c_rms"], i)
                    act.activation(junk_c[:, 0:QR], pj[:, PJ_CQ:PJ_CKV], ACT.Square, accum_out=ss[:, i % 2, 1:2]
                                   ).then_inc(S["c_squared"], 1)
                    act.activation(junk_c[:, QR:384], pj[:, PJ_CKV:PJ_KR], ACT.Square, accum_out=ss[:, i % 2, 2:3]
                                   ).then_inc(S["c_squared"], 1)
                latent(TT - 1)
                r_split(TT - 1, 2, pu[:, 0:BANK])
                r_split(TT - 1, 3, pu[:, BANK:2 * BANK])

            @block.tensor
            def _(pe):
                def h_turn(i):
                    pe.wait_ge(S["x_normed"], i + 1)
                    if i >= 1:
                        pe.wait_ge(S["h_full"], i)
                    if i >= 2:
                        pe.wait_ge(S["kv_read_act"], i - 1)
                        pe.wait_ge(S["v_hi"], 3 * (i - 1))
                        pe.wait_ge(S["v_lo"], 3 * (i - 1))
                    for k in range(KT):
                        mm = pe.transpose(pt[:, k * P:(k + 1) * P], xt[:, i % 2, k * P:(k + 1) * P], keep["ident"][:])
                    mm.then_inc(S["h_turned"], 1)

                def proj(i, n):
                    a, b = IN_BANKS[n], IN_BANKS[n + 1]
                    if n == 0:
                        pe.wait_ge(S["h_hi"], i + 1)
                        pe.wait_ge(S["h_lo"], i + 1)
                        if i >= 1:
                            pe.wait_ge(S["ropeA_done"], i)
                    if n == 1 and i >= 1:
                        pe.wait_ge(S["c_normed"], i)
                        pe.wait_ge(S["c_squared"], 2 * i)
                    for k in range(KT):
                        mm = three_pass(pe, pj[:, n * BANK:n * BANK + b - a], hT_hi[:, i % 2, k, :], hT_lo[:, i % 2, k, :],
                                        win_hi[:, k, a:b], win_lo[:, k, a:b], k == 0, k == KT - 1)
                    mm.then_inc(S["proj_done"], 1)

                def r_turn(i, g, bank):
                    for b in range(4):
                        c = (4 * g + b) * P
                        mm = pe.transpose(bank[:, b * P:(b + 1) * P], R[:, c:c + P], keep["ident"][:])
                    mm.then_inc(S["r_turned"], 1)

                def latent(i, step):
                    if step == 0:
                        pe.wait_ge(S["c_normed"], i + 1)
                        pe.wait_ge(S["h_full"], min(i + 2, TT))
                        for k in range(3):
                            mm = pe.transpose(pt[:, k * P:(k + 1) * P], cn[:, k * P:(k + 1) * P], keep["ident"][:])
                        mm.then_inc(S["c_turned"], 1)
                        r_turn(i, 0, pt[:, BANK:2 * BANK])
                        if i >= 1:
                            pe.wait_ge(S["t_hi"], 4 * i)
                            pe.wait_ge(S["t_lo"], 4 * i)
                        r_turn(i, 1, pu[:, 0:BANK])
                    elif step == 1:
                        pe.wait_ge(S["c_hi"], i + 1)
                        pe.wait_ge(S["c_lo"], i + 1)
                        pe.wait_ge(S["t_hi"], 4 * i + 2)
                        pe.wait_ge(S["t_lo"], 4 * i + 2)
                        for a, b in ((0, BANK), (BANK, QUP)):
                            for k in range(2):
                                mm = three_pass(pe, pu[:, a:b], cT_hi[:, k, :], cT_lo[:, k, :],
                                                wq_hi[:, k, a:b], wq_lo[:, k, a:b], k == 0, k == 1)
                        mm.then_inc(S["q_up"], 1)
                        for a, b in ((0, BANK), (BANK, KVUP)):
                            mm = three_pass(pe, pt[:, a:b], cT_hi[:, 2, :], cT_lo[:, 2, :],
                                            wkv_hi[:, a:b], wkv_lo[:, a:b], True, True)
                        mm.then_inc(S["kv_up"], 1)
                    else:
                        pe.wait_ge(S["q_read_act"], i + 1)
                        pe.wait_ge(S["q_read_dve"], i + 1)
                        pe.wait_ge(S["kv_read_act"], i + 1)
                        r_turn(i, 2, pu[:, 0:BANK])
                        r_turn(i, 3, pu[:, BANK:2 * BANK])

                h_turn(0)
                for i in range(TT):
                    proj(i, 0)
                    if i >= 1:
                        latent(i - 1, 0)
                    proj(i, 1)
                    if i >= 1:
                        latent(i - 1, 1)
                    proj(i, 2)
                    if i + 1 < TT:
                        h_turn(i + 1)
                    if i >= 1:
                        latent(i - 1, 2)
                    proj(i, 3)
                for step in range(3):
                    latent(TT - 1, step)

            @block.vector
            def _(dve):
                linked = 0

                def link(ins):
                    nonlocal linked
                    linked += 1
                    ins.then_inc(S["dve_own"], 1)
                    dve.wait_ge(S["dve_own"], linked)

                def h_full(i):
                    dve.wait_ge(S["h_turned"], i + 1)
                    c = 0 if i < TX else 1
                    for k in range(KT):
                        ins = dve.tensor_scalar(xt[:, i % 2, k * P:(k + 1) * P], pt[:, k * P:(k + 1) * P],
                                                keep["modT"][:, l, 1, k, c:c + 1], keep["modT"][:, l, 0, k, c:c + 1],
                                                ALU.mult, ALU.add)
                    ins.then_inc(S["h_full"], 1)

                def h_lo(i):
                    dve.wait_ge(S["h_hi"], i + 1)
                    dve.wait_ge(S["h_full"], i + 1)
                    if i >= 2:
                        dve.wait_ge(S["proj_done"], 4 * (i - 1))
                    dve.tensor_tensor(hT_lo[:, i % 2].rearrange("p k n -> p (k n)"), xt[:, i % 2, :],
                                      raw(hT_hi[:, i % 2].rearrange("p k n -> p (k n)")), ALU.subtract
                                      ).then_inc(S["h_lo"], 1)

                turn_used = None

                def place(dst, src_ap, heads, dim, tables, i, done):
                    nonlocal turn_used
                    if i >= TX:
                        dve.tensor_copy(dst, src_ap).then_inc(done, 1)
                        return
                    if turn_used is not None:
                        dve.wait_ge(*turn_used)
                    turn_used = (done, i + 1)
                    q = dim // 4
                    cos = tables[:, 0, i, :].unsqueeze(1).to_broadcast([P, heads, dim])
                    sin = tables[:, 1, i, :].rearrange("p (a s j) -> p a s j", a=2, s=2)
                    tv = turn[:, 0:heads * dim].rearrange("p (h a s j) -> p h a s j", h=heads, a=2, s=2)
                    sv = src_ap.rearrange("p h (a s j) -> p h a s j", a=2, s=2)
                    for z in range(2):
                        dve.tensor_tensor(tv[:, :, :, z, :], sv[:, :, :, 1 - z, :],
                                          sin[:, :, z, :].unsqueeze(1).to_broadcast([P, heads, 2, q]), ALU.mult)
                    link(dve.tensor_tensor(dst, src_ap, cos, ALU.mult))
                    dve.tensor_tensor(dst, dst, turn[:, 0:heads * dim].rearrange("p (h e) -> p h e", h=heads),
                                      ALU.add).then_inc(done, 1)

                def values_lo(i, part, src_ap, dst, hi):
                    dve.wait_ge(S["v_hi"], 3 * i + part + 1)
                    if i >= 1 and part == 0:
                        dve.wait_ge(S["v_stored"], 32 * i)
                    dve.tensor_tensor(dst, src_ap, raw(hi), ALU.subtract).then_inc(S["v_lo"], 1)

                def r_lo(i, g, bank):
                    dve.wait_ge(S["t_hi"], 4 * i + g + 1)
                    if g == 0 and i >= 1:
                        dve.wait_ge(S["t_stored"], 32 * i)
                    dve.tensor_tensor(T_lo[:, 4 * g:4 * g + 4].rearrange("p b n -> p (b n)"), bank,
                                      raw(T_hi[:, 4 * g:4 * g + 4].rearrange("p b n -> p (b n)")), ALU.subtract
                                      ).then_inc(S["t_lo"], 1)

                def latent(i, step):
                    if step == 0:
                        dve.wait_ge(S["c_turned"], i + 1)
                        for k in range(3):
                            ins = dve.tensor_scalar(cn[:, k * P:(k + 1) * P], pt[:, k * P:(k + 1) * P],
                                                    keep["cnorm"][:, l, k:k + 1], None, ALU.mult)
                        ins.then_inc(S["c_full"], 1)
                        dve.wait_ge(S["c_full"], i + 1)
                        dve.wait_ge(S["c_hi"], i + 1)
                        if i >= 1:
                            dve.wait_ge(S["kv_up"], i)
                        dve.tensor_tensor(cT_lo[:].rearrange("p k n -> p (k n)"), cn[:],
                                          raw(cT_hi[:].rearrange("p k n -> p (k n)")), ALU.subtract
                                          ).then_inc(S["c_lo"], 1)
                        r_lo(i, 0, pt[:, BANK:2 * BANK])
                        r_lo(i, 1, pu[:, 0:BANK])
                    elif step == 1:
                        dve.wait_ge(S["q_read_act"], i + 1)
                        if i >= 1:
                            dve.wait_ge(S["r_turned"], 4 * i)
                        place(heads_of(R[:, R_CQ:R_CN], 6)[:, :, 64:96], heads_of(pu[:, 0:QUP], 6)[:, :, 64:96],
                              6, 32, rot32, i, S["q_read_dve"])
                        dve.wait_ge(S["kv_up"], i + 1)
                        values_lo(i, 2, heads_of(pt[:, 0:KVUP], 6)[:, :, 64:128],
                                  heads_of(V_lo[:, V_C:VW], 6), heads_of(V_hi[:, V_C:VW], 6))
                    else:
                        r_lo(i, 2, pu[:, 0:BANK])
                        r_lo(i, 3, pu[:, BANK:2 * BANK])

                dve.memset(R[:, R_KR + 32:R_ALL], 0.0)
                dve.wait_ge(S["rot_loaded"], 32)
                h_full(0)
                h_lo(0)
                for i in range(TT):
                    dve.wait_ge(S["proj_done"], 4 * i + 1)
                    if i >= 1:
                        latent(i - 1, 0)
                        dve.wait_ge(S["r_turned"], 4 * (i - 1) + 2)
                    place(heads_of(R[:, R_AQ:R_BQ], 8), heads_of(pj[:, IN_AQ:IN_AV], 8), 8, 64, rot64, i,
                          S["ropeA_done"])
                    if i >= 1:
                        latent(i - 1, 1)
                    if i + 1 < TT:
                        h_full(i + 1)
                    if i + 1 < TT:
                        h_lo(i + 1)
                    dve.wait_ge(S["v_hi"], 3 * i + 2)
                    place(heads_of(R[:, R_BQ:R_CQ], 16), heads_of(pj[:, IN_BQ:IN_BV], 16), 16, 32, rot32, i,
                          S["ropeB_done"])
                    if i >= 1:
                        latent(i - 1, 2)
                    values_lo(i, 0, pj[:, IN_AV:IN_BQ], V_lo[:, V_A:V_B], V_hi[:, V_A:V_B])
                    values_lo(i, 1, pj[:, IN_BV:IN_CQ], V_lo[:, V_B:V_C], V_hi[:, V_B:V_C])
                    dve.wait_ge(S["c_squared"], 2 * (i + 1))
                    if i >= 1:
                        dve.wait_ge(S["r_turned"], 4 * i)
                    place(heads_of(R[:, R_KR:R_KR + 32], 1), heads_of(pj[:, PJ_KR:PJ_END], 1), 1, 32, rot32, i,
                          S["kr_done"])
                    dve.wait_ge(S["c_rms"], i + 1)
                    if i >= 1:
                        dve.wait_ge(S["c_hi"], i)
                        dve.wait_ge(S["c_lo"], i)
                    dve.tensor_scalar(cn[:, 0:QR], pj[:, PJ_CQ:PJ_CKV], rs[:, i % 2, 1:2], None, ALU.mult)
                    dve.tensor_scalar(cn[:, QR:384], pj[:, PJ_CKV:PJ_KR], rs[:, i % 2, 2:3], None, ALU.mult
                                      ).then_inc(S["c_normed"], 1)
                for step in range(3):
                    latent(TT - 1, step)


def attention_plan(l):
    units = [("A", g, g) for g in range(2)]
    units += [("B", m, 2 + m // 2) for m in range(8)]
    units += [("C", h, 6 + h) for h in range(6)]
    queries = TT if l < DEPTH - 1 else TX
    ctx_keys = list(range(TX, TT))
    steps, chunks, maxima, bounds = [], [], [], []
    for u, (kind, _, _) in enumerate(units):
        first = len(steps)
        if kind == "A":
            for q in range(queries):
                near = [] if q >= TX else [(k, m) for k, m in ((q - 1, "above"), (q, None), (q + 1, "below"))
                                           if 0 <= k < TX]
                for k, m in near + [(k, None) for k in ctx_keys]:
                    steps.append((u, len(chunks), k, m))
                chunks.append((u, q, 1, len(steps) - 1))
            maxima.append([(q, h) for h in range(3) for q in range(queries)])
        else:
            for q, n in ((0, 4), (4, 4)) + (((TX, TC),) if queries > TX else ()):
                for k in (range(TT) if q < TX else ctx_keys):
                    steps.append((u, len(chunks), k, None))
                chunks.append((u, q, n, len(steps) - 1))
            maxima.append([(q, 0) for q in range(queries)])
        bounds.append((first, len(steps)))
    return units, steps, chunks, maxima, bounds, queries


def attend(nc, t, dr, keep, l):
    units, steps, chunks, maxima, bounds, queries = attention_plan(l)
    G, LAG, RING = len(steps), 2, 3
    ends = {c[3]: n for n, c in enumerate(chunks)}
    starts = {b[0]: u for u, b in enumerate(bounds)}
    SCALE = {"A": A_SCALE, "B": B_SCALE, "C": C_SCALE}
    max_base = [sum(len(m) for m in maxima[:u]) for u in range(len(units))]
    max_at, row_at = {}, {}
    for u in range(1, len(units)):
        a, b = bounds[u - 1]
        for j in range(len(maxima[u])):
            max_at.setdefault(a + 3 + j * (b - a - 8) // len(maxima[u]), []).append((u, j))
        row_at[b - 4] = u
    two_maps = [units[c[0]][0] == "B" for c in chunks]
    kept = [units[c[0]][0] == "B" and units[c[0]][1] % 2 == 0 for c in chunks]
    order = [sum(not k for k in kept[:n]) for n in range(len(chunks))]
    second = [n for n in range(len(chunks)) if two_maps[n] and not kept[n]]
    nth_second = {n: j for j, n in enumerate(second)}
    before_slot = lambda g, lag: [n for e, n in ends.items() if e == g - lag]

    with ExitStack() as ctx:
        s = Scope(nc, ctx, f"at{l}")
        W = [s.sb(f"W{b}", [P, 8, TOK], F32R) for b in range(2)]
        Vh = [s.sb(f"Vh{b}", [P, TT, P], F32R) for b in range(2)]
        Vl = [s.sb(f"Vl{b}", [P, TT, P], F32R) for b in range(2)]
        E = s.sb("E", [P, RING, BANK])
        H, L = s.sb("H", [P, RING, BANK], F32R), s.sb("L", [P, RING, BANK], F32R)
        esink = s.sb("esink", [65, 3, TOK])
        zero_one = s.sb("zero_one", [65, P])
        mean64 = s.sb("mean64", [64, 64])
        mcol = s.sb("mcol", [P, 3 * TT])
        mrow = s.sb("mrow", [3 * TT, P], F32R)
        rec = s.sb("rec", [64, BANK])
        first_map = s.sb("first_map", [64, TOK])
        o = s.sb("o", [64, 3, BANK])
        osq, orn = s.sb("osq", [64, BANK]), s.sb("orn", [64, BANK])
        o_hi, o_lo = s.sb("o_hi", [64, 2, BANK], F32R), s.sb("o_lo", [64, 2, BANK], F32R)
        sc = s.ps("sc", [P, RING, BANK])
        av = s.ps("av", [P, 2, BANK])
        mx = s.ps("mx", [P, 3 * BANK])
        qk_loaded = [s.sem(f"qk_loaded{b}") for b in range(2)]
        v_loaded = [s.sem(f"v_loaded{b}") for b in range(2)]
        o_stored = [s.sem(f"o_stored{b}") for b in range(2)]
        names = ("s_done e_done h_done l_done av_done chunk_done o_done sink_done mx_done mx_read mcol_done mt_done "
                 "mneg_done mrow_loaded consts_done dve_own o_squared mean_done ln_read rn_done o_final o_hi_done "
                 "o_lo_done")
        S = {n: s.sem(n) for n in names.split()}
        block = ctx.enter_context(nc.Block())
        NLOAD = 7

        def width(n):
            return 3 * P if units[chunks[n][0]][0] == "A" else chunks[n][2] * P

        def use(u):
            return u // 2 + 1

        @block.sync
        def _(sp):
            T, V, ones = dr["T"], dr["V"], dr["ones"]

            def load(u):
                kind, i, v = units[u]
                w, sem = W[u % 2], qk_loaded[u % 2]
                if u >= 2:
                    sp.wait_ge(S["s_done"], bounds[u - 2][1])
                    if units[u - 2][0] == "A":
                        sp.wait_ge(S["sink_done"], 3 * (u - 1))
                if kind == "A":
                    q = [T[j, R_AQ + 192 * i:R_AQ + 192 * (i + 1), :].rearrange("(h p) n -> p h n", h=3)
                         for j in range(2)]
                    k = [T[j, R_AK + 64 * i:R_AK + 64 * (i + 1), :] for j in range(2)]
                    moves = [(w[0:64, 0:3, :], q[0]), (w[64:128, 0:3, :], q[0]), (w[0:64, 3:6, :], q[1]),
                             (w[0:64, 6, :], k[0]), (w[64:128, 6, :], k[1]), (w[0:64, 7, :], k[0]),
                             (w[64:65, 7, :], ones)]
                elif kind == "B":
                    q = [T[j, R_BQ + 32 * i:R_BQ + 32 * (i + 1), :] for j in range(2)]
                    k = [T[j, R_BK + 32 * i:R_BK + 32 * (i + 1), :] for j in range(2)]
                    moves = [(w[0:32, 0, :], q[0]), (w[32:64, 0, :], q[0]), (w[64:96, 0, :], q[1]),
                             (w[0:32, 1, :], k[0]), (w[32:64, 1, :], k[1]), (w[64:96, 1, :], k[0]),
                             (w[96:97, 1, :], ones)]
                else:
                    q = [T[j, R_CQ + 96 * i:R_CQ + 96 * (i + 1), :] for j in range(2)]
                    k = [T[j, R_CN + 64 * i:R_CN + 64 * (i + 1), :] for j in range(2)]
                    kr = [T[j, R_KR:R_KR + 32, :] for j in range(2)]
                    moves = [(w[0:96, 0, :], q[0]), (w[0:96, 2, :], q[1]), (w[0:64, 1, :], k[0]),
                             (w[64:96, 1, :], kr[0]), (w[96:97, 1, :], ones), (w[0:64, 3, :], k[1]),
                             (w[64:96, 3, :], kr[1])]
                for dst, src in moves:
                    sp.dma_start(raw(dst), src).then_inc(sem, 16)
                if u == 0 or units[u - 1][2] != v:
                    if v < 2:
                        sp.wait_ge(S["consts_done"], 7)
                    else:
                        last = max(x for x in range(u) if units[x][2] == v - 2)
                        sp.wait_ge(S["av_done"], bounds[last][1])
                    for j, buf in enumerate((Vh, Vl)):
                        sp.dma_start(raw(buf[v % 2][:, :, 0:64]),
                                     V[j, :, 64 * v:64 * (v + 1)].rearrange("(k p) e -> p k e", p=P)
                                     ).then_inc(v_loaded[v % 2], 16)

            def store(n):
                u, q, tiles, _ = chunks[n]
                kind, i, _ = units[u]
                b = order[n] % 2
                sp.wait_ge(S["o_lo_done"], order[n] + 1)
                for j, buf in enumerate((o_hi, o_lo)):
                    if kind == "A":
                        dst = dr["mix"][j, 192 * i:192 * (i + 1), q * P:(q + 1) * P].rearrange("(h p) n -> p h n", h=3)
                        src = buf[:, b, 0:3 * P].rearrange("p (h n) -> p h n", h=3)
                    else:
                        row = 384 + 64 * (i // 2) if kind == "B" else 640 + 64 * i
                        dst = dr["mix"][j, row:row + 64, q * P:(q + tiles) * P]
                        src = buf[:, b, 0:tiles * P]
                    sp.dma_start(dst, raw(src)).then_inc(o_stored[b], 16)

            load(0)
            for g in range(G + 11):
                if g in starts and starts[g] + 1 < len(units):
                    load(starts[g] + 1)
                for n in before_slot(g, 10):
                    if not kept[n]:
                        store(n)
            total = order[-1] + 1
            for b in range(2):
                sp.wait_ge(o_stored[b], 32 * ((total + 1 - b) // 2))

        @block.gpsimd
        def _(pool):
            for b in range(2):
                pool.memset(raw(Vh[b][:, :, 64:128]), 1.0).then_inc(S["consts_done"], 1)
                pool.memset(raw(Vl[b][:, :, 64:128]), 0.0).then_inc(S["consts_done"], 1)
            pool.wait_ge(S["consts_done"], 4)
            pool.memset(zero_one[64:65, 0:64], 0.0).then_inc(S["consts_done"], 1)
            pool.wait_ge(S["consts_done"], 5)
            pool.memset(zero_one[64:65, 64:128], 1.0).then_inc(S["consts_done"], 1)
            pool.wait_ge(S["consts_done"], 6)
            pool.memset(mean64[:], 1.0 / 64).then_inc(S["consts_done"], 1)

        rows_loaded = [16 * (3 * (u + 1) if u < 2 else 6 + (u - 1)) for u in range(len(units))]

        @block.scalar
        def _(act):
            def negate(u):
                rows = len(maxima[u])
                act.wait_ge(S["mt_done"], u + 1)
                if u >= 1:
                    act.wait_ge(S["mrow_loaded"], rows_loaded[u - 1])
                act.activation(mrow[0:rows, :], mx[0:rows, 1280:1280 + P], ACT.Copy, scale=-1.0
                               ).then_inc(S["mneg_done"], 1)
                act.wait_ge(S["mneg_done"], u + 1)
                if units[u][0] == "A":
                    for h in range(3):
                        act.dma_start(raw(W[u % 2][64:65, 3 + h, 0:queries * P]),
                                      raw(mrow[h * queries:(h + 1) * queries, :])).then_inc(S["mrow_loaded"], 16)
                else:
                    act.dma_start(raw(W[u % 2][96:97, 0, 0:queries * P]), raw(mrow[0:queries, :])
                                  ).then_inc(S["mrow_loaded"], 16)

            def hi(n):
                kind = units[chunks[n][0]][0]
                if kind == "B":
                    act.wait_ge(S["o_final"], nth_second[n] + 1)
                else:
                    act.wait_ge(S["o_done"], n + 1)
                b = order[n] % 2
                if order[n] >= 2:
                    act.wait_ge(o_stored[b], 32 * (order[n] // 2))
                act.copy(o_hi[:, b, 0:width(n)], o[:, n % 3, 0:width(n)]).then_inc(S["o_hi_done"], 1)

            negate(0)
            for g in range(G + 11):
                for n in before_slot(g, 4):
                    if n in nth_second:
                        j = nth_second[n]
                        act.wait_ge(S["o_done"], n + 1)
                        if j >= 1:
                            act.wait_ge(S["mean_done"], j)
                        act.activation(osq[:, 0:width(n)], o[:, n % 3, 0:width(n)], ACT.Square
                                       ).then_inc(S["o_squared"], 1)
                    elif not kept[n]:
                        hi(n)
                for n in before_slot(g, 6):
                    if n in nth_second:
                        j = nth_second[n]
                        act.wait_ge(S["mean_done"], j + 1)
                        if j >= 1:
                            act.wait_ge(S["o_final"], j)
                        act.activation(orn[:, 0:width(n)], av[0:64, n % 2, 0:width(n)], ACT.Ln,
                                       bias=keep["eps"][0:64, 0:1]).then_inc(S["ln_read"], 1)
                        act.wait_ge(S["ln_read"], j + 1)
                        act.activation(orn[:, 0:width(n)], orn[:, 0:width(n)], ACT.Exp, scale=-0.5
                                       ).then_inc(S["rn_done"], 1)
                for n in before_slot(g, 8):
                    if n in nth_second:
                        hi(n)
                if g < G:
                    u, n, _, _ = steps[g]
                    kind, i, _ = units[u]
                    if g in starts and kind == "A":
                        act.wait_ge(S["mrow_loaded"], rows_loaded[u])
                        if u == 1:
                            act.wait_ge(S["chunk_done"], queries)
                        for h in range(3):
                            act.activation(esink[64:65, h, 0:queries * P], raw(W[u % 2][64:65, 3 + h, 0:queries * P]),
                                           ACT.Exp, scale=A_SCALE, bias=keep["sink"][64:65, l, 3 * i + h:3 * i + h + 1]
                                           ).then_inc(S["sink_done"], 1)
                    w = width(n)
                    act.wait_ge(S["s_done"], g + 1)
                    if g >= RING:
                        act.wait_ge(S["l_done"], g - RING + 1)
                        act.wait_ge(S["av_done"], g - RING + 1)
                    act.activation(E[:, g % RING, 0:w], sc[:, g % RING, 0:w], ACT.Exp, scale=SCALE[kind]
                                   ).then_inc(S["e_done"], 1)
                    act.activation(H[:, g % RING, 0:w], sc[:, g % RING, 0:w], ACT.Exp, scale=SCALE[kind]
                                   ).then_inc(S["h_done"], 1)
                if g in row_at:
                    negate(row_at[g])

        @block.tensor
        def _(pe):
            def maximum(u, j):
                kind, i, _ = units[u]
                w = W[u % 2]
                q, h = maxima[u][j]
                x = max_base[u] + j
                if j == 0:
                    pe.wait_ge(qk_loaded[u % 2], 16 * NLOAD * use(u))
                    if u >= 1:
                        pe.wait_ge(S["mneg_done"], u)
                if x >= 1:
                    pe.wait_ge(S["mx_read"], x)
                cols = slice(q * P, (q + 1) * P)
                if kind == "A":
                    qs = w[:, h, cols]
                    if q < TX:
                        a, b = max(q - 1, 0), min(q + 2, TX)
                        near = (b - a) * P
                        pe.matmul(mx[:, BANK - near:BANK], qs, w[:, 6, a * P:b * P], start=True, stop=True)
                        for k in range(a, b):
                            if k != q:
                                at = BANK - near + (k - a) * P
                                pe.matmul(mx[:, at:at + P], keep["identb"][:],
                                          keep["below" if k < q else "above"][:], start=False, stop=True,
                                          skip_group_check=True)
                    mm = pe.matmul(mx[:, BANK:BANK + CTX], qs, w[:, 6, SEQ:TOK], start=True, stop=True)
                else:
                    qs = w[0:96, 0, cols]
                    if q < TX:
                        pe.matmul(mx[:, 0:BANK], qs, w[0:96, 1, 0:BANK], start=True, stop=True)
                        pe.matmul(mx[:, BANK:2 * BANK], qs, w[0:96, 1, BANK:2 * BANK], start=True, stop=True)
                        mm = pe.matmul(mx[:, 2 * BANK:1280], qs, w[0:96, 1, 2 * BANK:TOK], start=True, stop=True)
                    else:
                        mm = pe.matmul(mx[:, 0:CTX], qs, w[0:96, 1, SEQ:TOK], start=True, stop=True)
                mm.then_inc(S["mx_done"], 1)

            def turn_maxima(u):
                rows = len(maxima[u])
                if units[u][0] == "A":
                    pe.wait_ge(S["mcol_done"], u + 1)
                else:
                    pe.wait_ge(S["mx_read"], max_base[u] + rows)
                pe.transpose(mx[0:rows, 1280:1280 + P], mcol[:, 0:rows], keep["ident"][:]).then_inc(S["mt_done"], 1)

            def score(g):
                u, n, k, mask = steps[g]
                kind, i, _ = units[u]
                w = W[u % 2]
                _, q, tiles, _ = chunks[n]
                if g in starts:
                    pe.wait_ge(S["mrow_loaded"], rows_loaded[u])
                if g >= RING:
                    pe.wait_ge(S["h_done"], g - RING + 1)
                out = sc[:, g % RING, 0:width(n)]
                keys = slice(k * P, (k + 1) * P)
                cols = slice(q * P, (q + tiles) * P)
                if kind == "A":
                    o3 = out.rearrange("p (h n) -> p h n", h=3)
                    pe.matmul(o3, w[:, 6, keys], w[:, 0:3, cols], start=True, stop=False)
                    mm = pe.matmul(o3, w[0:65, 7, keys], w[0:65, 3:6, cols], start=False, stop=mask is None)
                    if mask is not None:
                        mm = pe.matmul(o3, keep["identb"][:], keep[mask][:].unsqueeze(1).to_broadcast([P, 3, P]),
                                       start=False, stop=True)
                elif kind == "B":
                    mm = pe.matmul(out, w[0:97, 1, keys], w[0:97, 0, cols], start=True, stop=True)
                else:
                    pe.matmul(out, w[0:97, 1, keys], w[0:97, 0, cols], start=True, stop=False)
                    pe.matmul(out, w[0:96, 1, keys], w[0:96, 2, cols], start=False, stop=False)
                    mm = pe.matmul(out, w[0:96, 3, keys], w[0:96, 0, cols], start=False, stop=True)
                mm.then_inc(S["s_done"], 1)

            def values(g):
                u, n, k, _ = steps[g]
                kind, i, v = units[u]
                first, last = g == 0 or steps[g - 1][1] != n, g in ends
                if first:
                    pe.wait_ge(v_loaded[v % 2], 32 * (v // 2 + 1))
                    if n >= 2:
                        pe.wait_ge(S["o_done"], n - 1)
                        if n - 2 in nth_second:
                            pe.wait_ge(S["ln_read"], nth_second[n - 2] + 1)
                pe.wait_ge(S["h_done"], g + 1)
                out = av[:, n % 2, 0:width(n)]
                h, lo = H[:, g % RING, 0:width(n)], L[:, g % RING, 0:width(n)]
                pe.matmul(out, Vh[v % 2][:, k, :], h, start=first, stop=False)
                pe.matmul(out, Vl[v % 2][:, k, :], h, start=False, stop=False)
                pe.wait_ge(S["l_done"], g + 1)
                mm = pe.matmul(out, Vh[v % 2][:, k, :], lo, start=False, stop=last and kind != "A")
                mm.then_inc(S["av_done"], 1)
                if last:
                    if kind == "A":
                        q = chunks[n][1]
                        pe.wait_ge(S["sink_done"], 3 * (u + 1))
                        pe.matmul(out.rearrange("p (h n) -> p h n", h=3), zero_one[64:65, :],
                                  esink[64:65, :, q * P:(q + 1) * P], start=False, stop=True
                                  ).then_inc(S["chunk_done"], 1)

            pe.wait_ge(S["consts_done"], 7)
            for j in range(len(maxima[0])):
                maximum(0, j)
            turn_maxima(0)
            for g in range(G + 6):
                for n in before_slot(g, 5):
                    if n in nth_second:
                        pe.wait_ge(S["o_squared"], nth_second[n] + 1)
                        pe.matmul(av[0:64, n % 2, 0:width(n)], mean64[:], osq[:, 0:width(n)], start=True, stop=True
                                  ).then_inc(S["mean_done"], 1)
                if g < G:
                    score(g)
                if 0 <= g - LAG < G:
                    values(g - LAG)
                for u, j in max_at.get(g, ()):
                    maximum(u, j)
                if g in row_at:
                    turn_maxima(row_at[g])

        @block.vector
        def _(dve):
            linked = 0

            def link(ins):
                nonlocal linked
                linked += 1
                ins.then_inc(S["dve_own"], 1)
                dve.wait_ge(S["dve_own"], linked)

            def reduce_max(u, j):
                kind = units[u][0]
                q, h = maxima[u][j]
                x = max_base[u] + j
                dve.wait_ge(S["mx_done"], x + 1)
                if j == 0 and u >= 1:
                    dve.wait_ge(S["mt_done"], u)
                if kind == "A":
                    near = (min(q + 2, TX) - max(q - 1, 0)) * P if q < TX else 0
                    a, b = BANK - near, BANK + CTX
                else:
                    a, b = 0, (TOK if q < TX else CTX)
                c = h * queries + q if kind == "A" else q
                dve.reduce_max(mcol[:, c:c + 1], mx[:, a:b], AX_X).then_inc(S["mx_read"], 1)

            def maxima_done(u):
                kind, i, _ = units[u]
                if kind == "A":
                    dve.wait_ge(S["mx_read"], max_base[u] + len(maxima[u]))
                    m3 = mcol[:, 0:3 * queries].rearrange("p (h q) -> p h q", h=3)
                    sink = keep["sinkdiv"][:, l, 3 * i:3 * i + 3].unsqueeze(2).to_broadcast([P, 3, queries])
                    dve.tensor_tensor(m3, m3, sink, ALU.max).then_inc(S["mcol_done"], 1)

            def normalise(n):
                w = width(n)
                if two_maps[n] or units[chunks[n][0]][0] == "C":
                    dve.wait_ge(S["av_done"], chunks[n][3] + 1)
                else:
                    dve.wait_ge(S["chunk_done"], n + 1)
                if n >= 3 and not kept[n]:
                    done = sum(1 for x in range(n - 2) if not kept[x])
                    if done:
                        dve.wait_ge(S["o_lo_done"], done)
                if n >= 1:
                    dve.wait_ge(S["o_done"], n)
                link(dve.reciprocal(rec[:, 0:w], av[64:128, n % 2, 0:w]))
                if not two_maps[n]:
                    dve.tensor_tensor(o[:, n % 3, 0:w], av[0:64, n % 2, 0:w], rec[:, 0:w], ALU.mult
                                      ).then_inc(S["o_done"], 1)
                    return
                c = slice(chunks[n][1] * P, chunks[n][1] * P + w)
                if kept[n]:
                    dve.tensor_tensor(first_map[:, c], av[0:64, n % 2, 0:w], rec[:, 0:w], ALU.mult
                                      ).then_inc(S["o_done"], 1)
                    return
                link(dve.tensor_tensor(o[:, n % 3, 0:w], av[0:64, n % 2, 0:w], rec[:, 0:w], ALU.mult))
                dve.scalar_tensor_tensor(out=o[:, n % 3, 0:w], in0=o[:, n % 3, 0:w],
                                         scalar=keep["neglam"][0:64, l:l + 1], in1=first_map[:, c],
                                         op0=ALU.mult, op1=ALU.add).then_inc(S["o_done"], 1)

            def lo(n):
                b = order[n] % 2
                dve.wait_ge(S["o_hi_done"], order[n] + 1)
                if order[n] >= 2:
                    dve.wait_ge(o_stored[b], 32 * (order[n] // 2))
                dve.tensor_tensor(o_lo[:, b, 0:width(n)], o[:, n % 3, 0:width(n)], raw(o_hi[:, b, 0:width(n)]),
                                  ALU.subtract).then_inc(S["o_lo_done"], 1)

            for j in range(len(maxima[0])):
                reduce_max(0, j)
            maxima_done(0)
            for g in range(G + 11):
                for n in before_slot(g, 3):
                    normalise(n)
                for n in before_slot(g, 5):
                    if not two_maps[n]:
                        lo(n)
                for n in before_slot(g, 7):
                    if n in nth_second:
                        dve.wait_ge(S["rn_done"], nth_second[n] + 1)
                        w = width(n)
                        dve.scalar_tensor_tensor(out=o[:, n % 3, 0:w], in0=o[:, n % 3, 0:w],
                                                 scalar=keep["dsn"][0:64, l:l + 1], in1=orn[:, 0:w],
                                                 op0=ALU.mult, op1=ALU.mult).then_inc(S["o_final"], 1)
                for n in before_slot(g, 9):
                    if n in nth_second:
                        dve.wait_ge(S["o_final"], nth_second[n] + 1)
                        lo(n)
                if g < G:
                    w = width(steps[g][1])
                    dve.wait_ge(S["h_done"], g + 1)
                    if g >= RING:
                        dve.wait_ge(S["av_done"], g - RING + 1)
                    dve.tensor_tensor(L[:, g % RING, 0:w], E[:, g % RING, 0:w], raw(H[:, g % RING, 0:w]), ALU.subtract
                                      ).then_inc(S["l_done"], 1)
                for u, j in max_at.get(g, ()):
                    reduce_max(u, j)
                if g in row_at:
                    maxima_done(row_at[g])


def mix_out(nc, t, dr, keep, l, h_hi, h_lo):
    NT = TT if l < DEPTH - 1 else TX
    with ExitStack() as outer:
        w = Scope(nc, outer, f"mw{l}")
        wo_hi, wo_lo = w.sb("wo_hi", [P, KT, D], F32R), w.sb("wo_lo", [P, KT, D], F32R)
        split_weights(nc, f"ms{l}", [(t["w_out"][l, k * P:(k + 1) * P, :], wo_hi[:, k, :], wo_lo[:, k, :])
                                     for k in range(KT)], D)
        with ExitStack() as ctx:
            s = Scope(nc, ctx, f"mo{l}")
            mix = s.sb("mix", [P, 2, 2, KT, P], F32R)
            x = s.sb("x", [P, 2, D])
            y = s.sb("y", [P, 2, D])
            gate = s.sb("gate", [P, 2, D])
            junk = s.sb("junk", [P, D], BF16)
            ss, ms, rs = s.sb("ss", [P, 2, 2]), s.sb("ms", [P, 2, 2]), s.sb("rs", [P, 2, 2])
            pm = s.ps("pm", [P, 2, 2 * BANK])
            pt = s.ps("pt", [P, 2 * BANK])
            loaded = [s.sem(f"loaded{b}") for b in range(2)]
            x_stored = [s.sem(f"x_stored{b}") for b in range(2)]
            names = ("gate_loaded mm_done m_squared m_rms y_done x_done x_squared x_rms normed turned full hi lo "
                     "pool_own")
            S = {n: s.sem(n) for n in names.split()}
            block = ctx.enter_context(nc.Block())

            @block.sync
            def _(sp):
                for c in range(2):
                    sp.dma_start(gate[:, c, :], dr["gate"][l, 0, c].partition_broadcast(P)).then_inc(S["gate_loaded"], 16)
                def store(i):
                    sp.wait_ge(S["x_done"], i + 1)
                    sp.dma_start(dr["x1"][i * P:(i + 1) * P, :], x[:, i % 2, :]).then_inc(x_stored[i % 2], 16)

                for i in range(NT):
                    b = i % 2
                    if i >= 2:
                        store(i - 2)
                        sp.wait_ge(S["mm_done"], i - 1)
                        sp.wait_ge(x_stored[b], 16 * (i // 2))
                        sp.wait_ge(S["normed"], i - 1)
                    for j in range(2):
                        sp.dma_start(raw(mix[:, b, j]), dr["mix"][j, :, i * P:(i + 1) * P].rearrange("(k p) n -> p k n", p=P)
                                     ).then_inc(loaded[b], 16)
                    if l == 0:
                        src = t["x"][0, i * P:(i + 1) * P, :] if i < TX else t["ctx"][0, (i - TX) * P:(i - TX + 1) * P, :]
                    else:
                        src = dr["x"][i * P:(i + 1) * P, :]
                    sp.dma_start(x[:, b, :], src).then_inc(loaded[b], 16)
                for i in (NT - 2, NT - 1):
                    store(i)
                for b in range(2):
                    sp.wait_ge(x_stored[b], 16 * ((NT + 1 - b) // 2))

            @block.gpsimd
            def _(pool):
                own = 0
                for i in range(NT):
                    b = i % 2
                    for c, before, after in ((0, "m_squared", "m_rms"), (1, "x_squared", "x_rms")):
                        pool.wait_ge(S[before], i + 1)
                        if i >= 2:
                            pool.wait_ge(S["normed"], i - 1)
                            pool.wait_ge(S["y_done"], i - 1)
                        pool.tensor_scalar(ms[:, b, c:c + 1], ss[:, b, c:c + 1], 1.0 / D, EPS, ALU.mult, ALU.add
                                           ).then_inc(S["pool_own"], 1)
                        own += 1
                        pool.wait_ge(S["pool_own"], own)
                        pool.tensor_tensor(rs[:, b, c:c + 1], ms[:, b, c:c + 1], keep["mhalf"][:, 0:1], ALU.pow
                                           ).then_inc(S[after], 1)

            @block.scalar
            def _(act):
                for i in range(NT + 1):
                    if i < NT:
                        act.wait_ge(S["mm_done"], i + 1)
                        if i >= 2:
                            act.wait_ge(S["m_rms"], i - 1)
                        act.activation(junk[:], pm[:, i % 2, :], ACT.Square, accum_out=ss[:, i % 2, 0:1]
                                       ).then_inc(S["m_squared"], 1)
                        act.wait_ge(S["x_done"], i + 1)
                        if i >= 2:
                            act.wait_ge(S["x_rms"], i - 1)
                        act.activation(junk[:], x[:, i % 2, :], ACT.Square, accum_out=ss[:, i % 2, 1:2]
                                       ).then_inc(S["x_squared"], 1)
                        act.wait_ge(S["x_rms"], i + 1)
                        act.activation(y[:, i % 2, :], x[:, i % 2, :], ACT.Copy, scale=rs[:, i % 2, 1:2]
                                       ).then_inc(S["normed"], 1)
                    if i >= 1:
                        j = i - 1
                        act.wait_ge(S["full"], j + 1)
                        act.copy(h_hi[:, :, j * P:(j + 1) * P], y[:, j % 2, :].rearrange("p (k n) -> p k n", k=KT)
                                 ).then_inc(S["hi"], 1)

            @block.tensor
            def _(pe):
                def turn(i):
                    pe.wait_ge(S["normed"], i + 1)
                    if i >= 1:
                        pe.wait_ge(S["full"], i)
                    for k in range(KT):
                        mm = pe.transpose(pt[:, k * P:(k + 1) * P], y[:, i % 2, k * P:(k + 1) * P], keep["ident"][:])
                    mm.then_inc(S["turned"], 1)

                for i in range(NT):
                    b = i % 2
                    pe.wait_ge(loaded[b], 48 * (i // 2 + 1))
                    if i >= 2:
                        pe.wait_ge(S["y_done"], i - 1)
                        pe.wait_ge(S["m_squared"], i - 1)
                    for n in range(2):
                        for k in range(KT):
                            c = slice(n * BANK, (n + 1) * BANK)
                            mm = three_pass(pe, pm[:, b, c], mix[:, b, 0, k, :], mix[:, b, 1, k, :],
                                            wo_hi[:, k, c], wo_lo[:, k, c], k == 0, k == KT - 1)
                    mm.then_inc(S["mm_done"], 1)
                    if i >= 1:
                        turn(i - 1)
                turn(NT - 1)

            @block.vector
            def _(dve):
                dve.wait_ge(S["gate_loaded"], 32)
                for i in range(NT + 1):
                    if i < NT:
                        b, c = i % 2, 0 if i < TX else 1
                        dve.wait_ge(S["m_rms"], i + 1)
                        if i >= 2:
                            dve.wait_ge(S["hi"], i - 1)
                            dve.wait_ge(S["lo"], i - 1)
                        dve.scalar_tensor_tensor(out=y[:, b, :], in0=pm[:, b, :], scalar=rs[:, b, 0:1],
                                                 in1=gate[:, c, :], op0=ALU.mult, op1=ALU.mult).then_inc(S["y_done"], 1)
                        dve.wait_ge(S["y_done"], i + 1)
                        dve.wait_ge(loaded[b], 48 * (i // 2 + 1))
                        dve.tensor_tensor(x[:, b, :], x[:, b, :], y[:, b, :], ALU.add).then_inc(S["x_done"], 1)
                    if i >= 1:
                        j = i - 1
                        c = 0 if j < TX else 1
                        dve.wait_ge(S["turned"], j + 1)
                        for k in range(KT):
                            ins = dve.tensor_scalar(y[:, j % 2, k * P:(k + 1) * P], pt[:, k * P:(k + 1) * P],
                                                    keep["modT"][:, l, 3, k, c:c + 1], keep["modT"][:, l, 2, k, c:c + 1],
                                                    ALU.mult, ALU.add)
                        ins.then_inc(S["full"], 1)
                        dve.wait_ge(S["full"], j + 1)
                        dve.wait_ge(S["hi"], j + 1)
                        sl = slice(j * P, (j + 1) * P)
                        dve.tensor_tensor(h_lo[:, :, sl], y[:, j % 2, :].rearrange("p (k n) -> p k n", k=KT),
                                          raw(h_hi[:, :, sl]), ALU.subtract).then_inc(S["lo"], 1)


def ffn(nc, t, dr, keep, l, h_hi, h_lo, acc):
    NT = TT if l < DEPTH - 1 else TX
    CH = [(a, min(a + BANK, NT * P)) for a in range(0, NT * P, BANK)]
    NC = len(CH)
    PAIRS = FT // 2
    with ExitStack() as ctx:
        s = Scope(nc, ctx, f"ff{l}")
        rawp = [s.sb(f"raw{b}", [P, D]) for b in range(3)]
        w_hi = s.sb("w_hi", [P, 2, 2, D], F32R)
        w_lo = s.sb("w_lo", [P, 2, 2, D], F32R)
        d_hi, d_lo = s.sb("d_hi", [P, 2, D], F32R), s.sb("d_lo", [P, 2, D], F32R)
        g_hi, g_lo = s.sb("g_hi", [P, 2, NT * P], F32R), s.sb("g_lo", [P, 2, NT * P], F32R)
        sg = s.sb("sg", [P, 2, BANK])
        pg = s.ps("pg", [P, 2, 2, BANK])
        pd = s.ps("pd", [P, 2, 2 * BANK])
        raw_loaded = [s.sem(f"raw_loaded{b}") for b in range(3)]
        names = "w_hi_done w_lo_done gu_bank silu_done prod_done g_hi_done g_lo_done d_tile acc_done zeroed"
        S = {n: s.sem(n) for n in names.split()}
        CREDIT, D_CREDIT = 2, 1
        block = ctx.enter_context(nc.Block())

        def gate_up(name, f):
            return t[name][l].rearrange("(k p) (f n) -> f p k n", p=P, n=P)[f]

        def down(f):
            return t["w_down"][l].rearrange("(f p) n -> f p n", p=P)[f]

        def count(i, p):
            return 6 * i + p + 4

        @block.sync
        def _(sp):
            def load(q, slot, src, wait):
                if wait is not None:
                    sp.wait_ge(S["w_lo_done"], wait)
                dst = rawp[slot][:]
                if len(src.shape) == 3:
                    dst = dst.rearrange("p (k n) -> p k n", k=KT)
                sp.dma_start(dst, src).then_inc(raw_loaded[slot], 16)

            def turn(i, last):
                for p in range(2 if last else 6):
                    src = down(2 * i + p) if p < 2 else gate_up(("w_gate", "w_up")[p % 2], 2 * (i + 1) + (p - 2) // 2)
                    load(None, (4 + p) % 3, src, 6 * i + p + 2)

            for p in range(4):
                load(None, p % 3, gate_up(("w_gate", "w_up")[p % 2], p // 2), p - 2 if p >= 3 else None)
            with sp.Fori(0, PAIRS - 1) as i:
                turn(i, False)
            turn(PAIRS - 1, True)

        @block.gpsimd
        def _(pool):
            for j in range(NT):
                ins = pool.memset(acc[:, j, :], 0.0)
            ins.then_inc(S["zeroed"], 1)

        def split(eng, p, i, hi_side):
            if p < 2:
                hi, lo = d_hi[:, p, :], d_lo[:, p, :]
            else:
                hi, lo = w_hi[:, (p - 2) // 2, p % 2, :], w_lo[:, (p - 2) // 2, p % 2, :]
            if i is None:
                q = p - 2
                slot, uses, done = q % 3, q // 3 + 1, q + 1
            else:
                slot, uses, done = (4 + p) % 3, 2 * i + (4 + p) // 3 + 1, count(i, p) + 1
                if p < 2:
                    eng.wait_ge(S["d_tile"], NT * i + D_CREDIT)
                else:
                    eng.wait_ge(S["gu_bank"], NC * (2 * i + (p - 2) // 2 + 1))
            if hi_side:
                eng.wait_ge(raw_loaded[slot], 16 * uses)
                eng.copy(hi, rawp[slot][:]).then_inc(S["w_hi_done"], 1)
            else:
                eng.wait_ge(S["w_hi_done"], done)
                eng.wait_ge(raw_loaded[slot], 16 * uses)
                eng.tensor_tensor(lo, rawp[slot][:], raw(hi), ALU.subtract).then_inc(S["w_lo_done"], 1)

        @block.scalar
        def _(act):
            def turn(i, last):
                for f in range(2):
                    for c, (a, b) in enumerate(CH):
                        e = 2 * NC * i + f * NC + c
                        z = (f * NC + c) % 2
                        act.wait_ge(S["gu_bank"], e + 1)
                        act.wait_ge(S["g_lo_done"], e + 1)
                        act.activation(sg[:, z, 0:b - a], pg[:, z, 0, 0:b - a], ACT.Silu).then_inc(S["silu_done"], 1)
                        if c < 2 and not (last and f == 1):
                            split(act, 2 * f + c, i, True)
                        act.wait_ge(S["prod_done"], e + 1 + CREDIT)
                        act.wait_ge(S["d_tile"], NT * i + D_CREDIT)
                        act.copy(g_hi[:, f, a:b], sg[:, z, 0:b - a]).then_inc(S["g_hi_done"], 1)
                if not last:
                    split(act, 4, i, True)
                    split(act, 5, i, True)

            for p in range(2, 6):
                split(act, p, None, True)
            with act.Fori(0, PAIRS - 1) as i:
                turn(i, False)
            turn(PAIRS - 1, True)

        @block.tensor
        def _(pe):
            def turn(i):
                for f in range(2):
                    pe.wait_ge(S["w_lo_done"], 6 * i + 2 * f + 2)
                    for c, (a, b) in enumerate(CH):
                        z = (f * NC + c) % 2
                        pe.wait_ge(S["prod_done"], 2 * NC * i + f * NC + c + 1)
                        for x in range(2):
                            for k in range(KT):
                                kk = slice(k * P, (k + 1) * P)
                                mm = three_pass(pe, pg[:, z, x, 0:b - a], w_hi[:, f, x, kk], w_lo[:, f, x, kk],
                                                h_hi[:, k, a:b], h_lo[:, k, a:b], k == 0, k == KT - 1)
                        mm.then_inc(S["gu_bank"], 1)
                pe.wait_ge(S["w_lo_done"], 6 * i + 6)
                for j in range(NT):
                    if j % 4 == 0:
                        pe.wait_ge(S["g_lo_done"], 2 * NC * i + NC + j // 4 + 1 + CREDIT)
                    pe.wait_ge(S["acc_done"], NT * i + j + 1)
                    tok = slice(j * P, (j + 1) * P)
                    for n in range(2):
                        c = slice(n * BANK, (n + 1) * BANK)
                        for f in range(2):
                            mm = three_pass(pe, pd[:, j % 2, c], g_hi[:, f, tok], g_lo[:, f, tok],
                                            d_hi[:, f, c], d_lo[:, f, c], f == 0, f == 1)
                    mm.then_inc(S["d_tile"], 1)

            pe.nop().then_inc(S["d_tile"], D_CREDIT)
            with pe.Fori(0, PAIRS) as i:
                turn(i)

        @block.vector
        def _(dve):
            def turn(i, last):
                for f in range(2):
                    for c, (a, b) in enumerate(CH):
                        e = 2 * NC * i + f * NC + c
                        z = (f * NC + c) % 2
                        dve.wait_ge(S["silu_done"], e + 1)
                        dve.tensor_tensor(sg[:, z, 0:b - a], sg[:, z, 0:b - a], pg[:, z, 1, 0:b - a], ALU.mult
                                          ).then_inc(S["prod_done"], 1)
                        if c < 2 and not (last and f == 1):
                            split(dve, 2 * f + c, i, False)
                        dve.wait_ge(S["g_hi_done"], e + 1)
                        dve.wait_ge(S["prod_done"], e + 1 + CREDIT)
                        dve.wait_ge(S["d_tile"], NT * i + D_CREDIT)
                        dve.tensor_tensor(g_lo[:, f, a:b], sg[:, z, 0:b - a], raw(g_hi[:, f, a:b]), ALU.subtract
                                          ).then_inc(S["g_lo_done"], 1)
                for j in range(NT):
                    if not last and j in (1, 3):
                        split(dve, 4 + j // 2, i, False)
                    dve.wait_ge(S["d_tile"], NT * i + j + 1 + D_CREDIT)
                    dve.tensor_tensor(acc[:, j, :], acc[:, j, :], pd[:, j % 2, :], ALU.add).then_inc(S["acc_done"], 1)

            for name in ("prod_done", "g_lo_done", "acc_done"):
                dve.nop().then_inc(S[name], CREDIT)
            dve.wait_ge(S["zeroed"], 1)
            for p in range(2, 6):
                split(dve, p, None, False)
            with dve.Fori(0, PAIRS - 1) as i:
                turn(i, False)
            turn(PAIRS - 1, True)


def ffn_out(nc, t, dr, keep, l, acc, out):
    NT = TT if l < DEPTH - 1 else TX
    with ExitStack() as ctx:
        s = Scope(nc, ctx, f"fo{l}")
        x = s.sb("x", [P, 3, D])
        gate = s.sb("gate", [P, 2, D])
        junk = s.sb("junk", [P, 2, D], BF16)
        ss, ms, rs = s.sb("ss", [P, NT]), s.sb("ms", [P, NT]), s.sb("rs", [P, NT])
        loaded = [s.sem(f"loaded{b}") for b in range(3)]
        stored = [s.sem(f"stored{b}") for b in range(3)]
        S = {n: s.sem(n) for n in ("gate_loaded", "squared", "rms", "pool_own", "gated", "x_done")}
        block = ctx.enter_context(nc.Block())

        @block.sync
        def _(sp):
            for c in range(2):
                sp.dma_start(gate[:, c, :], dr["gate"][l, 1, c].partition_broadcast(P)).then_inc(S["gate_loaded"], 16)
            def store(i):
                sp.wait_ge(S["x_done"], i + 1)
                dst = out[0, i * P:(i + 1) * P, :] if l == DEPTH - 1 else dr["x"][i * P:(i + 1) * P, :]
                sp.dma_start(dst, x[:, i % 3, :]).then_inc(stored[i % 3], 16)

            for i in range(NT):
                b = i % 3
                if i >= 3:
                    store(i - 3)
                    sp.wait_ge(stored[b], 16 * (i // 3))
                sp.dma_start(x[:, b, :], dr["x1"][i * P:(i + 1) * P, :]).then_inc(loaded[b], 16)
            for i in range(NT - 3, NT):
                store(i)
            for b in range(3):
                sp.wait_ge(stored[b], 16 * ((NT + 2 - b) // 3))

        @block.scalar
        def _(act):
            for i in range(NT):
                if i >= 2:
                    act.wait_ge(S["squared"], i - 1)
                act.activation(junk[:, i % 2, :], acc[:, i, :], ACT.Square, accum_out=ss[:, i:i + 1]).then_inc(S["squared"], 1)

        @block.gpsimd
        def _(pool):
            for i in range(NT):
                pool.wait_ge(S["squared"], i + 1)
                pool.tensor_scalar(ms[:, i:i + 1], ss[:, i:i + 1], 1.0 / D, EPS, ALU.mult, ALU.add
                                   ).then_inc(S["pool_own"], 1)
                pool.wait_ge(S["pool_own"], i + 1)
                pool.tensor_tensor(rs[:, i:i + 1], ms[:, i:i + 1], keep["mhalf"][:, 0:1], ALU.pow
                                   ).then_inc(S["rms"], 1)

        @block.vector
        def _(dve):
            dve.wait_ge(S["gate_loaded"], 32)
            for i in range(NT):
                dve.wait_ge(S["rms"], i + 1)
                dve.wait_ge(S["squared"], i + 1)
                dve.scalar_tensor_tensor(out=acc[:, i, :], in0=acc[:, i, :], scalar=rs[:, i:i + 1],
                                         in1=gate[:, 0 if i < TX else 1, :], op0=ALU.mult, op1=ALU.mult
                                         ).then_inc(S["gated"], 1)
                dve.wait_ge(S["gated"], i + 1)
                dve.wait_ge(loaded[i % 3], 16 * (i // 3 + 1))
                dve.tensor_tensor(x[:, i % 3, :], x[:, i % 3, :], acc[:, i, :], ALU.add).then_inc(S["x_done"], 1)


def trunk(nc, t, out):
    dr = {
        "T": nc.dram_tensor("rows_T", (2, R_ALL, TOK), F32, kind="Internal").ap(),
        "V": nc.dram_tensor("values", (2, TOK, VW), F32, kind="Internal").ap(),
        "mix": nc.dram_tensor("mix_T", (2, D, TOK), F32, kind="Internal").ap(),
        "x": nc.dram_tensor("residual", (TOK, D), F32, kind="Internal").ap(),
        "x1": nc.dram_tensor("residual_mid", (TOK, D), F32, kind="Internal").ap(),
        "gate": nc.dram_tensor("gates", (DEPTH, 2, 2, D), F32, kind="Internal").ap(),
        "ones": nc.dram_tensor("ones_row", (1, TOK), F32, kind="Internal").ap(),
    }
    with ExitStack() as ctx:
        s = Scope(nc, ctx, "keep")
        keep = {
            "vecs_loaded": s.sem("vecs_loaded"),
            "ident": s.sb("ident", [P, P]), "identb": s.sb("identb", [P, P], BF16),
            "above": s.sb("above", [P, P], BF16), "below": s.sb("below", [P, P], BF16),
            "eps": s.sb("eps", [P, 1]), "mhalf": s.sb("mhalf", [P, 4]),
            "modT": s.sb("modT", [P, DEPTH, 4, KT, 2]), "cnorm": s.sb("cnorm", [P, DEPTH, 3]),
            "neglam": s.sb("neglam", [P, DEPTH]), "dsn": s.sb("dsn", [64, DEPTH]),
            "sink": s.sb("sink", [P, DEPTH, 6]), "sinkdiv": s.sb("sinkdiv", [P, DEPTH, 6]),
        }
        modulation(nc, t, dr, keep)
        for l in range(DEPTH):
            project(nc, t, dr, keep, l)
            attend(nc, t, dr, keep, l)
            NT = TT if l < DEPTH - 1 else TX
            with ExitStack() as ffn_ctx:
                f = Scope(nc, ffn_ctx, f"h{l}")
                h_hi, h_lo = f.sb("hi", [P, KT, NT * P], F32R), f.sb("lo", [P, KT, NT * P], F32R)
                mix_out(nc, t, dr, keep, l, h_hi, h_lo)
                acc = f.sb("acc", [P, NT, D])
                ffn(nc, t, dr, keep, l, h_hi, h_lo, acc)
                ffn_out(nc, t, dr, keep, l, acc, out)


_INS = ["x", "c", "ctx", "c_ctx", "w_ada", "b_ada", "g_pre_mix", "g_post_mix", "w_in", "win_sink",
        "diff_lambda_q1", "diff_lambda_k1", "diff_lambda_q2", "diff_lambda_k2", "diff_sub_norm",
        "mla_q_norm", "mla_w_q_up", "mla_kv_norm", "mla_w_kv_up", "w_out",
        "g_pre_ffn", "g_post_ffn", "w_gate", "w_up", "w_down"]


def rotary_table(dim):
    half = dim // 2
    pos = np.arange(SEQ)
    freqs = (np.float32(10000.0) ** (-np.arange(0, half, 2, dtype=np.float32) / np.float32(half))).astype(np.float32)
    table = np.zeros((2, SEQ, dim), np.float32)
    for a, p in enumerate((pos // GRID_W, pos % GRID_W)):
        ang = p.astype(np.float32)[:, None] * freqs[None, :]
        cos, sin = np.cos(ang), np.sin(ang)
        o = a * half
        table[0, :, o:o + half] = np.concatenate([cos, cos], 1)
        table[1, :, o:o + half] = np.concatenate([-sin, sin], 1)
    return np.ascontiguousarray(table.reshape(2, TX, P, dim).transpose(2, 0, 1, 3))


def kernel(**inputs):
    import concourse.bacc as bacc
    from concourse.bass_utils import run_bass_kernel_spmd

    nc = bacc.Bacc("TRN2", target_bir_lowering=False, num_devices=1)
    arrays, t = {}, {}
    given = {name: np.ascontiguousarray(inputs[name]) for name in _INS}
    given["rot64"], given["rot32"] = rotary_table(64), rotary_table(32)
    for name, a in given.items():
        arrays[f"in_{name}"] = a
        t[name] = nc.dram_tensor(f"in_{name}", a.shape, mybir.dt.from_np(a.dtype), kind="ExternalInput").ap()
    out = nc.dram_tensor("out_x", (1, SEQ, D), F32, kind="ExternalOutput").ap()
    trunk(nc, t, out)
    r = run_bass_kernel_spmd(nc, [arrays], core_ids=[0])
    return r.results[0]["out_x"]
```

```python
from contextlib import ExitStack
import math

import numpy as np
import concourse.bass as bass
from concourse import mybir
from concourse.alu_op_type import AluOpType as ALU

F32 = mybir.dt.float32
F32R = mybir.dt.float32r
BF16 = mybir.dt.bfloat16
ACT = mybir.ActivationFunctionType
AX_X = mybir.AxisListType.X

P = 128
BANK = 512
D = 1024
KT = D // P
SEQ, CTX = 1024, 256
TX, TC = SEQ // P, CTX // P
TT = TX + TC
TOK = SEQ + CTX
DEPTH = 2
GRID_W = 64
EPS = 1e-6
NEG = -1e30
D_IN = 1824
QR, KVR = 256, 128
QUP, KVUP = 576, 768
VW = 768
DFF = 2816
FT = DFF // P
A_SCALE, B_SCALE, C_SCALE = 64 ** -0.5, 32 ** -0.5, 96 ** -0.5

IN_AQ, IN_AV, IN_BQ, IN_BV, IN_CQ, IN_CKV, IN_KR = 0, 512, 640, 1152, 1408, 1664, 1792
IN_BANKS = (0, 512, 1024, 1408, D_IN)
PJ_CQ, PJ_CKV, PJ_KR, PJ_END = (3 * BANK + c - IN_CQ for c in (IN_CQ, IN_CKV, IN_KR, D_IN))
R_AQ, R_AK, R_BQ, R_BK, R_CQ, R_CN, R_KR, R_ALL = 0, 384, 512, 768, 1024, 1600, 1984, 2048
V_A, V_B, V_C = 0, 128, 384


def lam_init(l):
    return 0.8 - 0.6 * math.exp(-0.3 * l)


def raw(ap):
    return ap.bitcast(F32)


def heads_of(ap, heads):
    return ap.rearrange("p (h e) -> p h e", h=heads)


class Scope:

    def __init__(self, nc, ctx, tag):
        self.nc, self.ctx, self.tag = nc, ctx, tag
        self.sems = []
        ctx.callback(self.close)

    def close(self):
        if self.sems:
            self.nc.clear_and_free_semaphores(self.sems)
            self.nc.all_engine_barrier()

    def sb(self, name, shape, dt=F32):
        return self.ctx.enter_context(self.nc.sbuf_tensor(f"{self.tag}_{name}", shape, dt))

    def ps(self, name, shape, dt=F32):
        return self.ctx.enter_context(self.nc.psum_tensor(f"{self.tag}_{name}", shape, dt))

    def sem(self, name):
        self.sems.append(self.nc.alloc_semaphore(f"{self.tag}_{name}"))
        return self.sems[-1]


def three_pass(pe, out, w_hi, w_lo, m_hi, m_lo, first, last):
    pe.matmul(out, w_hi, m_hi, start=first, stop=False)
    pe.matmul(out, w_hi, m_lo, start=False, stop=False)
    return pe.matmul(out, w_lo, m_hi, start=False, stop=last)


def modulation(nc, t, dr, keep):
    NCH = 6 * D // BANK
    RING = 4
    with ExitStack() as ctx:
        s = Scope(nc, ctx, "mod")
        cT = s.sb("cT", [P, 2, KT])
        sT = s.sb("sT", [P, 2, KT])
        bias = s.sb("bias", [2, DEPTH, 6 * D])
        rows = s.sb("rows", [2, DEPTH, 6 * D])
        gpost = s.sb("gpost", [2, DEPTH, 2, D])
        gpreT = s.sb("gpreT", [P, DEPTH, 2, KT])
        wring = s.sb("wring", [P, RING, KT, BANK])
        lamv = s.sb("lamv", [P, 4, DEPTH, 32])
        lamj = s.sb("lamj", [P, 2, DEPTH, 32])
        lamd = s.sb("lamd", [P, 2, DEPTH])
        lame = s.sb("lame", [P, 2, DEPTH])
        dsnr = s.sb("dsnr", [64, DEPTH])
        pm = s.ps("pm", [P, 2, BANK])
        pT = s.ps("pT", [P, BANK])
        cols_loaded, vecs_loaded = s.sem("cols_loaded"), keep["vecs_loaded"]
        w_loaded = [s.sem(f"w_loaded{i}") for i in range(RING)]
        silu_done, consts_done, chunk_summed, row_done = (
            s.sem("silu_done"), s.sem("consts_done"), s.sem("chunk_summed"), s.sem("row_done"))
        turned, lam_dots, lam_exp, own, stored = (
            s.sem("turned"), s.sem("lam_dots"), s.sem("lam_exp"), s.sem("own"), s.sem("stored"))
        ones = s.sb("ones", [1, TOK], F32R)
        ones_done = s.sem("ones_done")
        block = ctx.enter_context(nc.Block())
        NVEC = 13

        @block.sync
        def _(sp):
            sp.dma_start(cT[:, 0, :], t["c"].rearrange("o (k p) -> p (o k)", p=P),
                         allow_slow_non_contiguous=True).then_inc(cols_loaded, 16)
            sp.dma_start(cT[:, 1, :], t["c_ctx"].rearrange("(k p) -> p k", p=P),
                         allow_slow_non_contiguous=True).then_inc(cols_loaded, 16)
            for i in range(DEPTH * NCH):
                l, n = divmod(i, NCH)
                if i >= RING:
                    sp.wait_ge(chunk_summed, i - RING + 1)
                sp.dma_start(wring[:, i % RING, :, :],
                             t["w_ada"][l, :, n * BANK:(n + 1) * BANK].rearrange("(k p) n -> p k n", p=P)
                             ).then_inc(w_loaded[i % RING], 16)
            sp.wait_ge(own, 2 * DEPTH + 4)
            for l in range(DEPTH):
                for j in range(2):
                    sp.dma_start(dr["gate"][l, j], gpost[:, l, j, :]).then_inc(stored, 16)
            sp.wait_ge(ones_done, 1)
            sp.dma_start(dr["ones"], raw(ones[:])).then_inc(stored, 16)
            sp.wait_ge(stored, 16 * (2 * DEPTH + 1))

        @block.gpsimd
        def _(pool):
            pool.memset(raw(ones[:]), 1.0).then_inc(ones_done, 1)
            pool.memset(keep["ident"][:], 0.0).then_inc(consts_done, 1)
            pool.memset(keep["identb"][:], 0.0).then_inc(consts_done, 1)
            pool.memset(keep["above"][:], 0.0).then_inc(consts_done, 1)
            pool.memset(keep["below"][:], 0.0).then_inc(consts_done, 1)
            pool.wait_ge(consts_done, 4)
            for m in (keep["ident"], keep["identb"]):
                pool.affine_select(out=m[:], in_=m[:], compare_op=ALU.not_equal, fill=1.0, base=0,
                                   pattern=[[-1, P]], channel_multiplier=1).then_inc(consts_done, 1)
            pool.affine_select(out=keep["above"][:], in_=keep["above"][:], compare_op=ALU.is_ge, fill=NEG, base=0,
                               pattern=[[-1, P]], channel_multiplier=1).then_inc(consts_done, 1)
            pool.affine_select(out=keep["below"][:], in_=keep["below"][:], compare_op=ALU.is_ge, fill=NEG, base=0,
                               pattern=[[1, P]], channel_multiplier=-1).then_inc(consts_done, 1)
            pool.memset(keep["eps"][:], EPS).then_inc(consts_done, 1)
            pool.memset(keep["mhalf"][:], -0.5).then_inc(consts_done, 1)
            pool.dma_start(bias[:], t["b_ada"].partition_broadcast(2)).then_inc(vecs_loaded, 16)
            for j, name in enumerate(("g_post_mix", "g_post_ffn")):
                pool.dma_start(gpost[:, :, j, :], t[name].partition_broadcast(2)).then_inc(vecs_loaded, 16)
            for j, name in enumerate(("g_pre_mix", "g_pre_ffn")):
                for l in range(DEPTH):
                    pool.dma_start(gpreT[:, l, j, :], t[name][l].rearrange("(k p) -> p k", p=P),
                                   allow_slow_non_contiguous=True
                                   ).then_inc(vecs_loaded, 16)
            for j, name in enumerate(("diff_lambda_q1", "diff_lambda_k1", "diff_lambda_q2", "diff_lambda_k2")):
                pool.dma_start(lamv[:, j, :, :], t[name].partition_broadcast(P)).then_inc(vecs_loaded, 16)
            pool.dma_start(keep["sink"][:], t["win_sink"].partition_broadcast(P)).then_inc(vecs_loaded, 16)
            pool.dma_start(dsnr[:], t["diff_sub_norm"].rearrange("l v -> v l"),
                           allow_slow_non_contiguous=True).then_inc(vecs_loaded, 16)
            for l in range(DEPTH):
                pool.dma_start(keep["cnorm"][:, l, 0:2], t["mla_q_norm"][l].rearrange("(k p) -> p k", p=P),
                               allow_slow_non_contiguous=True
                               ).then_inc(vecs_loaded, 16)
                pool.dma_start(keep["cnorm"][:, l, 2:3], t["mla_kv_norm"][l].rearrange("(k p) -> p k", p=P),
                               allow_slow_non_contiguous=True
                               ).then_inc(vecs_loaded, 16)
            pool.wait_ge(vecs_loaded, 16 * (NVEC + 4))

        @block.scalar
        def _(act):
            act.wait_ge(cols_loaded, 32)
            act.activation(sT[:], cT[:], ACT.Silu).then_inc(silu_done, 1)
            act.wait_ge(lam_dots, 2 * DEPTH)
            act.activation(lame[:], lamd[:], ACT.Exp).then_inc(lam_exp, 1)

        @block.tensor
        def _(pe):
            pe.wait_ge(silu_done, 1)
            for i in range(DEPTH * NCH):
                pe.wait_ge(w_loaded[i % RING], 16 * (i // RING + 1))
                if i >= 2:
                    pe.wait_ge(row_done, i - 1)
                for k in range(KT):
                    mm = pe.matmul(pm[0:2, i % 2, :], sT[:, :, k], wring[:, i % RING, k, :],
                                   start=(k == 0), stop=(k == KT - 1))
                mm.then_inc(chunk_summed, 1)
            pe.wait_ge(row_done, DEPTH * NCH)
            pe.wait_ge(consts_done, 10)
            for l in range(DEPTH):
                for j, part in enumerate((0, 1, 3, 4)):
                    for k in range(KT):
                        at = ((l * 4 + j) * KT + k) * 2
                        mm = pe.transpose(pT[:, at:at + 2], rows[:, l, part * D + k * P:part * D + (k + 1) * P],
                                          keep["ident"][0:2, 0:2])
            mm.then_inc(turned, 1)

        @block.vector
        def _(dve):
            dve.wait_ge(vecs_loaded, 16 * (NVEC + 4))
            for l in range(DEPTH):
                for j in range(2):
                    dve.tensor_tensor_reduce(lamj[:, j, l, :], lamv[:, 2 * j, l, :], lamv[:, 2 * j + 1, l, :],
                                             1.0, 0.0, ALU.mult, ALU.add, lamd[:, j, l:l + 1]).then_inc(lam_dots, 1)
            for i in range(DEPTH * NCH):
                l, n = divmod(i, NCH)
                c = slice(n * BANK, (n + 1) * BANK)
                dve.wait_ge(chunk_summed, i + 1)
                dve.tensor_tensor(rows[:, l, c], pm[0:2, i % 2, :], bias[:, l, c], ALU.add).then_inc(row_done, 1)
            dve.wait_ge(row_done, DEPTH * NCH)
            for l in range(DEPTH):
                for j, part in enumerate((2, 5)):
                    dve.tensor_tensor(gpost[:, l, j, :], rows[:, l, part * D:(part + 1) * D], gpost[:, l, j, :],
                                      ALU.mult).then_inc(own, 1)
            dve.wait_ge(lam_exp, 1)
            for l in range(DEPTH):
                dve.scalar_tensor_tensor(out=keep["neglam"][:, l:l + 1], in0=lame[:, 1, l:l + 1], scalar=-lam_init(l),
                                         in1=lame[:, 0, l:l + 1], op0=ALU.add, op1=ALU.subtract).then_inc(own, 1)
                dve.tensor_scalar(keep["dsn"][:, l:l + 1], dsnr[:, l:l + 1], 1.0 - lam_init(l), None,
                                  ALU.mult).then_inc(own, 1)
            dve.tensor_scalar(keep["sinkdiv"][:], keep["sink"][:], 1.0 / A_SCALE, None, ALU.mult)
            dve.wait_ge(turned, 1)
            view = pT[:, 0:DEPTH * 4 * KT * 2].rearrange("p (l j k c) -> p l j k c", l=DEPTH, j=4, k=KT)
            for l in range(DEPTH):
                for j in range(2):
                    dve.tensor_copy(keep["modT"][:, l, 2 * j], view[:, l, 2 * j])
                    dve.scalar_tensor_tensor(out=keep["modT"][:, l, 2 * j + 1], in0=view[:, l, 2 * j + 1], scalar=1.0,
                                             in1=gpreT[:, l, j, :].unsqueeze(2).to_broadcast([P, KT, 2]),
                                             op0=ALU.add, op1=ALU.mult)


def split_weights(nc, tag, pieces, ring_cols):
    RING = 4
    with ExitStack() as ctx:
        s = Scope(nc, ctx, tag)
        ring = s.sb("ring", [P, RING, ring_cols])
        loaded = [s.sem(f"loaded{i}") for i in range(RING)]
        hi_done, lo_done = s.sem("hi_done"), s.sem("lo_done")
        block = ctx.enter_context(nc.Block())

        def slot(i, n):
            return ring[:, i % RING, 0:n]

        @block.sync
        def _(sp):
            for i, (src, hi, lo) in enumerate(pieces):
                if i >= RING:
                    sp.wait_ge(lo_done, i - RING + 1)
                sp.dma_start(slot(i, hi.shape[-1]), src).then_inc(loaded[i % RING], 16)

        @block.scalar
        def _(act):
            for i, (src, hi, lo) in enumerate(pieces):
                act.wait_ge(loaded[i % RING], 16 * (i // RING + 1))
                act.copy(hi, slot(i, hi.shape[-1])).then_inc(hi_done, 1)

        @block.vector
        def _(dve):
            for i, (src, hi, lo) in enumerate(pieces):
                dve.wait_ge(hi_done, i + 1)
                dve.wait_ge(loaded[i % RING], 16 * (i // RING + 1))
                dve.tensor_tensor(lo, slot(i, hi.shape[-1]), raw(hi), ALU.subtract).then_inc(lo_done, 1)


def project(nc, t, dr, keep, l):
    with ExitStack() as outer:
        w = Scope(nc, outer, f"pw{l}")
        win_hi, win_lo = w.sb("win_hi", [P, KT, D_IN], F32R), w.sb("win_lo", [P, KT, D_IN], F32R)
        wq_hi, wq_lo = w.sb("wq_hi", [P, 2, QUP], F32R), w.sb("wq_lo", [P, 2, QUP], F32R)
        wkv_hi, wkv_lo = w.sb("wkv_hi", [P, KVUP], F32R), w.sb("wkv_lo", [P, KVUP], F32R)
        pieces = [(t["w_in"][l, k * P:(k + 1) * P, :], win_hi[:, k, :], win_lo[:, k, :]) for k in range(KT)]
        pieces += [(t["mla_w_q_up"][l, k * P:(k + 1) * P, :], wq_hi[:, k, :], wq_lo[:, k, :]) for k in range(2)]
        pieces += [(t["mla_w_kv_up"][l], wkv_hi[:], wkv_lo[:])]
        split_weights(nc, f"ps{l}", pieces, D_IN)
        with ExitStack() as ctx:
            s = Scope(nc, ctx, f"pj{l}")
            xt = s.sb("xt", [P, 3, D])
            junk = s.sb("junk", [P, D], BF16)
            junk_c = s.sb("junk_c", [P, 384], BF16)
            hT_hi, hT_lo = s.sb("hT_hi", [P, 2, KT, P], F32R), s.sb("hT_lo", [P, 2, KT, P], F32R)
            R = s.sb("R", [P, R_ALL])
            T_hi, T_lo = s.sb("T_hi", [P, 16, P], F32R), s.sb("T_lo", [P, 16, P], F32R)
            V_hi, V_lo = s.sb("V_hi", [P, VW], F32R), s.sb("V_lo", [P, VW], F32R)
            cn = s.sb("cn", [P, 384])
            cT_hi, cT_lo = s.sb("cT_hi", [P, 3, P], F32R), s.sb("cT_lo", [P, 3, P], F32R)
            rot64, rot32 = s.sb("rot64", [P, 2, TX, 64]), s.sb("rot32", [P, 2, TX, 32])
            turn = s.sb("turn", [P, 512])
            ss, ms, rs = s.sb("ss", [P, 2, 4]), s.sb("ms", [P, 2, 4]), s.sb("rs", [P, 2, 4])
            pj = s.ps("pj", [P, 4 * BANK])
            pt = s.ps("pt", [P, 2 * BANK])
            pu = s.ps("pu", [P, 2 * BANK])
            x_loaded = [s.sem(f"x_loaded{b}") for b in range(3)]
            names = ("rot_loaded x_squared x_rms x_normed h_turned h_full h_hi h_lo proj_done c_squared "
                     " c_rms c_normed c_turned c_full c_hi c_lo q_up kv_up q_read_dve "
                     "q_read_act kv_read_dve kv_read_act r_turned t_hi t_lo v_hi v_lo pool_own dve_own t_stored0 t_stored1 v_stored "
                     "ropeA_done ropeB_done kr_done")
            S = {n: s.sem(n) for n in names.split()}
            block = ctx.enter_context(nc.Block())

            def src(i):
                if l == 0:
                    return t["x"][0, i * P:(i + 1) * P, :] if i < TX else t["ctx"][0, (i - TX) * P:(i - TX + 1) * P, :]
                return dr["x"][i * P:(i + 1) * P, :]

            def store(sp, i):
                store_turned(sp, i, 0)
                sp.wait_ge(S["v_hi"], 3 * (i + 1))
                sp.wait_ge(S["v_lo"], 3 * (i + 1))
                for j, v in enumerate((V_hi, V_lo)):
                    sp.dma_start(dr["V"][j, i * P:(i + 1) * P, :], raw(v[:])).then_inc(S["v_stored"], 16)
                store_turned(sp, i, 1)

            def store_turned(sp, i, half):
                sp.wait_ge(S["t_hi"], 4 * i + 2 * half + 2)
                sp.wait_ge(S["t_lo"], 4 * i + 2 * half + 2)
                for j, v in enumerate((T_hi, T_lo)):
                    sp.dma_start(dr["T"][j, half * D:(half + 1) * D, i * P:(i + 1) * P
                                         ].rearrange("(b p) n -> p b n", p=P),
                                 raw(v[:, 8 * half:8 * half + 8])).then_inc(S[f"t_stored{half}"], 16)

            @block.sync
            def _(sp):
                sp.dma_start(rot64[:], t["rot64"]).then_inc(S["rot_loaded"], 16)
                sp.dma_start(rot32[:], t["rot32"]).then_inc(S["rot_loaded"], 16)
                for i in range(3):
                    sp.dma_start(xt[:, i, :], src(i)).then_inc(x_loaded[i], 16)
                for i in range(TT):
                    if i + 3 < TT:
                        sp.wait_ge(S["h_lo"], i + 1)
                        sp.dma_start(xt[:, i % 3, :], src(i + 3)).then_inc(x_loaded[i % 3], 16)
                    store(sp, i)
                sp.wait_ge(S["t_stored0"], 32 * TT)
                sp.wait_ge(S["t_stored1"], 32 * TT)
                sp.wait_ge(S["v_stored"], 32 * TT)

            @block.gpsimd
            def _(pool):
                own = 0

                def rsqrt(cols, i, divs):
                    nonlocal own
                    b = i % 2
                    for c, n in zip(cols, divs):
                        pool.tensor_scalar(ms[:, b, c:c + 1], ss[:, b, c:c + 1], 1.0 / n, EPS, ALU.mult, ALU.add
                                           ).then_inc(S["pool_own"], 1)
                        own += 1
                    pool.wait_ge(S["pool_own"], own)
                    lo, hi = cols[0], cols[-1] + 1
                    return pool.tensor_tensor(rs[:, b, lo:hi], ms[:, b, lo:hi],
                                              keep["mhalf"][:, 0:hi - lo], ALU.pow)

                def x_rms(i):
                    pool.wait_ge(S["x_squared"], i + 1)
                    if i >= 2:
                        pool.wait_ge(S["x_normed"], i - 1)
                    rsqrt([0], i, [D]).then_inc(S["x_rms"], 1)

                x_rms(0)
                for i in range(TT):
                    if i + 1 < TT:
                        x_rms(i + 1)
                    pool.wait_ge(S["c_squared"], 2 * (i + 1))
                    if i >= 2:
                        pool.wait_ge(S["c_normed"], i - 1)
                    rsqrt([1, 2], i, [QR, KVR]).then_inc(S["c_rms"], 1)

            @block.scalar
            def _(act):
                def x_norm(i):
                    b = i % 2
                    act.wait_ge(x_loaded[i % 3], 16 * (i // 3 + 1))
                    if i >= 2:
                        act.wait_ge(S["x_rms"], i - 1)
                    act.activation(junk[:], xt[:, i % 3, :], ACT.Square, accum_out=ss[:, b, 0:1]
                                   ).then_inc(S["x_squared"], 1)
                    act.wait_ge(S["x_rms"], i + 1)
                    act.activation(xt[:, i % 3, :], xt[:, i % 3, :], ACT.Copy, scale=rs[:, b, 0:1]
                                   ).then_inc(S["x_normed"], 1)

                def h_split(i):
                    act.wait_ge(S["h_full"], i + 1)
                    if i >= 2:
                        act.wait_ge(S["proj_done"], 4 * (i - 1))
                    act.copy(hT_hi[:, i % 2].rearrange("p k n -> p (k n)"), xt[:, i % 3, :]).then_inc(S["h_hi"], 1)

                def r_split(i, g, bank):
                    act.wait_ge(S["r_turned"], 4 * i + g + 1)
                    if g % 2 == 0 and i >= 1:
                        act.wait_ge(S[f"t_stored{g // 2}"], 32 * i)
                    act.copy(T_hi[:, 4 * g:4 * g + 4].rearrange("p b n -> p (b n)"), bank).then_inc(S["t_hi"], 1)

                def latent(i):
                    act.wait_ge(S["c_full"], i + 1)
                    if i >= 1:
                        act.wait_ge(S["kv_up"], i)
                    act.copy(cT_hi[:].rearrange("p k n -> p (k n)"), cn[:]).then_inc(S["c_hi"], 1)
                    r_split(i, 0, pt[:, BANK:2 * BANK])
                    r_split(i, 1, pu[:, 0:BANK])
                    act.wait_ge(S["q_up"], i + 1)
                    if i >= 1:
                        act.wait_ge(S["r_turned"], 4 * i)
                    act.copy(heads_of(R[:, R_CQ:R_CN], 6)[:, :, 0:64], heads_of(pu[:, 0:QUP], 6)[:, :, 0:64]
                             ).then_inc(S["q_read_act"], 1)
                    act.wait_ge(S["kv_up"], i + 1)
                    kv = heads_of(pt[:, 0:KVUP], 6)
                    act.copy(heads_of(R[:, R_CN:R_KR], 6), kv[:, :, 0:64]).then_inc(S["kv_read_act"], 1)
                    act.copy(heads_of(V_hi[:, V_C:VW], 6), kv[:, :, 64:128]).then_inc(S["v_hi"], 1)

                x_norm(0)
                h_split(0)
                for i in range(TT):
                    if i + 1 < TT:
                        x_norm(i + 1)
                    if i >= 1:
                        latent(i - 1)
                    if i + 1 < TT:
                        h_split(i + 1)
                    if i >= 1:
                        r_split(i - 1, 2, pu[:, 0:BANK])
                        r_split(i - 1, 3, pu[:, BANK:2 * BANK])
                    act.wait_ge(S["proj_done"], 4 * i + 2)
                    if i >= 1:
                        act.wait_ge(S["v_stored"], 32 * i)
                    act.copy(V_hi[:, V_A:V_B], pj[:, IN_AV:IN_BQ]).then_inc(S["v_hi"], 1)
                    act.wait_ge(S["proj_done"], 4 * i + 3)
                    act.copy(V_hi[:, V_B:V_C], pj[:, IN_BV:IN_CQ]).then_inc(S["v_hi"], 1)
                    act.wait_ge(S["proj_done"], 4 * i + 4)
                    if i >= 1:
                        act.wait_ge(S["c_rms"], i)
                    act.activation(junk_c[:, 0:QR], pj[:, PJ_CQ:PJ_CKV], ACT.Square, accum_out=ss[:, i % 2, 1:2]
                                   ).then_inc(S["c_squared"], 1)
                    act.activation(junk_c[:, QR:384], pj[:, PJ_CKV:PJ_KR], ACT.Square, accum_out=ss[:, i % 2, 2:3]
                                   ).then_inc(S["c_squared"], 1)
                latent(TT - 1)
                r_split(TT - 1, 2, pu[:, 0:BANK])
                r_split(TT - 1, 3, pu[:, BANK:2 * BANK])

            @block.tensor
            def _(pe):
                def h_turn(i):
                    pe.wait_ge(S["x_normed"], i + 1)
                    if i >= 1:
                        pe.wait_ge(S["h_full"], i)
                    if i >= 2:
                        pe.wait_ge(S["kv_read_act"], i - 1)
                        pe.wait_ge(S["v_hi"], 3 * (i - 1))
                        pe.wait_ge(S["v_lo"], 3 * (i - 1))
                    for k in range(KT):
                        mm = pe.transpose(pt[:, k * P:(k + 1) * P], xt[:, i % 3, k * P:(k + 1) * P], keep["ident"][:])
                    mm.then_inc(S["h_turned"], 1)

                def proj(i, n):
                    a, b = IN_BANKS[n], IN_BANKS[n + 1]
                    if n == 0:
                        pe.wait_ge(S["h_hi"], i + 1)
                        pe.wait_ge(S["h_lo"], i + 1)
                        if i >= 1:
                            pe.wait_ge(S["ropeA_done"], i)
                    if n == 1 and i >= 1:
                        pe.wait_ge(S["c_normed"], i)
                        pe.wait_ge(S["c_squared"], 2 * i)
                    for k in range(KT):
                        mm = three_pass(pe, pj[:, n * BANK:n * BANK + b - a], hT_hi[:, i % 2, k, :], hT_lo[:, i % 2, k, :],
                                        win_hi[:, k, a:b], win_lo[:, k, a:b], k == 0, k == KT - 1)
                    mm.then_inc(S["proj_done"], 1)

                def r_turn(i, g, bank):
                    for b in range(4):
                        c = (4 * g + b) * P
                        mm = pe.transpose(bank[:, b * P:(b + 1) * P], R[:, c:c + P], keep["ident"][:])
                    mm.then_inc(S["r_turned"], 1)

                def latent(i, step):
                    if step == 0:
                        pe.wait_ge(S["c_normed"], i + 1)
                        pe.wait_ge(S["h_full"], min(i + 2, TT))
                        for k in range(3):
                            mm = pe.transpose(pt[:, k * P:(k + 1) * P], cn[:, k * P:(k + 1) * P], keep["ident"][:])
                        mm.then_inc(S["c_turned"], 1)
                        r_turn(i, 0, pt[:, BANK:2 * BANK])
                        if i >= 1:
                            pe.wait_ge(S["t_hi"], 4 * i)
                            pe.wait_ge(S["t_lo"], 4 * i)
                        r_turn(i, 1, pu[:, 0:BANK])
                    elif step == 1:
                        pe.wait_ge(S["c_hi"], i + 1)
                        pe.wait_ge(S["c_lo"], i + 1)
                        pe.wait_ge(S["t_hi"], 4 * i + 2)
                        pe.wait_ge(S["t_lo"], 4 * i + 2)
                        for a, b in ((0, BANK), (BANK, QUP)):
                            for k in range(2):
                                mm = three_pass(pe, pu[:, a:b], cT_hi[:, k, :], cT_lo[:, k, :],
                                                wq_hi[:, k, a:b], wq_lo[:, k, a:b], k == 0, k == 1)
                        mm.then_inc(S["q_up"], 1)
                        for a, b in ((0, BANK), (BANK, KVUP)):
                            mm = three_pass(pe, pt[:, a:b], cT_hi[:, 2, :], cT_lo[:, 2, :],
                                            wkv_hi[:, a:b], wkv_lo[:, a:b], True, True)
                        mm.then_inc(S["kv_up"], 1)
                    else:
                        pe.wait_ge(S["q_read_act"], i + 1)
                        pe.wait_ge(S["q_read_dve"], i + 1)
                        pe.wait_ge(S["kv_read_act"], i + 1)
                        r_turn(i, 2, pu[:, 0:BANK])
                        r_turn(i, 3, pu[:, BANK:2 * BANK])

                h_turn(0)
                for i in range(TT):
                    proj(i, 0)
                    if i >= 1:
                        latent(i - 1, 0)
                    proj(i, 1)
                    if i >= 1:
                        latent(i - 1, 1)
                    proj(i, 2)
                    if i + 1 < TT:
                        h_turn(i + 1)
                    if i >= 1:
                        latent(i - 1, 2)
                    proj(i, 3)
                for step in range(3):
                    latent(TT - 1, step)

            @block.vector
            def _(dve):
                linked = 0

                def link(ins):
                    nonlocal linked
                    linked += 1
                    ins.then_inc(S["dve_own"], 1)
                    dve.wait_ge(S["dve_own"], linked)

                def h_full(i):
                    dve.wait_ge(S["h_turned"], i + 1)
                    c = 0 if i < TX else 1
                    for k in range(KT):
                        ins = dve.tensor_scalar(xt[:, i % 3, k * P:(k + 1) * P], pt[:, k * P:(k + 1) * P],
                                                keep["modT"][:, l, 1, k, c:c + 1], keep["modT"][:, l, 0, k, c:c + 1],
                                                ALU.mult, ALU.add)
                    ins.then_inc(S["h_full"], 1)

                def h_lo(i):
                    dve.wait_ge(S["h_hi"], i + 1)
                    dve.wait_ge(S["h_full"], i + 1)
                    if i >= 2:
                        dve.wait_ge(S["proj_done"], 4 * (i - 1))
                    dve.tensor_tensor(hT_lo[:, i % 2].rearrange("p k n -> p (k n)"), xt[:, i % 3, :],
                                      raw(hT_hi[:, i % 2].rearrange("p k n -> p (k n)")), ALU.subtract
                                      ).then_inc(S["h_lo"], 1)

                turn_used = None

                def place(dst, src_ap, heads, dim, tables, i, done):
                    nonlocal turn_used
                    if i >= TX:
                        dve.tensor_copy(dst, src_ap).then_inc(done, 1)
                        return
                    if turn_used is not None:
                        dve.wait_ge(*turn_used)
                    turn_used = (done, i + 1)
                    q = dim // 4
                    cos = tables[:, 0, i, :].unsqueeze(1).to_broadcast([P, heads, dim])
                    sin = tables[:, 1, i, :].rearrange("p (a s j) -> p a s j", a=2, s=2)
                    tv = turn[:, 0:heads * dim].rearrange("p (h a s j) -> p h a s j", h=heads, a=2, s=2)
                    sv = src_ap.rearrange("p h (a s j) -> p h a s j", a=2, s=2)
                    for z in range(2):
                        dve.tensor_tensor(tv[:, :, :, z, :], sv[:, :, :, 1 - z, :],
                                          sin[:, :, z, :].unsqueeze(1).to_broadcast([P, heads, 2, q]), ALU.mult)
                    link(dve.tensor_tensor(dst, src_ap, cos, ALU.mult))
                    dve.tensor_tensor(dst, dst, turn[:, 0:heads * dim].rearrange("p (h e) -> p h e", h=heads),
                                      ALU.add).then_inc(done, 1)

                def values_lo(i, part, src_ap, dst, hi):
                    dve.wait_ge(S["v_hi"], 3 * i + part + 1)
                    if i >= 1 and part == 0:
                        dve.wait_ge(S["v_stored"], 32 * i)
                    dve.tensor_tensor(dst, src_ap, raw(hi), ALU.subtract).then_inc(S["v_lo"], 1)

                def r_lo(i, g, bank):
                    dve.wait_ge(S["t_hi"], 4 * i + g + 1)
                    if g % 2 == 0 and i >= 1:
                        dve.wait_ge(S[f"t_stored{g // 2}"], 32 * i)
                    dve.tensor_tensor(T_lo[:, 4 * g:4 * g + 4].rearrange("p b n -> p (b n)"), bank,
                                      raw(T_hi[:, 4 * g:4 * g + 4].rearrange("p b n -> p (b n)")), ALU.subtract
                                      ).then_inc(S["t_lo"], 1)

                def latent(i, step):
                    if step == 0:
                        dve.wait_ge(S["c_turned"], i + 1)
                        for k in range(3):
                            ins = dve.tensor_scalar(cn[:, k * P:(k + 1) * P], pt[:, k * P:(k + 1) * P],
                                                    keep["cnorm"][:, l, k:k + 1], None, ALU.mult)
                        ins.then_inc(S["c_full"], 1)
                        dve.wait_ge(S["c_full"], i + 1)
                        dve.wait_ge(S["c_hi"], i + 1)
                        if i >= 1:
                            dve.wait_ge(S["kv_up"], i)
                        dve.tensor_tensor(cT_lo[:].rearrange("p k n -> p (k n)"), cn[:],
                                          raw(cT_hi[:].rearrange("p k n -> p (k n)")), ALU.subtract
                                          ).then_inc(S["c_lo"], 1)
                        r_lo(i, 0, pt[:, BANK:2 * BANK])
                        r_lo(i, 1, pu[:, 0:BANK])
                    elif step == 1:
                        dve.wait_ge(S["q_read_act"], i + 1)
                        if i >= 1:
                            dve.wait_ge(S["r_turned"], 4 * i)
                        place(heads_of(R[:, R_CQ:R_CN], 6)[:, :, 64:96], heads_of(pu[:, 0:QUP], 6)[:, :, 64:96],
                              6, 32, rot32, i, S["q_read_dve"])
                        dve.wait_ge(S["kv_up"], i + 1)
                        values_lo(i, 2, heads_of(pt[:, 0:KVUP], 6)[:, :, 64:128],
                                  heads_of(V_lo[:, V_C:VW], 6), heads_of(V_hi[:, V_C:VW], 6))
                    else:
                        r_lo(i, 2, pu[:, 0:BANK])
                        r_lo(i, 3, pu[:, BANK:2 * BANK])

                dve.memset(R[:, R_KR + 32:R_ALL], 0.0)
                dve.wait_ge(S["rot_loaded"], 32)
                h_full(0)
                h_lo(0)
                for i in range(TT):
                    dve.wait_ge(S["proj_done"], 4 * i + 1)
                    if i >= 1:
                        latent(i - 1, 0)
                        dve.wait_ge(S["r_turned"], 4 * (i - 1) + 2)
                    place(heads_of(R[:, R_AQ:R_BQ], 8), heads_of(pj[:, IN_AQ:IN_AV], 8), 8, 64, rot64, i,
                          S["ropeA_done"])
                    if i >= 1:
                        latent(i - 1, 1)
                    if i + 1 < TT:
                        h_full(i + 1)
                    if i + 1 < TT:
                        h_lo(i + 1)
                    dve.wait_ge(S["v_hi"], 3 * i + 2)
                    place(heads_of(R[:, R_BQ:R_CQ], 16), heads_of(pj[:, IN_BQ:IN_BV], 16), 16, 32, rot32, i,
                          S["ropeB_done"])
                    if i >= 1:
                        latent(i - 1, 2)
                    values_lo(i, 0, pj[:, IN_AV:IN_BQ], V_lo[:, V_A:V_B], V_hi[:, V_A:V_B])
                    values_lo(i, 1, pj[:, IN_BV:IN_CQ], V_lo[:, V_B:V_C], V_hi[:, V_B:V_C])
                    dve.wait_ge(S["c_squared"], 2 * (i + 1))
                    if i >= 1:
                        dve.wait_ge(S["r_turned"], 4 * i)
                    place(heads_of(R[:, R_KR:R_KR + 32], 1), heads_of(pj[:, PJ_KR:PJ_END], 1), 1, 32, rot32, i,
                          S["kr_done"])
                    dve.wait_ge(S["c_rms"], i + 1)
                    if i >= 1:
                        dve.wait_ge(S["c_hi"], i)
                        dve.wait_ge(S["c_lo"], i)
                    dve.tensor_scalar(cn[:, 0:QR], pj[:, PJ_CQ:PJ_CKV], rs[:, i % 2, 1:2], None, ALU.mult)
                    dve.tensor_scalar(cn[:, QR:384], pj[:, PJ_CKV:PJ_KR], rs[:, i % 2, 2:3], None, ALU.mult
                                      ).then_inc(S["c_normed"], 1)
                for step in range(3):
                    latent(TT - 1, step)


def attention_plan(l):
    order = [("C", 0), ("A", 0), ("C", 1), ("B", 0), ("B", 1), ("C", 2), ("A", 1), ("C", 3), ("B", 2), ("B", 3),
             ("C", 4), ("B", 4), ("B", 5), ("C", 5), ("B", 6), ("B", 7)]
    units = [(kind, i, {"A": i, "B": 2 + i // 2, "C": 6 + i}[kind]) for kind, i in order]
    queries = TT if l < DEPTH - 1 else TX
    ctx_keys = list(range(TX, TT))
    steps, chunks, maxima, bounds = [], [], [], []
    for u, (kind, _, _) in enumerate(units):
        first = len(steps)
        if kind == "A":
            for q in range(queries):
                near = [] if q >= TX else [(k, m) for k, m in ((q - 1, "above"), (q, None), (q + 1, "below"))
                                           if 0 <= k < TX]
                for k, m in near + [(k, None) for k in ctx_keys]:
                    steps.append((u, len(chunks), k, m))
                chunks.append((u, q, 1, len(steps) - 1))
            rows = [(q, h) for h in range(3) for q in range(queries)]
            parts = (0,)
        else:
            for q, n in ((0, 4), (4, 4)) + (((TX, TC),) if queries > TX else ()):
                for k in (range(TT) if q < TX else ctx_keys):
                    steps.append((u, len(chunks), k, None))
                chunks.append((u, q, n, len(steps) - 1))
            rows = [(q, 0) for q in range(queries)]
            parts = (0, 1)
        tiles = []
        for j in range(0, len(rows), 2):
            tiles.append((2, rows[j:j + 2]))
            tiles += [(part, [row]) for row in rows[j:j + 2] if row[0] < TX for part in parts]
        maxima.append(tiles)
        bounds.append((first, len(steps)))
    return units, steps, chunks, maxima, bounds, queries


def attend(nc, t, dr, keep, l):
    units, steps, chunks, maxima, bounds, queries = attention_plan(l)
    G, LAG, RING, SRING = len(steps), 4, 6, 3
    NORM, SQUARE, MEAN, ROOT, FINAL, HI2, LO2, STORE = (LAG + x for x in range(1, 9))
    HI1, LO1 = SQUARE, MEAN
    TAIL = STORE + 1
    ends = {c[3]: n for n, c in enumerate(chunks)}
    starts = {b[0]: u for u, b in enumerate(bounds)}
    SCALE = {"A": A_SCALE, "B": B_SCALE, "C": C_SCALE}
    max_base = [sum(len(m) for m in maxima[:u]) for u in range(len(units))]
    TURN = 4
    jobs = [(-1, "tile", 0, j) for j in range(len(maxima[0]))] + [(-1, "turn", 0, 0)]
    for u in range(1, len(units)):
        a, b = bounds[u - 1][0] + 2, bounds[u - 1][1] - 10
        if units[u][0] == "B" and units[u][1] % 2 == 1:
            a, b = bounds[u - 2][1] - 10, bounds[u - 1][0] + 7
        elif units[u][0] == "B":
            b -= 2
        at = [a + j * (b - a) // len(maxima[u]) for j in range(len(maxima[u]))]
        jobs += [(g, "tile", u, j) for j, g in enumerate(at)] + [(at[-1] + TURN, "turn", u, 0)]
    jobs.sort(key=lambda job: job[0])
    jobs_at, bank_free = {}, []
    for x, (g, what, u, j) in enumerate(jobs):
        jobs_at.setdefault(g, []).append((what, u, j, x))
        bank_free.append(("mx_read", max_base[u] + j + 1) if what == "tile" else ("mneg_done", u + 1))
    two_maps = [units[c[0]][0] == "B" for c in chunks]
    kept = [units[c[0]][0] == "B" and units[c[0]][1] % 2 == 0 for c in chunks]
    order = [sum(not k for k in kept[:n]) for n in range(len(chunks))]
    second = [n for n in range(len(chunks)) if two_maps[n] and not kept[n]]
    nth_second = {n: j for j, n in enumerate(second)}
    before_slot = lambda g, lag: [n for e, n in ends.items() if e == g - lag]
    nth_a = [sum(x[0] == "A" for x in units[:u]) for u in range(len(units))]
    nth_a_chunk = [sum(units[c[0]][0] == "A" for c in chunks[:n]) for n in range(len(chunks))]
    v_load = [len({x[2] for x in units[:u + 1]}) - 1 for u in range(len(units))]

    with ExitStack() as ctx:
        s = Scope(nc, ctx, f"at{l}")
        WB = [s.sb(f"W{b}", [P, 4, TOK], F32R) for b in range(3)]
        WA = s.sb("WA", [P, 8, TOK], F32R)
        Vh = [s.sb(f"Vh{b}", [P, TT, P], F32R) for b in range(2)]
        Vl = [s.sb(f"Vl{b}", [P, TT, P], F32R) for b in range(2)]
        E = s.sb("E", [P, RING, BANK])
        H, L = s.sb("H", [P, RING, BANK], F32R), s.sb("L", [P, RING, BANK], F32R)
        esink = s.sb("esink", [65, 3, TOK])
        zero_one = s.sb("zero_one", [65, P])
        mean64 = s.sb("mean64", [64, 64])
        mcol = s.sb("mcol", [P, 2, 3 * TT])
        mpart = s.sb("mpart", [P, 2, 2, 3, TT])
        mrow = s.sb("mrow", [3 * TT, P], F32R)
        logs, rec = s.sb("logs", [64, BANK]), s.sb("rec", [64, BANK])
        first_map = s.sb("first_map", [64, TOK])
        o = s.sb("o", [64, 3, BANK])
        osq, orn = s.sb("osq", [64, BANK]), s.sb("orn", [64, BANK])
        o_hi, o_lo = s.sb("o_hi", [64, 2, BANK], F32R), s.sb("o_lo", [64, 2, BANK], F32R)
        sc = s.ps("sc", [P, SRING, BANK])
        av = s.ps("av", [P, 2, BANK])
        mx = s.ps("mx", [P, 3, BANK])
        qk_loaded = [s.sem(f"qk_loaded{b}") for b in range(4)]
        v_loaded = [s.sem(f"v_loaded{b}") for b in range(2)]
        o_stored = [s.sem(f"o_stored{b}") for b in range(2)]
        names = ("s_done e_done h_done l_done av_done chunk_done o_done sink_done mx_done mx_read mcol_done mt_done "
                 "mneg_done mrow_loaded consts_done dve_own o_squared mean_done ln_read rn_done o_final o_hi_done "
                 "o_lo_done log_done rec_done")
        S = {n: s.sem(n) for n in names.split()}
        block = ctx.enter_context(nc.Block())
        NLOAD = 7

        rows_loaded = [16 * sum(3 if x[0] == "A" else 1 for x in units[:u + 1]) for u in range(len(units))]

        def rows_of(u):
            return queries * (3 if units[u][0] == "A" else 1)

        def mcol_view(u):
            return mcol[:, u % 2, 0:rows_of(u)].rearrange("p (h q) -> p h q", q=queries)

        def width(n):
            return 3 * P if units[chunks[n][0]][0] == "A" else chunks[n][2] * P

        slot = [3 if x[0] == "A" else (u - nth_a[u]) % 3 for u, x in enumerate(units)]
        W = [WA if b == 3 else WB[b] for b in slot]
        holders = [[x for x in range(u) if slot[x] == slot[u]] for u in range(len(units))]

        def use(u):
            return len(holders[u]) + 1

        @block.sync
        def _(sp):
            T, V, ones = dr["T"], dr["V"], dr["ones"]

            def load(u):
                kind, i, v = units[u]
                w, sem = W[u], qk_loaded[slot[u]]
                if holders[u]:
                    sp.wait_ge(S["s_done"], bounds[holders[u][-1]][1])
                    if kind == "A":
                        sp.wait_ge(S["sink_done"], 3 * nth_a[u])
                if kind == "A":
                    q = [T[j, R_AQ + 192 * i:R_AQ + 192 * (i + 1), :].rearrange("(h p) n -> p h n", h=3)
                         for j in range(2)]
                    k = [T[j, R_AK + 64 * i:R_AK + 64 * (i + 1), :] for j in range(2)]
                    moves = [(w[0:64, 0:3, :], q[0]), (w[64:128, 0:3, :], q[0]), (w[0:64, 6, :], k[0]),
                             (w[64:128, 6, :], k[1]), (w[0:64, 3:6, :], q[1]), (w[0:64, 7, :], k[0]),
                             (w[64:65, 7, :], ones)]
                elif kind == "B":
                    q = [T[j, R_BQ + 32 * i:R_BQ + 32 * (i + 1), :] for j in range(2)]
                    k = [T[j, R_BK + 32 * i:R_BK + 32 * (i + 1), :] for j in range(2)]
                    moves = [(w[0:32, 0, :], q[0]), (w[32:64, 0, :], q[0]), (w[64:96, 0, :], q[1]),
                             (w[0:32, 1, :], k[0]), (w[32:64, 1, :], k[1]), (w[64:96, 1, :], k[0]),
                             (w[96:97, 1, :], ones)]
                else:
                    q = [T[j, R_CQ + 96 * i:R_CQ + 96 * (i + 1), :] for j in range(2)]
                    k = [T[j, R_CN + 64 * i:R_CN + 64 * (i + 1), :] for j in range(2)]
                    kr = [T[j, R_KR:R_KR + 32, :] for j in range(2)]
                    moves = [(w[0:96, 0, :], q[0]), (w[0:96, 2, :], q[1]), (w[0:64, 1, :], k[0]),
                             (w[64:96, 1, :], kr[0]), (w[96:97, 1, :], ones), (w[0:64, 3, :], k[1]),
                             (w[64:96, 3, :], kr[1])]
                for at, (dst, src) in enumerate(moves):
                    if u == 1 and at == 4:
                        sp.wait_ge(S["mrow_loaded"], rows_loaded[0])
                    sp.dma_start(raw(dst), src).then_inc(sem, 16)

            def load_values(u):
                v = units[u][2]
                if u == 0 or v_load[u - 1] != v_load[u]:
                    if v_load[u] < 2:
                        sp.wait_ge(S["consts_done"], 7)
                    else:
                        last = max(x for x in range(u) if v_load[x] == v_load[u] - 2)
                        sp.wait_ge(S["av_done"], bounds[last][1])
                    for j, buf in enumerate((Vh, Vl)):
                        sp.dma_start(raw(buf[v_load[u] % 2][:, :, 0:64]),
                                     V[j, :, 64 * v:64 * (v + 1)].rearrange("(k p) e -> p k e", p=P)
                                     ).then_inc(v_loaded[v_load[u] % 2], 16)

            def store(n):
                u, q, tiles, _ = chunks[n]
                kind, i, _ = units[u]
                b = order[n] % 2
                sp.wait_ge(S["o_lo_done"], order[n] + 1)
                for j, buf in enumerate((o_hi, o_lo)):
                    if kind == "A":
                        dst = dr["mix"][j, 192 * i:192 * (i + 1), q * P:(q + 1) * P].rearrange("(h p) n -> p h n", h=3)
                        src = buf[:, b, 0:3 * P].rearrange("p (h n) -> p h n", h=3)
                    else:
                        row = 384 + 64 * (i // 2) if kind == "B" else 640 + 64 * i
                        dst = dr["mix"][j, row:row + 64, q * P:(q + tiles) * P]
                        src = buf[:, b, 0:tiles * P]
                    sp.dma_start(dst, raw(src)).then_inc(o_stored[b], 16)

            load(0)
            load_values(0)
            load(1)
            for g in range(G + TAIL):
                if g in starts and starts[g] + 2 < len(units):
                    load(starts[g] + 2)
                if g - LAG - 2 in starts and starts[g - LAG - 2] + 1 < len(units):
                    load_values(starts[g - LAG - 2] + 1)
                for n in before_slot(g, STORE):
                    if not kept[n]:
                        store(n)
            total = order[-1] + 1
            for b in range(2):
                sp.wait_ge(o_stored[b], 32 * ((total + 1 - b) // 2))

        @block.gpsimd
        def _(pool):
            for b in range(2):
                pool.memset(raw(Vh[b][:, :, 64:128]), 1.0).then_inc(S["consts_done"], 1)
                pool.memset(raw(Vl[b][:, :, 64:128]), 0.0).then_inc(S["consts_done"], 1)
            pool.wait_ge(S["consts_done"], 4)
            pool.memset(zero_one[64:65, 0:64], 0.0).then_inc(S["consts_done"], 1)
            pool.wait_ge(S["consts_done"], 5)
            pool.memset(zero_one[64:65, 64:128], 1.0).then_inc(S["consts_done"], 1)
            pool.wait_ge(S["consts_done"], 6)
            pool.memset(mean64[:], 1.0 / 64).then_inc(S["consts_done"], 1)

            def lo(n):
                b = order[n] % 2
                pool.wait_ge(S["o_hi_done"], order[n] + 1)
                if n in nth_second:
                    pool.wait_ge(S["o_final"], nth_second[n] + 1)
                else:
                    pool.wait_ge(S["o_done"], n + 1)
                if order[n] >= 2:
                    pool.wait_ge(o_stored[b], 32 * (order[n] // 2))
                pool.tensor_tensor(o_lo[:, b, 0:width(n)], o[:, n % 3, 0:width(n)], raw(o_hi[:, b, 0:width(n)]),
                                  ALU.subtract).then_inc(S["o_lo_done"], 1)

            for g in range(G + TAIL):
                for n in before_slot(g, LO1):
                    if not two_maps[n]:
                        lo(n)
                for n in before_slot(g, LO2):
                    if n in nth_second:
                        lo(n)


        @block.scalar
        def _(act):
            def negate(u, x):
                rows = rows_of(u)
                act.wait_ge(S["mt_done"], u + 1)
                if u >= 1:
                    act.wait_ge(S["mrow_loaded"], rows_loaded[u - 1])
                act.activation(mrow[0:rows, :], mx[0:rows, x % 3, 0:P], ACT.Copy, scale=-1.0
                               ).then_inc(S["mneg_done"], 1)
                act.wait_ge(S["mneg_done"], u + 1)
                if units[u][0] == "A":
                    for h in range(3):
                        act.dma_start(raw(W[u][64:65, 3 + h, 0:queries * P]),
                                      raw(mrow[h * queries:(h + 1) * queries, :])).then_inc(S["mrow_loaded"], 16)
                else:
                    act.dma_start(raw(W[u][96:97, 0, 0:queries * P]), raw(mrow[0:queries, :])
                                  ).then_inc(S["mrow_loaded"], 16)

            def hi(n):
                kind = units[chunks[n][0]][0]
                if kind == "B":
                    act.wait_ge(S["o_final"], nth_second[n] + 1)
                else:
                    act.wait_ge(S["o_done"], n + 1)
                b = order[n] % 2
                if order[n] >= 2:
                    act.wait_ge(o_stored[b], 32 * (order[n] // 2))
                act.copy(o_hi[:, b, 0:width(n)], o[:, n % 3, 0:width(n)]).then_inc(S["o_hi_done"], 1)

            def weight_sums(n):
                w = width(n)
                if units[chunks[n][0]][0] == "A":
                    act.wait_ge(S["chunk_done"], nth_a_chunk[n] + 1)
                else:
                    act.wait_ge(S["av_done"], chunks[n][3] + 1)
                if n >= 1:
                    act.wait_ge(S["rec_done"], n)
                    act.wait_ge(S["o_done"], n)
                act.activation(logs[:, 0:w], av[64:128, n % 2, 0:w], ACT.Ln).then_inc(S["log_done"], 1)
                act.wait_ge(S["log_done"], n + 1)
                act.activation(rec[:, 0:w], logs[:, 0:w], ACT.Exp, scale=-1.0).then_inc(S["rec_done"], 1)

            act.preload_act_table_set("natural_log_exp_and_others")
            negate(0, jobs_at[-1][-1][-1])
            for g in range(G + TAIL):
                for n in before_slot(g, NORM):
                    weight_sums(n)
                for n in before_slot(g, SQUARE):
                    if n in nth_second:
                        j = nth_second[n]
                        act.wait_ge(S["o_done"], n + 1)
                        if j >= 1:
                            act.wait_ge(S["mean_done"], j)
                        act.activation(osq[:, 0:width(n)], o[:, n % 3, 0:width(n)], ACT.Square
                                       ).then_inc(S["o_squared"], 1)
                    elif not kept[n]:
                        hi(n)
                for n in before_slot(g, ROOT):
                    if n in nth_second:
                        j = nth_second[n]
                        act.wait_ge(S["mean_done"], j + 1)
                        if j >= 1:
                            act.wait_ge(S["o_final"], j)
                        act.activation(orn[:, 0:width(n)], av[0:64, n % 2, 0:width(n)], ACT.Ln,
                                       bias=keep["eps"][0:64, 0:1]).then_inc(S["ln_read"], 1)
                        act.wait_ge(S["ln_read"], j + 1)
                        act.activation(orn[:, 0:width(n)], orn[:, 0:width(n)], ACT.Exp, scale=-0.5
                                       ).then_inc(S["rn_done"], 1)
                for n in before_slot(g, HI2):
                    if n in nth_second:
                        hi(n)
                if g < G:
                    u, n, _, _ = steps[g]
                    kind, i, _ = units[u]
                    if g in starts and kind == "A":
                        act.wait_ge(S["mrow_loaded"], rows_loaded[u])
                        if nth_a[u]:
                            act.wait_ge(S["chunk_done"], queries)
                        for h in range(3):
                            act.activation(esink[64:65, h, 0:queries * P], raw(W[u][64:65, 3 + h, 0:queries * P]),
                                           ACT.Exp, scale=A_SCALE, bias=keep["sink"][64:65, l, 3 * i + h:3 * i + h + 1]
                                           ).then_inc(S["sink_done"], 1)
                    w = width(n)
                    act.wait_ge(S["s_done"], g + 1)
                    if g >= RING:
                        act.wait_ge(S["l_done"], g - RING + 1)
                        act.wait_ge(S["av_done"], g - RING + 1)
                    act.activation(E[:, g % RING, 0:w], sc[:, g % SRING, 0:w], ACT.Exp, scale=SCALE[kind]
                                   ).then_inc(S["e_done"], 1)
                    act.activation(H[:, g % RING, 0:w], sc[:, g % SRING, 0:w], ACT.Exp, scale=SCALE[kind]
                                   ).then_inc(S["h_done"], 1)
                for what, u, _, x in jobs_at.get(g, ()):
                    if what == "turn":
                        negate(u, x)

        @block.tensor
        def _(pe):
            def maximum(u, j, x):
                kind, i, _ = units[u]
                w = W[u]
                part, rows = maxima[u][j]
                keys = w[:, 6, :] if kind == "A" else w[0:96, 1, :]

                def stationary(q, h):
                    cols = slice(q * P, (q + 1) * P)
                    return w[:, h, cols] if kind == "A" else w[0:96, 0, cols]

                if j == 0:
                    pe.wait_ge(qk_loaded[slot[u]], 16 * NLOAD * use(u))
                ring_bank(x)
                bank = mx[:, x % 3, :]
                if part == 2:
                    for z, (q, h) in enumerate(rows):
                        mm = pe.matmul(bank[:, z * CTX:(z + 1) * CTX], stationary(q, h), keys[:, SEQ:TOK],
                                       start=True, stop=True)
                elif kind == "A":
                    q, h = rows[0]
                    a, b = max(q - 1, 0), min(q + 2, TX)
                    mm = pe.matmul(bank[:, 0:(b - a) * P], stationary(q, h), keys[:, a * P:b * P],
                                   start=True, stop=True)
                    for k in range(a, b):
                        if k != q:
                            mm = pe.matmul(bank[:, (k - a) * P:(k - a + 1) * P], keep["identb"][:],
                                           keep["below" if k < q else "above"][:], start=False, stop=True,
                                           skip_group_check=True)
                else:
                    mm = pe.matmul(bank, stationary(*rows[0]), keys[:, part * BANK:(part + 1) * BANK],
                                   start=True, stop=True)
                mm.then_inc(S["mx_done"], 1)

            def ring_bank(x):
                if x >= 3:
                    pe.wait_ge(S[bank_free[x - 3][0]], bank_free[x - 3][1])

            def turn_maxima(u, x):
                rows = rows_of(u)
                pe.wait_ge(S["mcol_done"], u + 1)
                ring_bank(x)
                pe.transpose(mx[0:rows, x % 3, 0:P], mcol_view(u).rearrange("p h q -> p (h q)"), keep["ident"][:]
                             ).then_inc(S["mt_done"], 1)

            def score(g):
                u, n, k, mask = steps[g]
                kind, i, _ = units[u]
                w = W[u]
                _, q, tiles, _ = chunks[n]
                if g in starts:
                    pe.wait_ge(S["mrow_loaded"], rows_loaded[u])
                if g >= SRING:
                    pe.wait_ge(S["h_done"], g - SRING + 1)
                out = sc[:, g % SRING, 0:width(n)]
                keys = slice(k * P, (k + 1) * P)
                cols = slice(q * P, (q + tiles) * P)
                if kind == "A":
                    o3 = out.rearrange("p (h n) -> p h n", h=3)
                    pe.matmul(o3, w[:, 6, keys], w[:, 0:3, cols], start=True, stop=False)
                    mm = pe.matmul(o3, w[0:65, 7, keys], w[0:65, 3:6, cols], start=False, stop=mask is None)
                    if mask is not None:
                        mm = pe.matmul(o3, keep["identb"][:], keep[mask][:].unsqueeze(1).to_broadcast([P, 3, P]),
                                       start=False, stop=True)
                elif kind == "B":
                    mm = pe.matmul(out, w[0:97, 1, keys], w[0:97, 0, cols], start=True, stop=True)
                else:
                    pe.matmul(out, w[0:97, 1, keys], w[0:97, 0, cols], start=True, stop=False)
                    pe.matmul(out, w[0:96, 1, keys], w[0:96, 2, cols], start=False, stop=False)
                    mm = pe.matmul(out, w[0:96, 3, keys], w[0:96, 0, cols], start=False, stop=True)
                mm.then_inc(S["s_done"], 1)

            def values(g):
                u, n, k, _ = steps[g]
                kind, v = units[u][0], v_load[u]
                first, last = g == 0 or steps[g - 1][1] != n, g in ends
                if first:
                    pe.wait_ge(v_loaded[v % 2], 32 * (v // 2 + 1))
                    if n >= 2:
                        pe.wait_ge(S["o_done"], n - 1)
                        if n - 2 in nth_second:
                            pe.wait_ge(S["ln_read"], nth_second[n - 2] + 1)
                pe.wait_ge(S["h_done"], g + 1)
                out = av[:, n % 2, 0:width(n)]
                h, lo = H[:, g % RING, 0:width(n)], L[:, g % RING, 0:width(n)]
                pe.matmul(out, Vh[v % 2][:, k, :], h, start=first, stop=False)
                pe.matmul(out, Vl[v % 2][:, k, :], h, start=False, stop=False)
                pe.wait_ge(S["l_done"], g + 1)
                mm = pe.matmul(out, Vh[v % 2][:, k, :], lo, start=False, stop=last and kind != "A")
                mm.then_inc(S["av_done"], 1)
                if last:
                    if kind == "A":
                        q = chunks[n][1]
                        pe.wait_ge(S["sink_done"], 3 * (nth_a[u] + 1))
                        pe.matmul(out.rearrange("p (h n) -> p h n", h=3), zero_one[64:65, :],
                                  esink[64:65, :, q * P:(q + 1) * P], start=False, stop=True
                                  ).then_inc(S["chunk_done"], 1)

            pe.wait_ge(S["consts_done"], 7)
            def job(what, u, j, x):
                if what == "tile":
                    maximum(u, j, x)
                else:
                    turn_maxima(u, x)

            for each in jobs_at[-1]:
                job(*each)
            for g in range(G + MEAN + 1):
                for n in before_slot(g, MEAN):
                    if n in nth_second:
                        pe.wait_ge(S["o_squared"], nth_second[n] + 1)
                        pe.matmul(av[0:64, n % 2, 0:width(n)], mean64[:], osq[:, 0:width(n)], start=True, stop=True
                                  ).then_inc(S["mean_done"], 1)
                if g < G:
                    score(g)
                ahead = jobs_at.get(g, [])
                for each in ahead[:1]:
                    job(*each)
                if 0 <= g - LAG < G:
                    values(g - LAG)
                for each in ahead[1:]:
                    job(*each)

        @block.vector
        def _(dve):
            linked = 0

            def link(ins):
                nonlocal linked
                linked += 1
                ins.then_inc(S["dve_own"], 1)
                dve.wait_ge(S["dve_own"], linked)

            def reduce_max(u, j, x):
                part, rows = maxima[u][j]
                q, h = rows[0]
                dve.wait_ge(S["mx_done"], max_base[u] + j + 1)
                if j == 0 and u >= 2:
                    dve.wait_ge(S["mt_done"], u - 1)
                if part == 2:
                    first = h * queries + q
                    dst = mcol[:, u % 2, first:first + 2]
                    src = mx[:, x % 3, :].rearrange("p (z n) -> p z n", z=2)
                else:
                    dst = mpart[:, u % 2, part, h, q:q + 1]
                    near = (min(q + 2, TX) - max(q - 1, 0)) * P if units[u][0] == "A" else BANK
                    src = mx[:, x % 3, 0:near]
                dve.reduce_max(dst, src, AX_X).then_inc(S["mx_read"], 1)

            def maxima_done(u):
                kind, i, _ = units[u]
                dve.wait_ge(S["mx_read"], max_base[u] + len(maxima[u]))
                whole = mcol_view(u)
                latent = whole[:, :, 0:TX]
                heads = whole.shape[1]
                ins = dve.tensor_tensor(latent, latent, mpart[:, u % 2, 0, 0:heads, 0:TX], ALU.max)
                link(ins)
                if kind == "A":
                    sink = keep["sinkdiv"][:, l, 3 * i:3 * i + 3].unsqueeze(2).to_broadcast([P, 3, queries])
                    dve.tensor_tensor(whole, whole, sink, ALU.max).then_inc(S["mcol_done"], 1)
                else:
                    dve.tensor_tensor(latent, latent, mpart[:, u % 2, 1, 0:1, 0:TX], ALU.max).then_inc(S["mcol_done"], 1)

            def normalise(n):
                w = width(n)
                if n >= 3 and not kept[n]:
                    done = sum(1 for x in range(n - 2) if not kept[x])
                    if done:
                        dve.wait_ge(S["o_lo_done"], done)
                dve.wait_ge(S["rec_done"], n + 1)
                if not two_maps[n]:
                    dve.tensor_tensor(o[:, n % 3, 0:w], av[0:64, n % 2, 0:w], rec[:, 0:w], ALU.mult
                                      ).then_inc(S["o_done"], 1)
                    return
                c = slice(chunks[n][1] * P, chunks[n][1] * P + w)
                if kept[n]:
                    dve.tensor_tensor(first_map[:, c], av[0:64, n % 2, 0:w], rec[:, 0:w], ALU.mult
                                      ).then_inc(S["o_done"], 1)
                    return
                link(dve.tensor_tensor(o[:, n % 3, 0:w], av[0:64, n % 2, 0:w], rec[:, 0:w], ALU.mult))
                dve.scalar_tensor_tensor(out=o[:, n % 3, 0:w], in0=o[:, n % 3, 0:w],
                                         scalar=keep["neglam"][0:64, l:l + 1], in1=first_map[:, c],
                                         op0=ALU.mult, op1=ALU.add).then_inc(S["o_done"], 1)

            def row_maxima(g):
                for what, u, j, x in jobs_at.get(g, ()):
                    if what == "tile":
                        reduce_max(u, j, x)
                        if j == len(maxima[u]) - 1:
                            maxima_done(u)

            row_maxima(-1)
            for g in range(G + TAIL):
                for n in before_slot(g, NORM):
                    normalise(n)
                for n in before_slot(g, FINAL):
                    if n in nth_second:
                        dve.wait_ge(S["rn_done"], nth_second[n] + 1)
                        w = width(n)
                        dve.scalar_tensor_tensor(out=o[:, n % 3, 0:w], in0=o[:, n % 3, 0:w],
                                                 scalar=keep["dsn"][0:64, l:l + 1], in1=orn[:, 0:w],
                                                 op0=ALU.mult, op1=ALU.mult).then_inc(S["o_final"], 1)
                row_maxima(g)
                if g < G:
                    w = width(steps[g][1])
                    dve.wait_ge(S["h_done"], g + 1)
                    if g >= RING:
                        dve.wait_ge(S["av_done"], g - RING + 1)
                    dve.tensor_tensor(L[:, g % RING, 0:w], E[:, g % RING, 0:w], raw(H[:, g % RING, 0:w]), ALU.subtract
                                      ).then_inc(S["l_done"], 1)


def mix_out(nc, t, dr, keep, l, h_hi, h_lo):
    NT = TT if l < DEPTH - 1 else TX
    with ExitStack() as outer:
        w = Scope(nc, outer, f"mw{l}")
        wo_hi, wo_lo = w.sb("wo_hi", [P, KT, D], F32R), w.sb("wo_lo", [P, KT, D], F32R)
        split_weights(nc, f"ms{l}", [(t["w_out"][l, k * P:(k + 1) * P, :], wo_hi[:, k, :], wo_lo[:, k, :])
                                     for k in range(KT)], D)
        with ExitStack() as ctx:
            s = Scope(nc, ctx, f"mo{l}")
            mix = s.sb("mix", [P, 2, 2, KT, P], F32R)
            x = s.sb("x", [P, 2, D])
            y = s.sb("y", [P, 2, D])
            gate = s.sb("gate", [P, 2, D])
            junk = s.sb("junk", [P, D], BF16)
            ss, ms, rs = s.sb("ss", [P, 2, 2]), s.sb("ms", [P, 2, 2]), s.sb("rs", [P, 2, 2])
            pm = s.ps("pm", [P, 2, 2 * BANK])
            pt = s.ps("pt", [P, 2 * BANK])
            loaded = [s.sem(f"loaded{b}") for b in range(2)]
            x_stored = [s.sem(f"x_stored{b}") for b in range(2)]
            names = ("gate_loaded mm_done m_squared m_rms y_done x_done x_squared x_rms normed turned full hi lo "
                     "pool_own")
            S = {n: s.sem(n) for n in names.split()}
            block = ctx.enter_context(nc.Block())

            @block.sync
            def _(sp):
                for c in range(2):
                    sp.dma_start(gate[:, c, :], dr["gate"][l, 0, c].partition_broadcast(P)).then_inc(S["gate_loaded"], 16)
                def store(i):
                    sp.wait_ge(S["x_done"], i + 1)
                    sp.dma_start(dr["x1"][i * P:(i + 1) * P, :], x[:, i % 2, :]).then_inc(x_stored[i % 2], 16)

                for i in range(NT):
                    b = i % 2
                    if i >= 2:
                        store(i - 2)
                        sp.wait_ge(S["mm_done"], i - 1)
                        sp.wait_ge(x_stored[b], 16 * (i // 2))
                        sp.wait_ge(S["normed"], i - 1)
                    for j in range(2):
                        sp.dma_start(raw(mix[:, b, j]), dr["mix"][j, :, i * P:(i + 1) * P].rearrange("(k p) n -> p k n", p=P)
                                     ).then_inc(loaded[b], 16)
                    if l == 0:
                        src = t["x"][0, i * P:(i + 1) * P, :] if i < TX else t["ctx"][0, (i - TX) * P:(i - TX + 1) * P, :]
                    else:
                        src = dr["x"][i * P:(i + 1) * P, :]
                    sp.dma_start(x[:, b, :], src).then_inc(loaded[b], 16)
                for i in (NT - 2, NT - 1):
                    store(i)
                for b in range(2):
                    sp.wait_ge(x_stored[b], 16 * ((NT + 1 - b) // 2))

            @block.gpsimd
            def _(pool):
                own = 0
                for i in range(NT):
                    b = i % 2
                    for c, before, after in ((0, "m_squared", "m_rms"), (1, "x_squared", "x_rms")):
                        pool.wait_ge(S[before], i + 1)
                        if i >= 2:
                            pool.wait_ge(S["normed"], i - 1)
                            pool.wait_ge(S["y_done"], i - 1)
                        pool.tensor_scalar(ms[:, b, c:c + 1], ss[:, b, c:c + 1], 1.0 / D, EPS, ALU.mult, ALU.add
                                           ).then_inc(S["pool_own"], 1)
                        own += 1
                        pool.wait_ge(S["pool_own"], own)
                        pool.tensor_tensor(rs[:, b, c:c + 1], ms[:, b, c:c + 1], keep["mhalf"][:, 0:1], ALU.pow
                                           ).then_inc(S[after], 1)

            @block.scalar
            def _(act):
                for i in range(NT + 1):
                    if i < NT:
                        act.wait_ge(S["mm_done"], i + 1)
                        if i >= 2:
                            act.wait_ge(S["m_rms"], i - 1)
                        act.activation(junk[:], pm[:, i % 2, :], ACT.Square, accum_out=ss[:, i % 2, 0:1]
                                       ).then_inc(S["m_squared"], 1)
                        act.wait_ge(S["x_done"], i + 1)
                        if i >= 2:
                            act.wait_ge(S["x_rms"], i - 1)
                        act.activation(junk[:], x[:, i % 2, :], ACT.Square, accum_out=ss[:, i % 2, 1:2]
                                       ).then_inc(S["x_squared"], 1)
                        act.wait_ge(S["x_rms"], i + 1)
                        act.activation(y[:, i % 2, :], x[:, i % 2, :], ACT.Copy, scale=rs[:, i % 2, 1:2]
                                       ).then_inc(S["normed"], 1)
                    if i >= 1:
                        j = i - 1
                        act.wait_ge(S["full"], j + 1)
                        act.copy(h_hi[:, :, j * P:(j + 1) * P], y[:, j % 2, :].rearrange("p (k n) -> p k n", k=KT)
                                 ).then_inc(S["hi"], 1)

            @block.tensor
            def _(pe):
                def turn(i):
                    pe.wait_ge(S["normed"], i + 1)
                    if i >= 1:
                        pe.wait_ge(S["full"], i)
                    for k in range(KT):
                        mm = pe.transpose(pt[:, k * P:(k + 1) * P], y[:, i % 2, k * P:(k + 1) * P], keep["ident"][:])
                    mm.then_inc(S["turned"], 1)

                for i in range(NT):
                    b = i % 2
                    pe.wait_ge(loaded[b], 48 * (i // 2 + 1))
                    if i >= 2:
                        pe.wait_ge(S["y_done"], i - 1)
                        pe.wait_ge(S["m_squared"], i - 1)
                    for n in range(2):
                        for k in range(KT):
                            c = slice(n * BANK, (n + 1) * BANK)
                            mm = three_pass(pe, pm[:, b, c], mix[:, b, 0, k, :], mix[:, b, 1, k, :],
                                            wo_hi[:, k, c], wo_lo[:, k, c], k == 0, k == KT - 1)
                    mm.then_inc(S["mm_done"], 1)
                    if i >= 1:
                        turn(i - 1)
                turn(NT - 1)

            @block.vector
            def _(dve):
                dve.wait_ge(S["gate_loaded"], 32)
                for i in range(NT + 1):
                    if i < NT:
                        b, c = i % 2, 0 if i < TX else 1
                        dve.wait_ge(S["m_rms"], i + 1)
                        if i >= 2:
                            dve.wait_ge(S["hi"], i - 1)
                            dve.wait_ge(S["lo"], i - 1)
                        dve.scalar_tensor_tensor(out=y[:, b, :], in0=pm[:, b, :], scalar=rs[:, b, 0:1],
                                                 in1=gate[:, c, :], op0=ALU.mult, op1=ALU.mult).then_inc(S["y_done"], 1)
                        dve.wait_ge(S["y_done"], i + 1)
                        dve.wait_ge(loaded[b], 48 * (i // 2 + 1))
                        dve.tensor_tensor(x[:, b, :], x[:, b, :], y[:, b, :], ALU.add).then_inc(S["x_done"], 1)
                    if i >= 1:
                        j = i - 1
                        c = 0 if j < TX else 1
                        dve.wait_ge(S["turned"], j + 1)
                        for k in range(KT):
                            ins = dve.tensor_scalar(y[:, j % 2, k * P:(k + 1) * P], pt[:, k * P:(k + 1) * P],
                                                    keep["modT"][:, l, 3, k, c:c + 1], keep["modT"][:, l, 2, k, c:c + 1],
                                                    ALU.mult, ALU.add)
                        ins.then_inc(S["full"], 1)
                        dve.wait_ge(S["full"], j + 1)
                        dve.wait_ge(S["hi"], j + 1)
                        sl = slice(j * P, (j + 1) * P)
                        dve.tensor_tensor(h_lo[:, :, sl], y[:, j % 2, :].rearrange("p (k n) -> p k n", k=KT),
                                          raw(h_hi[:, :, sl]), ALU.subtract).then_inc(S["lo"], 1)


def ffn(nc, t, dr, keep, l, h_hi, h_lo, acc):
    NT = TT if l < DEPTH - 1 else TX
    CH = [(a, min(a + BANK, NT * P)) for a in range(0, NT * P, BANK)]
    NC = len(CH)
    PAIRS = FT // 2
    with ExitStack() as ctx:
        s = Scope(nc, ctx, f"ff{l}")
        rawp = [s.sb(f"raw{b}", [P, D]) for b in range(3)]
        w_hi = s.sb("w_hi", [P, 2, 2, D], F32R)
        w_lo = s.sb("w_lo", [P, 2, 2, D], F32R)
        d_hi, d_lo = s.sb("d_hi", [P, 2, D], F32R), s.sb("d_lo", [P, 2, D], F32R)
        g_hi, g_lo = s.sb("g_hi", [P, 2, NT * P], F32R), s.sb("g_lo", [P, 2, NT * P], F32R)
        sg = s.sb("sg", [P, 2, BANK])
        pg = s.ps("pg", [P, 2, 2, BANK])
        pd = s.ps("pd", [P, 2, 2 * BANK])
        raw_loaded = [s.sem(f"raw_loaded{b}") for b in range(3)]
        names = "w_hi_done w_lo_done gu_bank silu_done prod_done g_hi_done g_lo_done d_tile acc_done zeroed"
        S = {n: s.sem(n) for n in names.split()}
        CREDIT, D_CREDIT = 2, 1
        block = ctx.enter_context(nc.Block())

        def gate_up(name, f):
            return t[name][l].rearrange("(k p) (f n) -> f p k n", p=P, n=P)[f]

        def down(f):
            return t["w_down"][l].rearrange("(f p) n -> f p n", p=P)[f]

        def count(i, p):
            return 6 * i + p + 4

        @block.sync
        def _(sp):
            def load(q, slot, src, wait):
                if wait is not None:
                    sp.wait_ge(S["w_lo_done"], wait)
                dst = rawp[slot][:]
                if len(src.shape) == 3:
                    dst = dst.rearrange("p (k n) -> p k n", k=KT)
                sp.dma_start(dst, src).then_inc(raw_loaded[slot], 16)

            def turn(i, last):
                for p in range(2 if last else 6):
                    src = down(2 * i + p) if p < 2 else gate_up(("w_gate", "w_up")[p % 2], 2 * (i + 1) + (p - 2) // 2)
                    load(None, (4 + p) % 3, src, 6 * i + p + 2)

            for p in range(4):
                load(None, p % 3, gate_up(("w_gate", "w_up")[p % 2], p // 2), p - 2 if p >= 3 else None)
            with sp.Fori(0, PAIRS - 1) as i:
                turn(i, False)
            turn(PAIRS - 1, True)

        @block.gpsimd
        def _(pool):
            for j in range(NT):
                ins = pool.memset(acc[:, j, :], 0.0)
            ins.then_inc(S["zeroed"], 1)

        def split(eng, p, i, hi_side):
            if p < 2:
                hi, lo = d_hi[:, p, :], d_lo[:, p, :]
            else:
                hi, lo = w_hi[:, (p - 2) // 2, p % 2, :], w_lo[:, (p - 2) // 2, p % 2, :]
            if i is None:
                q = p - 2
                slot, uses, done = q % 3, q // 3 + 1, q + 1
            else:
                slot, uses, done = (4 + p) % 3, 2 * i + (4 + p) // 3 + 1, count(i, p) + 1
                if p < 2:
                    eng.wait_ge(S["d_tile"], NT * i + D_CREDIT)
                else:
                    eng.wait_ge(S["gu_bank"], NC * (2 * i + (p - 2) // 2 + 1))
            if hi_side:
                eng.wait_ge(raw_loaded[slot], 16 * uses)
                eng.copy(hi, rawp[slot][:]).then_inc(S["w_hi_done"], 1)
            else:
                eng.wait_ge(S["w_hi_done"], done)
                eng.wait_ge(raw_loaded[slot], 16 * uses)
                eng.tensor_tensor(lo, rawp[slot][:], raw(hi), ALU.subtract).then_inc(S["w_lo_done"], 1)

        @block.scalar
        def _(act):
            def turn(i, last):
                for f in range(2):
                    for c, (a, b) in enumerate(CH):
                        e = 2 * NC * i + f * NC + c
                        z = (f * NC + c) % 2
                        act.wait_ge(S["gu_bank"], e + 1)
                        act.wait_ge(S["g_lo_done"], e + 1)
                        act.activation(sg[:, z, 0:b - a], pg[:, z, 0, 0:b - a], ACT.Silu).then_inc(S["silu_done"], 1)
                        if c < 2 and not (last and f == 1):
                            split(act, 2 * f + c, i, True)
                        act.wait_ge(S["prod_done"], e + 1 + CREDIT)
                        act.wait_ge(S["d_tile"], NT * i + D_CREDIT)
                        act.copy(g_hi[:, f, a:b], sg[:, z, 0:b - a]).then_inc(S["g_hi_done"], 1)
                if not last:
                    split(act, 4, i, True)
                    split(act, 5, i, True)

            for p in range(2, 6):
                split(act, p, None, True)
            with act.Fori(0, PAIRS - 1) as i:
                turn(i, False)
            turn(PAIRS - 1, True)

        @block.tensor
        def _(pe):
            def turn(i):
                for f in range(2):
                    pe.wait_ge(S["w_lo_done"], 6 * i + 2 * f + 2)
                    for c, (a, b) in enumerate(CH):
                        z = (f * NC + c) % 2
                        pe.wait_ge(S["prod_done"], 2 * NC * i + f * NC + c + 1)
                        for x in range(2):
                            for k in range(KT):
                                kk = slice(k * P, (k + 1) * P)
                                mm = three_pass(pe, pg[:, z, x, 0:b - a], w_hi[:, f, x, kk], w_lo[:, f, x, kk],
                                                h_hi[:, k, a:b], h_lo[:, k, a:b], k == 0, k == KT - 1)
                        mm.then_inc(S["gu_bank"], 1)
                pe.wait_ge(S["w_lo_done"], 6 * i + 6)
                for j in range(NT):
                    if j % 4 == 0:
                        pe.wait_ge(S["g_lo_done"], 2 * NC * i + NC + j // 4 + 1 + CREDIT)
                    pe.wait_ge(S["acc_done"], NT * i + j + 1)
                    tok = slice(j * P, (j + 1) * P)
                    for n in range(2):
                        c = slice(n * BANK, (n + 1) * BANK)
                        for f in range(2):
                            mm = three_pass(pe, pd[:, j % 2, c], g_hi[:, f, tok], g_lo[:, f, tok],
                                            d_hi[:, f, c], d_lo[:, f, c], f == 0, f == 1)
                    mm.then_inc(S["d_tile"], 1)

            pe.nop().then_inc(S["d_tile"], D_CREDIT)
            with pe.Fori(0, PAIRS) as i:
                turn(i)

        @block.vector
        def _(dve):
            def turn(i, last):
                for f in range(2):
                    for c, (a, b) in enumerate(CH):
                        e = 2 * NC * i + f * NC + c
                        z = (f * NC + c) % 2
                        dve.wait_ge(S["silu_done"], e + 1)
                        dve.tensor_tensor(sg[:, z, 0:b - a], sg[:, z, 0:b - a], pg[:, z, 1, 0:b - a], ALU.mult
                                          ).then_inc(S["prod_done"], 1)
                        if c < 2 and not (last and f == 1):
                            split(dve, 2 * f + c, i, False)
                        dve.wait_ge(S["g_hi_done"], e + 1)
                        dve.wait_ge(S["prod_done"], e + 1 + CREDIT)
                        dve.wait_ge(S["d_tile"], NT * i + D_CREDIT)
                        dve.tensor_tensor(g_lo[:, f, a:b], sg[:, z, 0:b - a], raw(g_hi[:, f, a:b]), ALU.subtract
                                          ).then_inc(S["g_lo_done"], 1)
                for j in range(NT):
                    if not last and j in (1, 3):
                        split(dve, 4 + j // 2, i, False)
                    dve.wait_ge(S["d_tile"], NT * i + j + 1 + D_CREDIT)
                    dve.tensor_tensor(acc[:, j, :], acc[:, j, :], pd[:, j % 2, :], ALU.add).then_inc(S["acc_done"], 1)

            for name in ("prod_done", "g_lo_done", "acc_done"):
                dve.nop().then_inc(S[name], CREDIT)
            dve.wait_ge(S["zeroed"], 1)
            for p in range(2, 6):
                split(dve, p, None, False)
            with dve.Fori(0, PAIRS - 1) as i:
                turn(i, False)
            turn(PAIRS - 1, True)


def ffn_out(nc, t, dr, keep, l, acc, out):
    NT = TT if l < DEPTH - 1 else TX
    with ExitStack() as ctx:
        s = Scope(nc, ctx, f"fo{l}")
        x = s.sb("x", [P, 3, D])
        gate = s.sb("gate", [P, 2, D])
        junk = s.sb("junk", [P, 2, D], BF16)
        ss, ms, rs = s.sb("ss", [P, NT]), s.sb("ms", [P, NT]), s.sb("rs", [P, NT])
        loaded = [s.sem(f"loaded{b}") for b in range(3)]
        stored = [s.sem(f"stored{b}") for b in range(3)]
        S = {n: s.sem(n) for n in ("gate_loaded", "squared", "rms", "pool_own", "gated", "x_done")}
        block = ctx.enter_context(nc.Block())

        @block.sync
        def _(sp):
            for c in range(2):
                sp.dma_start(gate[:, c, :], dr["gate"][l, 1, c].partition_broadcast(P)).then_inc(S["gate_loaded"], 16)
            def store(i):
                sp.wait_ge(S["x_done"], i + 1)
                dst = out[0, i * P:(i + 1) * P, :] if l == DEPTH - 1 else dr["x"][i * P:(i + 1) * P, :]
                sp.dma_start(dst, x[:, i % 3, :]).then_inc(stored[i % 3], 16)

            for i in range(NT):
                b = i % 3
                if i >= 3:
                    store(i - 3)
                    sp.wait_ge(stored[b], 16 * (i // 3))
                sp.dma_start(x[:, b, :], dr["x1"][i * P:(i + 1) * P, :]).then_inc(loaded[b], 16)
            for i in range(NT - 3, NT):
                store(i)
            for b in range(3):
                sp.wait_ge(stored[b], 16 * ((NT + 2 - b) // 3))

        @block.scalar
        def _(act):
            for i in range(NT):
                if i >= 2:
                    act.wait_ge(S["squared"], i - 1)
                act.activation(junk[:, i % 2, :], acc[:, i, :], ACT.Square, accum_out=ss[:, i:i + 1]).then_inc(S["squared"], 1)

        @block.gpsimd
        def _(pool):
            for i in range(NT):
                pool.wait_ge(S["squared"], i + 1)
                pool.tensor_scalar(ms[:, i:i + 1], ss[:, i:i + 1], 1.0 / D, EPS, ALU.mult, ALU.add
                                   ).then_inc(S["pool_own"], 1)
                pool.wait_ge(S["pool_own"], i + 1)
                pool.tensor_tensor(rs[:, i:i + 1], ms[:, i:i + 1], keep["mhalf"][:, 0:1], ALU.pow
                                   ).then_inc(S["rms"], 1)

        @block.vector
        def _(dve):
            dve.wait_ge(S["gate_loaded"], 32)
            for i in range(NT):
                dve.wait_ge(S["rms"], i + 1)
                dve.wait_ge(S["squared"], i + 1)
                dve.scalar_tensor_tensor(out=acc[:, i, :], in0=acc[:, i, :], scalar=rs[:, i:i + 1],
                                         in1=gate[:, 0 if i < TX else 1, :], op0=ALU.mult, op1=ALU.mult
                                         ).then_inc(S["gated"], 1)
                dve.wait_ge(S["gated"], i + 1)
                dve.wait_ge(loaded[i % 3], 16 * (i // 3 + 1))
                dve.tensor_tensor(x[:, i % 3, :], x[:, i % 3, :], acc[:, i, :], ALU.add).then_inc(S["x_done"], 1)


def trunk(nc, t, out):
    dr = {
        "T": nc.dram_tensor("rows_T", (2, R_ALL, TOK), F32, kind="Internal").ap(),
        "V": nc.dram_tensor("values", (2, TOK, VW), F32, kind="Internal").ap(),
        "mix": nc.dram_tensor("mix_T", (2, D, TOK), F32, kind="Internal").ap(),
        "x": nc.dram_tensor("residual", (TOK, D), F32, kind="Internal").ap(),
        "x1": nc.dram_tensor("residual_mid", (TOK, D), F32, kind="Internal").ap(),
        "gate": nc.dram_tensor("gates", (DEPTH, 2, 2, D), F32, kind="Internal").ap(),
        "ones": nc.dram_tensor("ones_row", (1, TOK), F32, kind="Internal").ap(),
    }
    with ExitStack() as ctx:
        s = Scope(nc, ctx, "keep")
        keep = {
            "vecs_loaded": s.sem("vecs_loaded"),
            "ident": s.sb("ident", [P, P]), "identb": s.sb("identb", [P, P], BF16),
            "above": s.sb("above", [P, P], BF16), "below": s.sb("below", [P, P], BF16),
            "eps": s.sb("eps", [P, 1]), "mhalf": s.sb("mhalf", [P, 4]),
            "modT": s.sb("modT", [P, DEPTH, 4, KT, 2]), "cnorm": s.sb("cnorm", [P, DEPTH, 3]),
            "neglam": s.sb("neglam", [P, DEPTH]), "dsn": s.sb("dsn", [64, DEPTH]),
            "sink": s.sb("sink", [P, DEPTH, 6]), "sinkdiv": s.sb("sinkdiv", [P, DEPTH, 6]),
        }
        modulation(nc, t, dr, keep)
        for l in range(DEPTH):
            project(nc, t, dr, keep, l)
            attend(nc, t, dr, keep, l)
            NT = TT if l < DEPTH - 1 else TX
            with ExitStack() as ffn_ctx:
                f = Scope(nc, ffn_ctx, f"h{l}")
                h_hi, h_lo = f.sb("hi", [P, KT, NT * P], F32R), f.sb("lo", [P, KT, NT * P], F32R)
                mix_out(nc, t, dr, keep, l, h_hi, h_lo)
                acc = f.sb("acc", [P, NT, D])
                ffn(nc, t, dr, keep, l, h_hi, h_lo, acc)
                ffn_out(nc, t, dr, keep, l, acc, out)


_INS = ["x", "c", "ctx", "c_ctx", "w_ada", "b_ada", "g_pre_mix", "g_post_mix", "w_in", "win_sink",
        "diff_lambda_q1", "diff_lambda_k1", "diff_lambda_q2", "diff_lambda_k2", "diff_sub_norm",
        "mla_q_norm", "mla_w_q_up", "mla_kv_norm", "mla_w_kv_up", "w_out",
        "g_pre_ffn", "g_post_ffn", "w_gate", "w_up", "w_down"]


def rotary_table(dim):
    half = dim // 2
    pos = np.arange(SEQ)
    freqs = (np.float32(10000.0) ** (-np.arange(0, half, 2, dtype=np.float32) / np.float32(half))).astype(np.float32)
    table = np.zeros((2, SEQ, dim), np.float32)
    for a, p in enumerate((pos // GRID_W, pos % GRID_W)):
        ang = p.astype(np.float32)[:, None] * freqs[None, :]
        cos, sin = np.cos(ang), np.sin(ang)
        o = a * half
        table[0, :, o:o + half] = np.concatenate([cos, cos], 1)
        table[1, :, o:o + half] = np.concatenate([-sin, sin], 1)
    return np.ascontiguousarray(table.reshape(2, TX, P, dim).transpose(2, 0, 1, 3))


def kernel(**inputs):
    import concourse.bacc as bacc
    from concourse.bass_utils import run_bass_kernel_spmd

    nc = bacc.Bacc("TRN2", target_bir_lowering=False, num_devices=1)
    arrays, t = {}, {}
    given = {name: np.ascontiguousarray(inputs[name]) for name in _INS}
    given["rot64"], given["rot32"] = rotary_table(64), rotary_table(32)
    for name, a in given.items():
        arrays[f"in_{name}"] = a
        t[name] = nc.dram_tensor(f"in_{name}", a.shape, mybir.dt.from_np(a.dtype), kind="ExternalInput").ap()
    out = nc.dram_tensor("out_x", (1, SEQ, D), F32, kind="ExternalOutput").ap()
    trunk(nc, t, out)
    r = run_bass_kernel_spmd(nc, [arrays], core_ids=[0])
    return r.results[0]["out_x"]
```

```python
from contextlib import ExitStack
import math

import numpy as np
import concourse.bass as bass
from concourse import mybir
from concourse.alu_op_type import AluOpType as ALU

F32 = mybir.dt.float32
F32R = mybir.dt.float32r
BF16 = mybir.dt.bfloat16
ACT = mybir.ActivationFunctionType
AX_X = mybir.AxisListType.X

P = 128
BANK = 512
D = 1024
KT = D // P
SEQ, CTX = 1024, 256
TX, TC = SEQ // P, CTX // P
TT = TX + TC
TOK = SEQ + CTX
DEPTH = 2
GRID_W = 64
EPS = 1e-6
NEG = -1e30
D_IN = 1824
QR, KVR = 256, 128
QUP, KVUP = 576, 768
VW = 768
DFF = 2816
FT = DFF // P
A_SCALE, B_SCALE, C_SCALE = 64 ** -0.5, 32 ** -0.5, 96 ** -0.5

IN_AQ, IN_AV, IN_BQ, IN_BV, IN_CQ, IN_CKV, IN_KR = 0, 512, 640, 1152, 1408, 1664, 1792
IN_BANKS = (0, 512, 1024, 1408, D_IN)
PJ_CQ, PJ_CKV, PJ_KR, PJ_END = (3 * BANK + c - IN_CQ for c in (IN_CQ, IN_CKV, IN_KR, D_IN))
R_AQ, R_AK, R_BQ, R_BK, R_CQ, R_CN, R_KR, R_ALL = 0, 384, 512, 768, 1024, 1600, 1984, 2048
V_A, V_B, V_C = 0, 128, 384


def lam_init(l):
    return 0.8 - 0.6 * math.exp(-0.3 * l)


def raw(ap):
    return ap.bitcast(F32)


def heads_of(ap, heads):
    return ap.rearrange("p (h e) -> p h e", h=heads)


class Scope:

    def __init__(self, nc, ctx, tag):
        self.nc, self.ctx, self.tag = nc, ctx, tag
        self.sems = []
        ctx.callback(self.close)

    def close(self):
        if self.sems:
            self.nc.clear_and_free_semaphores(self.sems)
            self.nc.all_engine_barrier()

    def sb(self, name, shape, dt=F32):
        return self.ctx.enter_context(self.nc.sbuf_tensor(f"{self.tag}_{name}", shape, dt))

    def ps(self, name, shape, dt=F32):
        return self.ctx.enter_context(self.nc.psum_tensor(f"{self.tag}_{name}", shape, dt))

    def sem(self, name):
        self.sems.append(self.nc.alloc_semaphore(f"{self.tag}_{name}"))
        return self.sems[-1]


def three_pass(pe, out, w_hi, w_lo, m_hi, m_lo, first, last):
    pe.matmul(out, w_hi, m_hi, start=first, stop=False)
    pe.matmul(out, w_hi, m_lo, start=False, stop=False)
    return pe.matmul(out, w_lo, m_hi, start=False, stop=last)


def modulation(nc, t, dr, keep):
    NCH = 6 * D // BANK
    RING = 3
    LO = 32
    with ExitStack() as ctx:
        s = Scope(nc, ctx, "mod")
        cT = s.sb("cT", [P, 2, KT])
        sT = s.sb("sT", [P, 2, KT])
        s_parts = s.sb("s_parts", [P, KT, LO + 2], F32R)
        w_hi, w_lo = s.sb("w_hi", [P, 2, KT, BANK], F32R), s.sb("w_lo", [P, 2, KT, BANK], F32R)
        bias = s.sb("bias", [1, RING, BANK])
        on_hi = s.sb("on_hi", [1, LO + 2])
        lo_rows = s.sb("lo_rows", [2, 2, BANK])
        rows = s.sb("rows", [2, DEPTH, 6 * D])
        gpost = s.sb("gpost", [2, DEPTH, 2, D])
        gpreT = s.sb("gpreT", [P, DEPTH, 2, KT])
        wring = s.sb("wring", [P, RING, KT, BANK])
        lamv = s.sb("lamv", [P, 4, DEPTH, 32])
        lamj = s.sb("lamj", [P, 2, DEPTH, 32])
        lamd = s.sb("lamd", [P, 2, DEPTH])
        lame = s.sb("lame", [P, 2, DEPTH])
        dsnr = s.sb("dsnr", [64, DEPTH])
        pm = s.ps("pm", [P, 2, BANK])
        pT = s.ps("pT", [P, BANK])
        cols_loaded, vecs_loaded = s.sem("cols_loaded"), keep["vecs_loaded"]
        w_loaded = [s.sem(f"w_loaded{i}") for i in range(RING)]
        silu_done, consts_done, chunk_summed, row_done = (
            s.sem("silu_done"), s.sem("consts_done"), s.sem("chunk_summed"), s.sem("row_done"))
        turned, lam_dots, lam_exp, own, stored = (
            s.sem("turned"), s.sem("lam_dots"), s.sem("lam_exp"), s.sem("own"), s.sem("stored"))
        ones = s.sb("ones", [1, TOK], F32R)
        ones_done = s.sem("ones_done")
        s_hi_done, s_lo_done, w_hi_done, w_lo_done, lo_copied = (
            s.sem("s_hi_done"), s.sem("s_lo_done"), s.sem("w_hi_done"), s.sem("w_lo_done"), s.sem("lo_copied"))
        block = ctx.enter_context(nc.Block())
        NVEC = 12

        @block.sync
        def _(sp):
            sp.dma_start(cT[:, 0, :], t["c"].rearrange("o (k p) -> p (o k)", p=P),
                         allow_slow_non_contiguous=True).then_inc(cols_loaded, 16)
            sp.dma_start(cT[:, 1, :], t["c_ctx"].rearrange("(k p) -> p k", p=P),
                         allow_slow_non_contiguous=True).then_inc(cols_loaded, 16)
            for i in range(DEPTH * NCH):
                l, n = divmod(i, NCH)
                if i >= RING:
                    sp.wait_ge(w_lo_done, i - RING + 1)
                sp.dma_start(wring[:, i % RING, :, :],
                             t["w_ada"][l, :, n * BANK:(n + 1) * BANK].rearrange("(k p) n -> p k n", p=P)
                             ).then_inc(w_loaded[i % RING], 16)
                if i >= RING:
                    sp.wait_ge(chunk_summed, i - RING + 1)
                sp.dma_start(bias[:, i % RING, :], t["b_ada"][l:l + 1, n * BANK:(n + 1) * BANK]
                             ).then_inc(w_loaded[i % RING], 16)
            sp.wait_ge(own, 2 * DEPTH + 4)
            for l in range(DEPTH):
                for j in range(2):
                    sp.dma_start(dr["gate"][l, j], gpost[:, l, j, :]).then_inc(stored, 16)
            sp.wait_ge(ones_done, 4)
            sp.dma_start(dr["ones"], raw(ones[:])).then_inc(stored, 16)
            sp.wait_ge(stored, 16 * (2 * DEPTH + 1))

        @block.gpsimd
        def _(pool):
            pool.memset(raw(s_parts[:]), 0.0).then_inc(ones_done, 1)
            pool.memset(on_hi[:], 0.0).then_inc(ones_done, 1)
            pool.wait_ge(ones_done, 2)
            pool.memset(on_hi[:, 0:2], 1.0).then_inc(ones_done, 1)
            pool.memset(raw(ones[:]), 1.0).then_inc(ones_done, 1)
            pool.memset(keep["ident"][:], 0.0).then_inc(consts_done, 1)
            pool.memset(keep["identb"][:], 0.0).then_inc(consts_done, 1)
            pool.memset(keep["above"][:], 0.0).then_inc(consts_done, 1)
            pool.memset(keep["below"][:], 0.0).then_inc(consts_done, 1)
            pool.wait_ge(consts_done, 4)
            for m in (keep["ident"], keep["identb"]):
                pool.affine_select(out=m[:], in_=m[:], compare_op=ALU.not_equal, fill=1.0, base=0,
                                   pattern=[[-1, P]], channel_multiplier=1).then_inc(consts_done, 1)
            pool.affine_select(out=keep["above"][:], in_=keep["above"][:], compare_op=ALU.is_ge, fill=NEG, base=0,
                               pattern=[[-1, P]], channel_multiplier=1).then_inc(consts_done, 1)
            pool.affine_select(out=keep["below"][:], in_=keep["below"][:], compare_op=ALU.is_ge, fill=NEG, base=0,
                               pattern=[[1, P]], channel_multiplier=-1).then_inc(consts_done, 1)
            pool.memset(keep["eps"][:], EPS).then_inc(consts_done, 1)
            pool.memset(keep["mhalf"][:], -0.5).then_inc(consts_done, 1)
            for j, name in enumerate(("g_post_mix", "g_post_ffn")):
                pool.dma_start(gpost[:, :, j, :], t[name].partition_broadcast(2)).then_inc(vecs_loaded, 16)
            for j, name in enumerate(("g_pre_mix", "g_pre_ffn")):
                for l in range(DEPTH):
                    pool.dma_start(gpreT[:, l, j, :], t[name][l].rearrange("(k p) -> p k", p=P),
                                   allow_slow_non_contiguous=True
                                   ).then_inc(vecs_loaded, 16)
            for j, name in enumerate(("diff_lambda_q1", "diff_lambda_k1", "diff_lambda_q2", "diff_lambda_k2")):
                pool.dma_start(lamv[:, j, :, :], t[name].partition_broadcast(P)).then_inc(vecs_loaded, 16)
            pool.dma_start(keep["sink"][:], t["win_sink"].partition_broadcast(P)).then_inc(vecs_loaded, 16)
            pool.dma_start(dsnr[:], t["diff_sub_norm"].rearrange("l v -> v l"),
                           allow_slow_non_contiguous=True).then_inc(vecs_loaded, 16)
            for l in range(DEPTH):
                pool.dma_start(keep["cnorm"][:, l, 0:2], t["mla_q_norm"][l].rearrange("(k p) -> p k", p=P),
                               allow_slow_non_contiguous=True
                               ).then_inc(vecs_loaded, 16)
                pool.dma_start(keep["cnorm"][:, l, 2:3], t["mla_kv_norm"][l].rearrange("(k p) -> p k", p=P),
                               allow_slow_non_contiguous=True
                               ).then_inc(vecs_loaded, 16)
            pool.wait_ge(vecs_loaded, 16 * (NVEC + 4))

        @block.scalar
        def _(act):
            act.wait_ge(cols_loaded, 32)
            act.activation(sT[:], cT[:], ACT.Silu).then_inc(silu_done, 1)
            act.wait_ge(silu_done, 1)
            act.wait_ge(ones_done, 1)
            act.copy(s_parts[:, :, 0:2], sT[:].rearrange("p c k -> p k c")).then_inc(s_hi_done, 1)
            for i in range(DEPTH * NCH + 1):
                if i < DEPTH * NCH:
                    act.wait_ge(w_loaded[i % RING], 32 * (i // RING + 1))
                    if i >= 2:
                        act.wait_ge(chunk_summed, i - 1)
                    act.copy(w_hi[:, i % 2], wring[:, i % RING]).then_inc(w_hi_done, 1)
                if i >= 1:
                    act.wait_ge(chunk_summed, i)
                    if i >= 3:
                        act.wait_ge(row_done, i - 2)
                    act.copy(lo_rows[:, (i - 1) % 2, :], pm[LO:LO + 2, (i - 1) % 2, :]).then_inc(lo_copied, 1)
            act.wait_ge(lam_dots, 2 * DEPTH)
            act.activation(lame[:], lamd[:], ACT.Exp).then_inc(lam_exp, 1)

        @block.tensor
        def _(pe):
            pe.wait_ge(s_hi_done, 1)
            pe.wait_ge(s_lo_done, 1)
            pe.wait_ge(ones_done, 3)
            for i in range(DEPTH * NCH):
                pe.wait_ge(w_loaded[i % RING], 32 * (i // RING + 1))
                pe.wait_ge(w_hi_done, i + 1)
                if i >= 2:
                    pe.wait_ge(row_done, i - 1)
                out = pm[0:LO + 2, i % 2, :]
                pe.matmul(out, on_hi[:], bias[:, i % RING, :], start=True, stop=False)
                for k in range(KT):
                    pe.matmul(out, s_parts[:, k, :], w_hi[:, i % 2, k, :], start=False, stop=False)
                pe.wait_ge(w_lo_done, i + 1)
                for k in range(KT):
                    mm = pe.matmul(out, s_parts[:, k, :], w_lo[:, i % 2, k, :], start=False, stop=(k == KT - 1))
                mm.then_inc(chunk_summed, 1)
            pe.wait_ge(row_done, DEPTH * NCH)
            pe.wait_ge(consts_done, 10)
            for l in range(DEPTH):
                for j, part in enumerate((0, 1, 3, 4)):
                    for k in range(KT):
                        at = ((l * 4 + j) * KT + k) * 2
                        mm = pe.transpose(pT[:, at:at + 2], rows[:, l, part * D + k * P:part * D + (k + 1) * P],
                                          keep["ident"][0:2, 0:2])
            mm.then_inc(turned, 1)

        @block.vector
        def _(dve):
            dve.wait_ge(s_hi_done, 1)
            dve.wait_ge(silu_done, 1)
            dve.tensor_tensor(s_parts[:, :, LO:LO + 2], sT[:].rearrange("p c k -> p k c"), raw(s_parts[:, :, 0:2]),
                              ALU.subtract).then_inc(s_lo_done, 1)
            dve.wait_ge(vecs_loaded, 16 * (NVEC + 4))
            for l in range(DEPTH):
                for j in range(2):
                    dve.tensor_tensor_reduce(lamj[:, j, l, :], lamv[:, 2 * j, l, :], lamv[:, 2 * j + 1, l, :],
                                             1.0, 0.0, ALU.mult, ALU.add, lamd[:, j, l:l + 1]).then_inc(lam_dots, 1)
            for i in range(DEPTH * NCH + 1):
                if i < DEPTH * NCH:
                    dve.wait_ge(w_hi_done, i + 1)
                    dve.wait_ge(w_loaded[i % RING], 32 * (i // RING + 1))
                    if i >= 2:
                        dve.wait_ge(chunk_summed, i - 1)
                    dve.tensor_tensor(w_lo[:, i % 2], wring[:, i % RING], raw(w_hi[:, i % 2]), ALU.subtract
                                      ).then_inc(w_lo_done, 1)
                if i >= 1:
                    l, n = divmod(i - 1, NCH)
                    dve.wait_ge(lo_copied, i)
                    dve.tensor_tensor(rows[:, l, n * BANK:(n + 1) * BANK], pm[0:2, (i - 1) % 2, :],
                                      lo_rows[:, (i - 1) % 2, :], ALU.add).then_inc(row_done, 1)
            dve.wait_ge(row_done, DEPTH * NCH)
            for l in range(DEPTH):
                for j, part in enumerate((2, 5)):
                    dve.tensor_tensor(gpost[:, l, j, :], rows[:, l, part * D:(part + 1) * D], gpost[:, l, j, :],
                                      ALU.mult).then_inc(own, 1)
            dve.wait_ge(lam_exp, 1)
            for l in range(DEPTH):
                dve.scalar_tensor_tensor(out=keep["neglam"][:, l:l + 1], in0=lame[:, 1, l:l + 1], scalar=-lam_init(l),
                                         in1=lame[:, 0, l:l + 1], op0=ALU.add, op1=ALU.subtract).then_inc(own, 1)
                dve.tensor_scalar(keep["dsn"][:, l:l + 1], dsnr[:, l:l + 1], 1.0 - lam_init(l), None,
                                  ALU.mult).then_inc(own, 1)
            dve.tensor_scalar(keep["sinkdiv"][:], keep["sink"][:], 1.0 / A_SCALE, None, ALU.mult)
            dve.wait_ge(turned, 1)
            view = pT[:, 0:DEPTH * 4 * KT * 2].rearrange("p (l j k c) -> p l j k c", l=DEPTH, j=4, k=KT)
            for l in range(DEPTH):
                for j in range(2):
                    dve.tensor_copy(keep["modT"][:, l, 2 * j], view[:, l, 2 * j])
                    dve.scalar_tensor_tensor(out=keep["modT"][:, l, 2 * j + 1], in0=view[:, l, 2 * j + 1], scalar=1.0,
                                             in1=gpreT[:, l, j, :].unsqueeze(2).to_broadcast([P, KT, 2]),
                                             op0=ALU.add, op1=ALU.mult)


def split_hi(act, i, ring_slot, loaded, hi, hi_done):
    act.wait_ge(loaded[i % len(loaded)], 16 * (i // len(loaded) + 1))
    act.copy(hi, ring_slot).then_inc(hi_done, 1)


def split_lo(dve, i, ring_slot, loaded, hi, lo, hi_done, lo_done):
    dve.wait_ge(hi_done, i + 1)
    dve.wait_ge(loaded[i % len(loaded)], 16 * (i // len(loaded) + 1))
    dve.tensor_tensor(lo, ring_slot, raw(hi), ALU.subtract).then_inc(lo_done, 1)


def project(nc, t, dr, keep, l):
    with ExitStack() as outer:
        w = Scope(nc, outer, f"pw{l}")
        win_hi, win_lo = w.sb("win_hi", [P, KT, D_IN], F32R), w.sb("win_lo", [P, KT, D_IN], F32R)
        wq_hi, wq_lo = w.sb("wq_hi", [P, 2, QUP], F32R), w.sb("wq_lo", [P, 2, QUP], F32R)
        wkv_hi, wkv_lo = w.sb("wkv_hi", [P, KVUP], F32R), w.sb("wkv_lo", [P, KVUP], F32R)
        pieces = [(t["w_in"][l, k * P:(k + 1) * P, :], win_hi[:, k, :], win_lo[:, k, :]) for k in range(KT)]
        pieces += [(t["mla_w_q_up"][l].rearrange("(k p) n -> p k n", p=P), wq_hi[:], wq_lo[:]),
                   (t["mla_w_kv_up"][l], wkv_hi[:], wkv_lo[:])]
        with ExitStack() as ctx:
            s = Scope(nc, ctx, f"pj{l}")
            xt = s.sb("xt", [P, 3, D])
            junk = s.sb("junk", [P, D], BF16)
            junk_c = s.sb("junk_c", [P, 384], BF16)
            hT_hi, hT_lo = s.sb("hT_hi", [P, 2, KT, P], F32R), s.sb("hT_lo", [P, 2, KT, P], F32R)
            R = s.sb("R", [P, R_ALL])
            T_hi, T_lo = s.sb("T_hi", [P, 16, P], F32R), s.sb("T_lo", [P, 16, P], F32R)
            V_hi, V_lo = s.sb("V_hi", [P, VW], F32R), s.sb("V_lo", [P, VW], F32R)
            cn = s.sb("cn", [P, 384])
            cT_hi, cT_lo = s.sb("cT_hi", [P, 3, P], F32R), s.sb("cT_lo", [P, 3, P], F32R)
            rot64, rot32 = s.sb("rot64", [P, 2, TX, 64]), s.sb("rot32", [P, 2, TX, 32])
            turn = s.sb("turn", [P, 512])
            ss, ms, rs = s.sb("ss", [P, 2, 4]), s.sb("ms", [P, 2, 4]), s.sb("rs", [P, 2, 4])
            pj = s.ps("pj", [P, 4 * BANK])
            pt = s.ps("pt", [P, 2 * BANK])
            pu = s.ps("pu", [P, 2 * BANK])
            wring = [raw(T_hi[:].rearrange("p b n -> p (b n)")), raw(T_lo[:].rearrange("p b n -> p (b n)")), R[:]]
            w_loaded = [s.sem(f"w_loaded{b}") for b in range(3)]

            def in_ring(m):
                hi = pieces[m][1]
                if len(hi.shape) == 3:
                    return wring[m % 3][:, 0:hi.shape[1] * hi.shape[2]].rearrange("p (k n) -> p k n", k=hi.shape[1])
                return wring[m % 3][:, 0:hi.shape[1]]

            x_loaded = [s.sem(f"x_loaded{b}") for b in range(3)]
            names = ("rot_loaded x_squared x_rms x_normed h_turned h_full h_hi h_lo proj_done c_squared "
                     " c_rms c_normed c_turned c_full c_hi c_lo q_up kv_up q_read_dve "
                     "q_read_act kv_read_act r_turned t_hi t_lo v_hi v_lo pool_own dve_own t_stored0 t_stored1 v_stored "
                     "ropeA_done ropeB_done kr_done w_hi_done w_lo_done")
            S = {n: s.sem(n) for n in names.split()}
            block = ctx.enter_context(nc.Block())

            def src(i):
                if l == 0:
                    return t["x"][0, i * P:(i + 1) * P, :] if i < TX else t["ctx"][0, (i - TX) * P:(i - TX + 1) * P, :]
                return dr["x"][i * P:(i + 1) * P, :]

            def store(sp, i):
                store_turned(sp, i, 0)
                sp.wait_ge(S["v_hi"], 3 * (i + 1))
                sp.wait_ge(S["v_lo"], 3 * (i + 1))
                for j, v in enumerate((V_hi, V_lo)):
                    sp.dma_start(dr["V"][j, i * P:(i + 1) * P, :], raw(v[:])).then_inc(S["v_stored"], 16)
                store_turned(sp, i, 1)

            def store_turned(sp, i, half):
                sp.wait_ge(S["t_hi"], 4 * i + 2 * half + 2)
                sp.wait_ge(S["t_lo"], 4 * i + 2 * half + 2)
                for j, v in enumerate((T_hi, T_lo)):
                    sp.dma_start(dr["T"][j, half * D:(half + 1) * D, i * P:(i + 1) * P
                                         ].rearrange("(b p) n -> p b n", p=P),
                                 raw(v[:, 8 * half:8 * half + 8])).then_inc(S[f"t_stored{half}"], 16)

            @block.sync
            def _(sp):
                sp.dma_start(xt[:, 0, :], src(0)).then_inc(x_loaded[0], 16)
                for m in range(len(pieces)):
                    if m >= 3:
                        sp.wait_ge(S["w_lo_done"], m - 2)
                    sp.dma_start(in_ring(m), pieces[m][0]).then_inc(w_loaded[m % 3], 16)
                    if m == 2:
                        sp.dma_start(rot64[:], t["rot64"]).then_inc(S["rot_loaded"], 16)
                        sp.dma_start(rot32[:], t["rot32"]).then_inc(S["rot_loaded"], 16)
                for i in (1, 2):
                    sp.dma_start(xt[:, i, :], src(i)).then_inc(x_loaded[i], 16)
                for i in range(TT):
                    if i + 3 < TT:
                        sp.wait_ge(S["h_lo"], i + 1)
                        sp.dma_start(xt[:, i % 3, :], src(i + 3)).then_inc(x_loaded[i % 3], 16)
                    store(sp, i)
                sp.wait_ge(S["t_stored0"], 32 * TT)
                sp.wait_ge(S["t_stored1"], 32 * TT)
                sp.wait_ge(S["v_stored"], 32 * TT)

            @block.gpsimd
            def _(pool):
                own = 0

                def rsqrt(cols, i, divs):
                    nonlocal own
                    b = i % 2
                    for c, n in zip(cols, divs):
                        pool.tensor_scalar(ms[:, b, c:c + 1], ss[:, b, c:c + 1], 1.0 / n, EPS, ALU.mult, ALU.add
                                           ).then_inc(S["pool_own"], 1)
                        own += 1
                    pool.wait_ge(S["pool_own"], own)
                    lo, hi = cols[0], cols[-1] + 1
                    return pool.tensor_tensor(rs[:, b, lo:hi], ms[:, b, lo:hi],
                                              keep["mhalf"][:, 0:hi - lo], ALU.pow)

                def x_rms(i):
                    pool.wait_ge(S["x_squared"], i + 1)
                    if i >= 2:
                        pool.wait_ge(S["x_normed"], i - 1)
                    rsqrt([0], i, [D]).then_inc(S["x_rms"], 1)

                x_rms(0)
                for i in range(TT):
                    if i + 1 < TT:
                        x_rms(i + 1)
                    pool.wait_ge(S["c_squared"], 2 * (i + 1))
                    if i >= 2:
                        pool.wait_ge(S["c_normed"], i - 1)
                    rsqrt([1, 2], i, [QR, KVR]).then_inc(S["c_rms"], 1)

            @block.scalar
            def _(act):
                def x_norm(i):
                    b = i % 2
                    act.wait_ge(x_loaded[i % 3], 16 * (i // 3 + 1))
                    if i >= 2:
                        act.wait_ge(S["x_rms"], i - 1)
                    act.activation(junk[:], xt[:, i % 3, :], ACT.Square, accum_out=ss[:, b, 0:1]
                                   ).then_inc(S["x_squared"], 1)
                    act.wait_ge(S["x_rms"], i + 1)
                    act.activation(xt[:, i % 3, :], xt[:, i % 3, :], ACT.Copy, scale=rs[:, b, 0:1]
                                   ).then_inc(S["x_normed"], 1)

                def h_split(i):
                    act.wait_ge(S["h_full"], i + 1)
                    if i >= 2:
                        act.wait_ge(S["proj_done"], 4 * (i - 1))
                    act.copy(hT_hi[:, i % 2].rearrange("p k n -> p (k n)"), xt[:, i % 3, :]).then_inc(S["h_hi"], 1)

                def r_split(i, g, bank):
                    act.wait_ge(S["r_turned"], 4 * i + g + 1)
                    if i == 0:
                        act.wait_ge(S["w_lo_done"], len(pieces))
                    if g % 2 == 0 and i >= 1:
                        act.wait_ge(S[f"t_stored{g // 2}"], 32 * i)
                    act.copy(T_hi[:, 4 * g:4 * g + 4].rearrange("p b n -> p (b n)"), bank).then_inc(S["t_hi"], 1)

                def latent(i):
                    act.wait_ge(S["c_full"], i + 1)
                    if i >= 1:
                        act.wait_ge(S["kv_up"], i)
                    act.copy(cT_hi[:].rearrange("p k n -> p (k n)"), cn[:]).then_inc(S["c_hi"], 1)
                    r_split(i, 0, pt[:, BANK:2 * BANK])
                    r_split(i, 1, pu[:, 0:BANK])
                    act.wait_ge(S["q_up"], i + 1)
                    if i >= 1:
                        act.wait_ge(S["r_turned"], 4 * i)
                    act.copy(heads_of(R[:, R_CQ:R_CN], 6)[:, :, 0:64], heads_of(pu[:, 0:QUP], 6)[:, :, 0:64]
                             ).then_inc(S["q_read_act"], 1)
                    act.wait_ge(S["kv_up"], i + 1)
                    kv = heads_of(pt[:, 0:KVUP], 6)
                    act.copy(heads_of(R[:, R_CN:R_KR], 6), kv[:, :, 0:64]).then_inc(S["kv_read_act"], 1)
                    act.copy(heads_of(V_hi[:, V_C:VW], 6), kv[:, :, 64:128]).then_inc(S["v_hi"], 1)

                def weights_hi(m):
                    split_hi(act, m, in_ring(m), w_loaded, pieces[m][1], S["w_hi_done"])

                x_norm(0)
                weights_hi(0)
                weights_hi(1)
                h_split(0)
                for m in range(2, len(pieces)):
                    weights_hi(m)
                for i in range(TT):
                    if i + 1 < TT:
                        x_norm(i + 1)
                    if i >= 1:
                        latent(i - 1)
                    if i + 1 < TT:
                        h_split(i + 1)
                    if i >= 1:
                        r_split(i - 1, 2, pu[:, 0:BANK])
                        r_split(i - 1, 3, pu[:, BANK:2 * BANK])
                    act.wait_ge(S["proj_done"], 4 * i + 2)
                    if i >= 1:
                        act.wait_ge(S["v_stored"], 32 * i)
                    act.copy(V_hi[:, V_A:V_B], pj[:, IN_AV:IN_BQ]).then_inc(S["v_hi"], 1)
                    act.wait_ge(S["proj_done"], 4 * i + 3)
                    act.copy(V_hi[:, V_B:V_C], pj[:, IN_BV:IN_CQ]).then_inc(S["v_hi"], 1)
                    act.wait_ge(S["proj_done"], 4 * i + 4)
                    if i >= 1:
                        act.wait_ge(S["c_rms"], i)
                    act.activation(junk_c[:, 0:QR], pj[:, PJ_CQ:PJ_CKV], ACT.Square, accum_out=ss[:, i % 2, 1:2]
                                   ).then_inc(S["c_squared"], 1)
                    act.activation(junk_c[:, QR:384], pj[:, PJ_CKV:PJ_KR], ACT.Square, accum_out=ss[:, i % 2, 2:3]
                                   ).then_inc(S["c_squared"], 1)
                latent(TT - 1)
                r_split(TT - 1, 2, pu[:, 0:BANK])
                r_split(TT - 1, 3, pu[:, BANK:2 * BANK])

            @block.tensor
            def _(pe):
                def h_turn(i):
                    pe.wait_ge(S["x_normed"], i + 1)
                    if i >= 1:
                        pe.wait_ge(S["h_full"], i)
                    if i >= 2:
                        pe.wait_ge(S["kv_read_act"], i - 1)
                        pe.wait_ge(S["v_hi"], 3 * (i - 1))
                        pe.wait_ge(S["v_lo"], 3 * (i - 1))
                    for k in range(KT):
                        mm = pe.transpose(pt[:, k * P:(k + 1) * P], xt[:, i % 3, k * P:(k + 1) * P], keep["ident"][:])
                    mm.then_inc(S["h_turned"], 1)

                def proj(i, n):
                    a, b = IN_BANKS[n], IN_BANKS[n + 1]
                    if n == 0:
                        pe.wait_ge(S["h_hi"], i + 1)
                        pe.wait_ge(S["h_lo"], i + 1)
                        if i >= 1:
                            pe.wait_ge(S["ropeA_done"], i)
                    if n == 1 and i >= 1:
                        pe.wait_ge(S["c_normed"], i)
                        pe.wait_ge(S["c_squared"], 2 * i)
                    for k in range(KT):
                        if i == 0 and n == 0:
                            pe.wait_ge(S["w_lo_done"], k + 1)
                        mm = three_pass(pe, pj[:, n * BANK:n * BANK + b - a], hT_hi[:, i % 2, k, :], hT_lo[:, i % 2, k, :],
                                        win_hi[:, k, a:b], win_lo[:, k, a:b], k == 0, k == KT - 1)
                    mm.then_inc(S["proj_done"], 1)

                def r_turn(i, g, bank):
                    for b in range(4):
                        c = (4 * g + b) * P
                        mm = pe.transpose(bank[:, b * P:(b + 1) * P], R[:, c:c + P], keep["ident"][:])
                    mm.then_inc(S["r_turned"], 1)

                def latent(i, step):
                    if step == 0:
                        pe.wait_ge(S["c_normed"], i + 1)
                        pe.wait_ge(S["h_full"], min(i + 2, TT))
                        for k in range(3):
                            mm = pe.transpose(pt[:, k * P:(k + 1) * P], cn[:, k * P:(k + 1) * P], keep["ident"][:])
                        mm.then_inc(S["c_turned"], 1)
                        r_turn(i, 0, pt[:, BANK:2 * BANK])
                        if i >= 1:
                            pe.wait_ge(S["t_hi"], 4 * i)
                            pe.wait_ge(S["t_lo"], 4 * i)
                        r_turn(i, 1, pu[:, 0:BANK])
                    elif step == 1:
                        pe.wait_ge(S["c_hi"], i + 1)
                        pe.wait_ge(S["c_lo"], i + 1)
                        if i == 0:
                            pe.wait_ge(S["w_lo_done"], len(pieces))
                        pe.wait_ge(S["t_hi"], 4 * i + 2)
                        pe.wait_ge(S["t_lo"], 4 * i + 2)
                        for a, b in ((0, BANK), (BANK, QUP)):
                            for k in range(2):
                                mm = three_pass(pe, pu[:, a:b], cT_hi[:, k, :], cT_lo[:, k, :],
                                                wq_hi[:, k, a:b], wq_lo[:, k, a:b], k == 0, k == 1)
                        mm.then_inc(S["q_up"], 1)
                        for a, b in ((0, BANK), (BANK, KVUP)):
                            mm = three_pass(pe, pt[:, a:b], cT_hi[:, 2, :], cT_lo[:, 2, :],
                                            wkv_hi[:, a:b], wkv_lo[:, a:b], True, True)
                        mm.then_inc(S["kv_up"], 1)
                    else:
                        pe.wait_ge(S["q_read_act"], i + 1)
                        pe.wait_ge(S["q_read_dve"], i + 1)
                        pe.wait_ge(S["kv_read_act"], i + 1)
                        r_turn(i, 2, pu[:, 0:BANK])
                        r_turn(i, 3, pu[:, BANK:2 * BANK])

                h_turn(0)
                for i in range(TT):
                    proj(i, 0)
                    if i >= 1:
                        latent(i - 1, 0)
                    proj(i, 1)
                    if i >= 1:
                        latent(i - 1, 1)
                    proj(i, 2)
                    if i + 1 < TT:
                        h_turn(i + 1)
                    if i >= 1:
                        latent(i - 1, 2)
                    proj(i, 3)
                for step in range(3):
                    latent(TT - 1, step)

            @block.vector
            def _(dve):
                linked = 0

                def link(ins):
                    nonlocal linked
                    linked += 1
                    ins.then_inc(S["dve_own"], 1)
                    dve.wait_ge(S["dve_own"], linked)

                def h_full(i):
                    dve.wait_ge(S["h_turned"], i + 1)
                    c = 0 if i < TX else 1
                    for k in range(KT):
                        ins = dve.tensor_scalar(xt[:, i % 3, k * P:(k + 1) * P], pt[:, k * P:(k + 1) * P],
                                                keep["modT"][:, l, 1, k, c:c + 1], keep["modT"][:, l, 0, k, c:c + 1],
                                                ALU.mult, ALU.add)
                    ins.then_inc(S["h_full"], 1)

                def h_lo(i):
                    dve.wait_ge(S["h_hi"], i + 1)
                    dve.wait_ge(S["h_full"], i + 1)
                    if i >= 2:
                        dve.wait_ge(S["proj_done"], 4 * (i - 1))
                    dve.tensor_tensor(hT_lo[:, i % 2].rearrange("p k n -> p (k n)"), xt[:, i % 3, :],
                                      raw(hT_hi[:, i % 2].rearrange("p k n -> p (k n)")), ALU.subtract
                                      ).then_inc(S["h_lo"], 1)

                turn_used = None

                def place(dst, src_ap, heads, dim, tables, i, done):
                    nonlocal turn_used
                    if i >= TX:
                        dve.tensor_copy(dst, src_ap).then_inc(done, 1)
                        return
                    if turn_used is not None:
                        dve.wait_ge(*turn_used)
                    turn_used = (done, i + 1)
                    q = dim // 4
                    cos = tables[:, 0, i, :].unsqueeze(1).to_broadcast([P, heads, dim])
                    sin = tables[:, 1, i, :].rearrange("p (a s j) -> p a s j", a=2, s=2)
                    tv = turn[:, 0:heads * dim].rearrange("p (h a s j) -> p h a s j", h=heads, a=2, s=2)
                    sv = src_ap.rearrange("p h (a s j) -> p h a s j", a=2, s=2)
                    for z in range(2):
                        dve.tensor_tensor(tv[:, :, :, z, :], sv[:, :, :, 1 - z, :],
                                          sin[:, :, z, :].unsqueeze(1).to_broadcast([P, heads, 2, q]), ALU.mult)
                    link(dve.tensor_tensor(dst, src_ap, cos, ALU.mult))
                    dve.tensor_tensor(dst, dst, turn[:, 0:heads * dim].rearrange("p (h e) -> p h e", h=heads),
                                      ALU.add).then_inc(done, 1)

                def values_lo(i, part, src_ap, dst, hi):
                    dve.wait_ge(S["v_hi"], 3 * i + part + 1)
                    if i >= 1 and part == 0:
                        dve.wait_ge(S["v_stored"], 32 * i)
                    dve.tensor_tensor(dst, src_ap, raw(hi), ALU.subtract).then_inc(S["v_lo"], 1)

                def r_lo(i, g, bank):
                    dve.wait_ge(S["t_hi"], 4 * i + g + 1)
                    if g % 2 == 0 and i >= 1:
                        dve.wait_ge(S[f"t_stored{g // 2}"], 32 * i)
                    dve.tensor_tensor(T_lo[:, 4 * g:4 * g + 4].rearrange("p b n -> p (b n)"), bank,
                                      raw(T_hi[:, 4 * g:4 * g + 4].rearrange("p b n -> p (b n)")), ALU.subtract
                                      ).then_inc(S["t_lo"], 1)

                def latent(i, step):
                    if step == 0:
                        dve.wait_ge(S["c_turned"], i + 1)
                        for k in range(3):
                            ins = dve.tensor_scalar(cn[:, k * P:(k + 1) * P], pt[:, k * P:(k + 1) * P],
                                                    keep["cnorm"][:, l, k:k + 1], None, ALU.mult)
                        ins.then_inc(S["c_full"], 1)
                        dve.wait_ge(S["c_full"], i + 1)
                        dve.wait_ge(S["c_hi"], i + 1)
                        if i >= 1:
                            dve.wait_ge(S["kv_up"], i)
                        dve.tensor_tensor(cT_lo[:].rearrange("p k n -> p (k n)"), cn[:],
                                          raw(cT_hi[:].rearrange("p k n -> p (k n)")), ALU.subtract
                                          ).then_inc(S["c_lo"], 1)
                        r_lo(i, 0, pt[:, BANK:2 * BANK])
                        r_lo(i, 1, pu[:, 0:BANK])
                    elif step == 1:
                        dve.wait_ge(S["q_read_act"], i + 1)
                        if i >= 1:
                            dve.wait_ge(S["r_turned"], 4 * i)
                        place(heads_of(R[:, R_CQ:R_CN], 6)[:, :, 64:96], heads_of(pu[:, 0:QUP], 6)[:, :, 64:96],
                              6, 32, rot32, i, S["q_read_dve"])
                        dve.wait_ge(S["kv_up"], i + 1)
                        values_lo(i, 2, heads_of(pt[:, 0:KVUP], 6)[:, :, 64:128],
                                  heads_of(V_lo[:, V_C:VW], 6), heads_of(V_hi[:, V_C:VW], 6))
                    else:
                        r_lo(i, 2, pu[:, 0:BANK])
                        r_lo(i, 3, pu[:, BANK:2 * BANK])

                def weights_lo(m):
                    split_lo(dve, m, in_ring(m), w_loaded, pieces[m][1], pieces[m][2], S["w_hi_done"], S["w_lo_done"])

                dve.memset(R[:, R_KR + 32:R_ALL], 0.0)
                weights_lo(0)
                weights_lo(1)
                h_full(0)
                h_lo(0)
                for m in range(2, len(pieces)):
                    weights_lo(m)
                dve.wait_ge(S["w_lo_done"], len(pieces))
                dve.wait_ge(S["rot_loaded"], 32)
                for i in range(TT):
                    dve.wait_ge(S["proj_done"], 4 * i + 1)
                    if i >= 1:
                        latent(i - 1, 0)
                        dve.wait_ge(S["r_turned"], 4 * (i - 1) + 2)
                    place(heads_of(R[:, R_AQ:R_BQ], 8), heads_of(pj[:, IN_AQ:IN_AV], 8), 8, 64, rot64, i,
                          S["ropeA_done"])
                    if i >= 1:
                        latent(i - 1, 1)
                    if i + 1 < TT:
                        h_full(i + 1)
                    if i + 1 < TT:
                        h_lo(i + 1)
                    dve.wait_ge(S["v_hi"], 3 * i + 2)
                    place(heads_of(R[:, R_BQ:R_CQ], 16), heads_of(pj[:, IN_BQ:IN_BV], 16), 16, 32, rot32, i,
                          S["ropeB_done"])
                    if i >= 1:
                        latent(i - 1, 2)
                    values_lo(i, 0, pj[:, IN_AV:IN_BQ], V_lo[:, V_A:V_B], V_hi[:, V_A:V_B])
                    values_lo(i, 1, pj[:, IN_BV:IN_CQ], V_lo[:, V_B:V_C], V_hi[:, V_B:V_C])
                    dve.wait_ge(S["c_squared"], 2 * (i + 1))
                    if i >= 1:
                        dve.wait_ge(S["r_turned"], 4 * i)
                    place(heads_of(R[:, R_KR:R_KR + 32], 1), heads_of(pj[:, PJ_KR:PJ_END], 1), 1, 32, rot32, i,
                          S["kr_done"])
                    dve.wait_ge(S["c_rms"], i + 1)
                    if i >= 1:
                        dve.wait_ge(S["c_hi"], i)
                        dve.wait_ge(S["c_lo"], i)
                    dve.tensor_scalar(cn[:, 0:QR], pj[:, PJ_CQ:PJ_CKV], rs[:, i % 2, 1:2], None, ALU.mult)
                    dve.tensor_scalar(cn[:, QR:384], pj[:, PJ_CKV:PJ_KR], rs[:, i % 2, 2:3], None, ALU.mult
                                      ).then_inc(S["c_normed"], 1)
                for step in range(3):
                    latent(TT - 1, step)


def attention_plan(l):
    order = [("C", 0), ("A", 0), ("C", 1), ("B", 0), ("B", 1), ("C", 2), ("A", 1), ("C", 3), ("B", 2), ("B", 3),
             ("C", 4), ("B", 4), ("B", 5), ("C", 5), ("B", 6), ("B", 7)]
    units = [(kind, i, {"A": i, "B": 2 + i // 2, "C": 6 + i}[kind]) for kind, i in order]
    queries = TT if l < DEPTH - 1 else TX
    ctx_keys = list(range(TX, TT))
    steps, chunks, maxima, bounds = [], [], [], []
    for u, (kind, _, _) in enumerate(units):
        first = len(steps)
        if kind == "A":
            for q in range(queries):
                near = [] if q >= TX else [(k, m) for k, m in ((q - 1, "above"), (q, None), (q + 1, "below"))
                                           if 0 <= k < TX]
                for k, m in near + [(k, None) for k in ctx_keys]:
                    steps.append((u, len(chunks), k, m))
                chunks.append((u, q, 1, len(steps) - 1))
            rows = [(q, h) for h in range(3) for q in range(queries)]
            parts = (0,)
        else:
            for q, n in ((0, 4), (4, 4)) + (((TX, TC),) if queries > TX else ()):
                for k in (range(TT) if q < TX else ctx_keys):
                    steps.append((u, len(chunks), k, None))
                chunks.append((u, q, n, len(steps) - 1))
            rows = [(q, 0) for q in range(queries)]
            parts = (0, 1)
        tiles = []
        for j in range(0, len(rows), 2):
            tiles.append((2, rows[j:j + 2]))
            tiles += [(part, [row]) for row in rows[j:j + 2] if row[0] < TX for part in parts]
        maxima.append(tiles)
        bounds.append((first, len(steps)))
    return units, steps, chunks, maxima, bounds, queries


def attend(nc, t, dr, keep, l):
    units, steps, chunks, maxima, bounds, queries = attention_plan(l)
    G, LAG, RING, SRING = len(steps), 5, 6, 3
    NORM, SQUARE, MEAN, ROOT, FINAL, SPLIT2, STORE = (LAG + x for x in (1, 2, 3, 4, 5, 6, 8))
    SPLIT1 = SQUARE
    TAIL = STORE + 1
    ends = {c[3]: n for n, c in enumerate(chunks)}
    starts = {b[0]: u for u, b in enumerate(bounds)}
    SCALE = {"A": A_SCALE, "B": B_SCALE, "C": C_SCALE}
    max_base = [sum(len(m) for m in maxima[:u]) for u in range(len(units))]
    TURN = 3
    jobs = [(-1, "tile", 0, j) for j in range(len(maxima[0]))] + [(-1, "turn", 0, 0)]
    for u in range(1, len(units)):
        a, b = bounds[u - 1][0] + 2, bounds[u - 1][1] - 8
        if units[u][0] == "B" and units[u][1] % 2 == 1:
            a, b = bounds[u - 2][1] - 10, bounds[u - 1][0] + 7
        elif units[u][0] == "B":
            b -= 2
        at = [a + j * (b - a) // len(maxima[u]) for j in range(len(maxima[u]))]
        jobs += [(g, "tile", u, j) for j, g in enumerate(at)] + [(at[-1] + TURN, "turn", u, 0)]
    jobs.sort(key=lambda job: job[0])
    jobs_at, bank_free = {}, []
    for x, (g, what, u, j) in enumerate(jobs):
        jobs_at.setdefault(g, []).append((what, u, j, x))
        bank_free.append(("mx_read", max_base[u] + j + 1) if what == "tile" else ("mneg_done", u + 1))
    two_maps = [units[c[0]][0] == "B" for c in chunks]
    kept = [units[c[0]][0] == "B" and units[c[0]][1] % 2 == 0 for c in chunks]
    order = [sum(not k for k in kept[:n]) for n in range(len(chunks))]
    second = [n for n in range(len(chunks)) if two_maps[n] and not kept[n]]
    nth_second = {n: j for j, n in enumerate(second)}
    before_slot = lambda g, lag: [n for e, n in ends.items() if e == g - lag]
    nth_a = [sum(x[0] == "A" for x in units[:u]) for u in range(len(units))]
    nth_a_chunk = [sum(units[c[0]][0] == "A" for c in chunks[:n]) for n in range(len(chunks))]
    v_load = [len({x[2] for x in units[:u + 1]}) - 1 for u in range(len(units))]

    with ExitStack() as ctx:
        s = Scope(nc, ctx, f"at{l}")
        WB = [s.sb(f"W{b}", [P, 4, TOK], F32R) for b in range(3)]
        WA = s.sb("WA", [P, 8, TOK], F32R)
        Vh = [s.sb(f"Vh{b}", [P, TT, P], F32R) for b in range(2)]
        Vl = [s.sb(f"Vl{b}", [P, TT, P], F32R) for b in range(2)]
        E = s.sb("E", [P, RING, BANK])
        H, L = s.sb("H", [P, RING, BANK], F32R), s.sb("L", [P, RING, BANK], F32R)
        esink = s.sb("esink", [65, 3, TOK])
        zero_one = s.sb("zero_one", [65, P])
        mean64 = s.sb("mean64", [64, 64])
        mcol = s.sb("mcol", [P, 2, 3 * TT])
        mpart = s.sb("mpart", [P, 2, 2, 3, TT])
        mrow = s.sb("mrow", [3 * TT, P], F32R)
        logs, rec = s.sb("logs", [64, BANK]), s.sb("rec", [64, BANK])
        first_map = s.sb("first_map", [64, TOK])
        o = s.sb("o", [64, 3, BANK])
        osq, orn = s.sb("osq", [64, BANK]), s.sb("orn", [64, BANK])
        o_hi, o_lo = s.sb("o_hi", [64, 2, BANK], F32R), s.sb("o_lo", [64, 2, BANK], F32R)
        sc = s.ps("sc", [P, SRING, BANK])
        av = s.ps("av", [P, 2, BANK])
        mx = s.ps("mx", [P, 3, BANK])
        qk_loaded = [s.sem(f"qk_loaded{b}") for b in range(4)]
        v_loaded = [s.sem(f"v_loaded{b}") for b in range(2)]
        o_stored = [s.sem(f"o_stored{b}") for b in range(2)]
        names = ("s_done e_done h_done l_done av_done chunk_done o_done sink_done mx_done mx_read mcol_done mt_done "
                 "mneg_done mrow_loaded consts_done dve_own o_squared mean_done ln_read rn_done o_final o_hi_done "
                 "o_lo_done log_done rec_done")
        S = {n: s.sem(n) for n in names.split()}
        block = ctx.enter_context(nc.Block())
        NLOAD = 7

        rows_loaded = [16 * sum(3 if x[0] == "A" else 1 for x in units[:u + 1]) for u in range(len(units))]

        def rows_of(u):
            return queries * (3 if units[u][0] == "A" else 1)

        def mcol_view(u):
            return mcol[:, u % 2, 0:rows_of(u)].rearrange("p (h q) -> p h q", q=queries)

        def width(n):
            return 3 * P if units[chunks[n][0]][0] == "A" else chunks[n][2] * P

        slot = [3 if x[0] == "A" else (u - nth_a[u]) % 3 for u, x in enumerate(units)]
        W = [WA if b == 3 else WB[b] for b in slot]
        holders = [[x for x in range(u) if slot[x] == slot[u]] for u in range(len(units))]

        def use(u):
            return len(holders[u]) + 1

        @block.sync
        def _(sp):
            T, V, ones = dr["T"], dr["V"], dr["ones"]

            def load(u):
                kind, i, v = units[u]
                w, sem = W[u], qk_loaded[slot[u]]
                if holders[u]:
                    sp.wait_ge(S["s_done"], bounds[holders[u][-1]][1])
                    if kind == "A":
                        sp.wait_ge(S["sink_done"], 3 * nth_a[u])
                if kind == "A":
                    q = [T[j, R_AQ + 192 * i:R_AQ + 192 * (i + 1), :].rearrange("(h p) n -> p h n", h=3)
                         for j in range(2)]
                    k = [T[j, R_AK + 64 * i:R_AK + 64 * (i + 1), :] for j in range(2)]
                    moves = [(w[0:64, 0:3, :], q[0]), (w[64:128, 0:3, :], q[0]), (w[0:64, 6, :], k[0]),
                             (w[64:128, 6, :], k[1]), (w[0:64, 3:6, :], q[1]), (w[0:64, 7, :], k[0]),
                             (w[64:65, 7, :], ones)]
                elif kind == "B":
                    q = [T[j, R_BQ + 32 * i:R_BQ + 32 * (i + 1), :] for j in range(2)]
                    k = [T[j, R_BK + 32 * i:R_BK + 32 * (i + 1), :] for j in range(2)]
                    moves = [(w[0:32, 0, :], q[0]), (w[32:64, 0, :], q[0]), (w[64:96, 0, :], q[1]),
                             (w[0:32, 1, :], k[0]), (w[32:64, 1, :], k[1]), (w[64:96, 1, :], k[0]),
                             (w[96:97, 1, :], ones)]
                else:
                    q = [T[j, R_CQ + 96 * i:R_CQ + 96 * (i + 1), :] for j in range(2)]
                    k = [T[j, R_CN + 64 * i:R_CN + 64 * (i + 1), :] for j in range(2)]
                    kr = [T[j, R_KR:R_KR + 32, :] for j in range(2)]
                    moves = [(w[0:96, 0, :], q[0]), (w[0:96, 2, :], q[1]), (w[0:64, 1, :], k[0]),
                             (w[64:96, 1, :], kr[0]), (w[96:97, 1, :], ones), (w[0:64, 3, :], k[1]),
                             (w[64:96, 3, :], kr[1])]
                for at, (dst, src) in enumerate(moves):
                    if u == 1 and at == 4:
                        sp.wait_ge(S["mrow_loaded"], rows_loaded[0])
                    sp.dma_start(raw(dst), src).then_inc(sem, 16)

            def load_values(u):
                v = units[u][2]
                if u == 0 or v_load[u - 1] != v_load[u]:
                    if v_load[u] < 2:
                        sp.wait_ge(S["consts_done"], 7)
                    else:
                        last = max(x for x in range(u) if v_load[x] == v_load[u] - 2)
                        sp.wait_ge(S["av_done"], bounds[last][1])
                    for j, buf in enumerate((Vh, Vl)):
                        sp.dma_start(raw(buf[v_load[u] % 2][:, :, 0:64]),
                                     V[j, :, 64 * v:64 * (v + 1)].rearrange("(k p) e -> p k e", p=P)
                                     ).then_inc(v_loaded[v_load[u] % 2], 16)

            def store(n):
                u, q, tiles, _ = chunks[n]
                kind, i, _ = units[u]
                b = order[n] % 2
                sp.wait_ge(S["o_lo_done"], order[n] + 1)
                for j, buf in enumerate((o_hi, o_lo)):
                    if kind == "A":
                        dst = dr["mix"][j, 192 * i:192 * (i + 1), q * P:(q + 1) * P].rearrange("(h p) n -> p h n", h=3)
                        src = buf[:, b, 0:3 * P].rearrange("p (h n) -> p h n", h=3)
                    else:
                        row = 384 + 64 * (i // 2) if kind == "B" else 640 + 64 * i
                        dst = dr["mix"][j, row:row + 64, q * P:(q + tiles) * P]
                        src = buf[:, b, 0:tiles * P]
                    sp.dma_start(dst, raw(src)).then_inc(o_stored[b], 16)

            load(0)
            load_values(0)
            load(1)
            for g in range(G + TAIL):
                if g in starts and starts[g] + 2 < len(units):
                    load(starts[g] + 2)
                if g - LAG - 2 in starts and starts[g - LAG - 2] + 1 < len(units):
                    load_values(starts[g - LAG - 2] + 1)
                for n in before_slot(g, STORE):
                    if not kept[n]:
                        store(n)
            total = order[-1] + 1
            for b in range(2):
                sp.wait_ge(o_stored[b], 32 * ((total + 1 - b) // 2))

        @block.gpsimd
        def _(pool):
            for b in range(2):
                pool.memset(raw(Vh[b][:, :, 64:128]), 1.0).then_inc(S["consts_done"], 1)
                pool.memset(raw(Vl[b][:, :, 64:128]), 0.0).then_inc(S["consts_done"], 1)
            pool.wait_ge(S["consts_done"], 4)
            pool.memset(zero_one[64:65, 0:64], 0.0).then_inc(S["consts_done"], 1)
            pool.wait_ge(S["consts_done"], 5)
            pool.memset(zero_one[64:65, 64:128], 1.0).then_inc(S["consts_done"], 1)
            pool.wait_ge(S["consts_done"], 6)
            pool.memset(mean64[:], 1.0 / 64).then_inc(S["consts_done"], 1)

            def hi(n):
                kind = units[chunks[n][0]][0]
                if kind == "B":
                    pool.wait_ge(S["o_final"], nth_second[n] + 1)
                else:
                    pool.wait_ge(S["o_done"], n + 1)
                b = order[n] % 2
                if order[n] >= 2:
                    pool.wait_ge(o_stored[b], 32 * (order[n] // 2))
                pool.tensor_copy(o_hi[:, b, 0:width(n)], o[:, n % 3, 0:width(n)]).then_inc(S["o_hi_done"], 1)

            def lo(n):
                b = order[n] % 2
                pool.wait_ge(S["o_hi_done"], order[n] + 1)
                if n in nth_second:
                    pool.wait_ge(S["o_final"], nth_second[n] + 1)
                else:
                    pool.wait_ge(S["o_done"], n + 1)
                if order[n] >= 2:
                    pool.wait_ge(o_stored[b], 32 * (order[n] // 2))
                pool.tensor_tensor(o_lo[:, b, 0:width(n)], o[:, n % 3, 0:width(n)], raw(o_hi[:, b, 0:width(n)]),
                                  ALU.subtract).then_inc(S["o_lo_done"], 1)

            for g in range(G + TAIL):
                for n in before_slot(g, SPLIT1):
                    if not two_maps[n]:
                        hi(n)
                        lo(n)
                for n in before_slot(g, SPLIT2):
                    if n in nth_second:
                        hi(n)
                        lo(n)


        @block.scalar
        def _(act):
            def negate(u, x):
                rows = rows_of(u)
                act.wait_ge(S["mt_done"], u + 1)
                if u >= 1:
                    act.wait_ge(S["mrow_loaded"], rows_loaded[u - 1])
                act.activation(mrow[0:rows, :], mx[0:rows, x % 3, 0:P], ACT.Copy, scale=-1.0
                               ).then_inc(S["mneg_done"], 1)
                act.wait_ge(S["mneg_done"], u + 1)
                if units[u][0] == "A":
                    for h in range(3):
                        act.dma_start(raw(W[u][64:65, 3 + h, 0:queries * P]),
                                      raw(mrow[h * queries:(h + 1) * queries, :])).then_inc(S["mrow_loaded"], 16)
                else:
                    act.dma_start(raw(W[u][96:97, 0, 0:queries * P]), raw(mrow[0:queries, :])
                                  ).then_inc(S["mrow_loaded"], 16)

            def weight_sums(n):
                w = width(n)
                if units[chunks[n][0]][0] == "A":
                    act.wait_ge(S["chunk_done"], nth_a_chunk[n] + 1)
                else:
                    act.wait_ge(S["av_done"], chunks[n][3] + 1)
                if n >= 1:
                    act.wait_ge(S["rec_done"], n)
                    act.wait_ge(S["o_done"], n)
                act.activation(logs[:, 0:w], av[64:128, n % 2, 0:w], ACT.Ln).then_inc(S["log_done"], 1)
                act.wait_ge(S["log_done"], n + 1)
                act.activation(rec[:, 0:w], logs[:, 0:w], ACT.Exp, scale=-1.0).then_inc(S["rec_done"], 1)

            act.preload_act_table_set("natural_log_exp_and_others")
            negate(0, jobs_at[-1][-1][-1])
            for g in range(G + TAIL):
                for n in before_slot(g, NORM):
                    weight_sums(n)
                for n in before_slot(g, SQUARE):
                    if n in nth_second:
                        j = nth_second[n]
                        act.wait_ge(S["o_done"], n + 1)
                        if j >= 1:
                            act.wait_ge(S["mean_done"], j)
                        act.activation(osq[:, 0:width(n)], o[:, n % 3, 0:width(n)], ACT.Square
                                       ).then_inc(S["o_squared"], 1)
                for n in before_slot(g, ROOT):
                    if n in nth_second:
                        j = nth_second[n]
                        act.wait_ge(S["mean_done"], j + 1)
                        if j >= 1:
                            act.wait_ge(S["o_final"], j)
                        act.activation(orn[:, 0:width(n)], av[0:64, n % 2, 0:width(n)], ACT.Ln,
                                       bias=keep["eps"][0:64, 0:1]).then_inc(S["ln_read"], 1)
                        act.wait_ge(S["ln_read"], j + 1)
                        act.activation(orn[:, 0:width(n)], orn[:, 0:width(n)], ACT.Exp, scale=-0.5
                                       ).then_inc(S["rn_done"], 1)
                if g < G:
                    u, n, _, _ = steps[g]
                    kind, i, _ = units[u]
                    if g in starts and kind == "A":
                        act.wait_ge(S["mrow_loaded"], rows_loaded[u])
                        if nth_a[u]:
                            act.wait_ge(S["chunk_done"], queries)
                        for h in range(3):
                            act.activation(esink[64:65, h, 0:queries * P], raw(W[u][64:65, 3 + h, 0:queries * P]),
                                           ACT.Exp, scale=A_SCALE, bias=keep["sink"][64:65, l, 3 * i + h:3 * i + h + 1]
                                           ).then_inc(S["sink_done"], 1)
                    w = width(n)
                    act.wait_ge(S["s_done"], g + 1)
                    if g >= RING:
                        act.wait_ge(S["l_done"], g - RING + 1)
                        act.wait_ge(S["av_done"], g - RING + 1)
                    act.activation(E[:, g % RING, 0:w], sc[:, g % SRING, 0:w], ACT.Exp, scale=SCALE[kind]
                                   ).then_inc(S["e_done"], 1)
                    act.activation(H[:, g % RING, 0:w], sc[:, g % SRING, 0:w], ACT.Exp, scale=SCALE[kind]
                                   ).then_inc(S["h_done"], 1)
                for what, u, _, x in jobs_at.get(g, ()):
                    if what == "turn":
                        negate(u, x)

        @block.tensor
        def _(pe):
            def maximum(u, j, x):
                kind, i, _ = units[u]
                w = W[u]
                part, rows = maxima[u][j]
                keys = w[:, 6, :] if kind == "A" else w[0:96, 1, :]

                def stationary(q, h):
                    cols = slice(q * P, (q + 1) * P)
                    return w[:, h, cols] if kind == "A" else w[0:96, 0, cols]

                if j == 0:
                    pe.wait_ge(qk_loaded[slot[u]], 16 * NLOAD * use(u))
                ring_bank(x)
                bank = mx[:, x % 3, :]
                if part == 2:
                    for z, (q, h) in enumerate(rows):
                        mm = pe.matmul(bank[:, z * CTX:(z + 1) * CTX], stationary(q, h), keys[:, SEQ:TOK],
                                       start=True, stop=True)
                elif kind == "A":
                    q, h = rows[0]
                    a, b = max(q - 1, 0), min(q + 2, TX)
                    mm = pe.matmul(bank[:, 0:(b - a) * P], stationary(q, h), keys[:, a * P:b * P],
                                   start=True, stop=True)
                    for k in range(a, b):
                        if k != q:
                            mm = pe.matmul(bank[:, (k - a) * P:(k - a + 1) * P], keep["identb"][:],
                                           keep["below" if k < q else "above"][:], start=False, stop=True,
                                           skip_group_check=True)
                else:
                    mm = pe.matmul(bank, stationary(*rows[0]), keys[:, part * BANK:(part + 1) * BANK],
                                   start=True, stop=True)
                mm.then_inc(S["mx_done"], 1)

            def ring_bank(x):
                if x >= 3:
                    pe.wait_ge(S[bank_free[x - 3][0]], bank_free[x - 3][1])

            def turn_maxima(u, x):
                rows = rows_of(u)
                pe.wait_ge(S["mcol_done"], u + 1)
                ring_bank(x)
                pe.transpose(mx[0:rows, x % 3, 0:P], mcol_view(u).rearrange("p h q -> p (h q)"), keep["ident"][:]
                             ).then_inc(S["mt_done"], 1)

            def score(g):
                u, n, k, mask = steps[g]
                kind, i, _ = units[u]
                w = W[u]
                _, q, tiles, _ = chunks[n]
                if g in starts:
                    pe.wait_ge(S["mrow_loaded"], rows_loaded[u])
                if g >= SRING:
                    pe.wait_ge(S["h_done"], g - SRING + 1)
                out = sc[:, g % SRING, 0:width(n)]
                keys = slice(k * P, (k + 1) * P)
                cols = slice(q * P, (q + tiles) * P)
                if kind == "A":
                    o3 = out.rearrange("p (h n) -> p h n", h=3)
                    pe.matmul(o3, w[:, 6, keys], w[:, 0:3, cols], start=True, stop=False)
                    mm = pe.matmul(o3, w[0:65, 7, keys], w[0:65, 3:6, cols], start=False, stop=mask is None)
                    if mask is not None:
                        mm = pe.matmul(o3, keep["identb"][:], keep[mask][:].unsqueeze(1).to_broadcast([P, 3, P]),
                                       start=False, stop=True)
                elif kind == "B":
                    mm = pe.matmul(out, w[0:97, 1, keys], w[0:97, 0, cols], start=True, stop=True)
                else:
                    pe.matmul(out, w[0:97, 1, keys], w[0:97, 0, cols], start=True, stop=False)
                    pe.matmul(out, w[0:96, 1, keys], w[0:96, 2, cols], start=False, stop=False)
                    mm = pe.matmul(out, w[0:96, 3, keys], w[0:96, 0, cols], start=False, stop=True)
                mm.then_inc(S["s_done"], 1)

            def values(g):
                u, n, k, _ = steps[g]
                kind, v = units[u][0], v_load[u]
                first, last = g == 0 or steps[g - 1][1] != n, g in ends
                if first:
                    pe.wait_ge(v_loaded[v % 2], 32 * (v // 2 + 1))
                    if n >= 2:
                        pe.wait_ge(S["o_done"], n - 1)
                        if n - 2 in nth_second:
                            pe.wait_ge(S["ln_read"], nth_second[n - 2] + 1)
                pe.wait_ge(S["h_done"], g + 1)
                out = av[:, n % 2, 0:width(n)]
                h, lo = H[:, g % RING, 0:width(n)], L[:, g % RING, 0:width(n)]
                pe.matmul(out, Vh[v % 2][:, k, :], h, start=first, stop=False)
                pe.matmul(out, Vl[v % 2][:, k, :], h, start=False, stop=False)
                pe.wait_ge(S["l_done"], g + 1)
                mm = pe.matmul(out, Vh[v % 2][:, k, :], lo, start=False, stop=last and kind != "A")
                mm.then_inc(S["av_done"], 1)
                if last:
                    if kind == "A":
                        q = chunks[n][1]
                        pe.wait_ge(S["sink_done"], 3 * (nth_a[u] + 1))
                        pe.matmul(out.rearrange("p (h n) -> p h n", h=3), zero_one[64:65, :],
                                  esink[64:65, :, q * P:(q + 1) * P], start=False, stop=True
                                  ).then_inc(S["chunk_done"], 1)

            pe.wait_ge(S["consts_done"], 7)
            def job(what, u, j, x):
                if what == "tile":
                    maximum(u, j, x)
                else:
                    turn_maxima(u, x)

            for each in jobs_at[-1]:
                job(*each)
            for g in range(G + MEAN + 1):
                for n in before_slot(g, MEAN):
                    if n in nth_second:
                        pe.wait_ge(S["o_squared"], nth_second[n] + 1)
                        pe.matmul(av[0:64, n % 2, 0:width(n)], mean64[:], osq[:, 0:width(n)], start=True, stop=True
                                  ).then_inc(S["mean_done"], 1)
                if g < G:
                    score(g)
                ahead = jobs_at.get(g, [])
                for each in ahead[:1]:
                    job(*each)
                if 0 <= g - LAG < G:
                    values(g - LAG)
                for each in ahead[1:]:
                    job(*each)

        @block.vector
        def _(dve):
            linked = 0

            def link(ins):
                nonlocal linked
                linked += 1
                ins.then_inc(S["dve_own"], 1)
                dve.wait_ge(S["dve_own"], linked)

            def reduce_max(u, j, x):
                part, rows = maxima[u][j]
                q, h = rows[0]
                dve.wait_ge(S["mx_done"], max_base[u] + j + 1)
                if j == 0 and u >= 2:
                    dve.wait_ge(S["mt_done"], u - 1)
                if part == 2:
                    first = h * queries + q
                    dst = mcol[:, u % 2, first:first + 2]
                    src = mx[:, x % 3, :].rearrange("p (z n) -> p z n", z=2)
                else:
                    dst = mpart[:, u % 2, part, h, q:q + 1]
                    near = (min(q + 2, TX) - max(q - 1, 0)) * P if units[u][0] == "A" else BANK
                    src = mx[:, x % 3, 0:near]
                dve.reduce_max(dst, src, AX_X).then_inc(S["mx_read"], 1)

            def maxima_done(u):
                kind, i, _ = units[u]
                dve.wait_ge(S["mx_read"], max_base[u] + len(maxima[u]))
                whole = mcol_view(u)
                latent = whole[:, :, 0:TX]
                heads = whole.shape[1]
                ins = dve.tensor_tensor(latent, latent, mpart[:, u % 2, 0, 0:heads, 0:TX], ALU.max)
                link(ins)
                if kind == "A":
                    sink = keep["sinkdiv"][:, l, 3 * i:3 * i + 3].unsqueeze(2).to_broadcast([P, 3, queries])
                    dve.tensor_tensor(whole, whole, sink, ALU.max).then_inc(S["mcol_done"], 1)
                else:
                    dve.tensor_tensor(latent, latent, mpart[:, u % 2, 1, 0:1, 0:TX], ALU.max).then_inc(S["mcol_done"], 1)

            def normalise(n):
                w = width(n)
                if n >= 3 and not kept[n]:
                    done = sum(1 for x in range(n - 2) if not kept[x])
                    if done:
                        dve.wait_ge(S["o_lo_done"], done)
                dve.wait_ge(S["rec_done"], n + 1)
                if not two_maps[n]:
                    dve.tensor_tensor(o[:, n % 3, 0:w], av[0:64, n % 2, 0:w], rec[:, 0:w], ALU.mult
                                      ).then_inc(S["o_done"], 1)
                    return
                c = slice(chunks[n][1] * P, chunks[n][1] * P + w)
                if kept[n]:
                    dve.tensor_tensor(first_map[:, c], av[0:64, n % 2, 0:w], rec[:, 0:w], ALU.mult
                                      ).then_inc(S["o_done"], 1)
                    return
                link(dve.tensor_tensor(o[:, n % 3, 0:w], av[0:64, n % 2, 0:w], rec[:, 0:w], ALU.mult))
                dve.scalar_tensor_tensor(out=o[:, n % 3, 0:w], in0=o[:, n % 3, 0:w],
                                         scalar=keep["neglam"][0:64, l:l + 1], in1=first_map[:, c],
                                         op0=ALU.mult, op1=ALU.add).then_inc(S["o_done"], 1)

            def row_maxima(g):
                for what, u, j, x in jobs_at.get(g, ()):
                    if what == "tile":
                        reduce_max(u, j, x)
                        if j == len(maxima[u]) - 1:
                            maxima_done(u)

            row_maxima(-1)
            for g in range(G + TAIL):
                for n in before_slot(g, NORM):
                    normalise(n)
                for n in before_slot(g, FINAL):
                    if n in nth_second:
                        dve.wait_ge(S["rn_done"], nth_second[n] + 1)
                        w = width(n)
                        dve.scalar_tensor_tensor(out=o[:, n % 3, 0:w], in0=o[:, n % 3, 0:w],
                                                 scalar=keep["dsn"][0:64, l:l + 1], in1=orn[:, 0:w],
                                                 op0=ALU.mult, op1=ALU.mult).then_inc(S["o_final"], 1)
                row_maxima(g)
                if g < G:
                    w = width(steps[g][1])
                    dve.wait_ge(S["h_done"], g + 1)
                    if g >= RING:
                        dve.wait_ge(S["av_done"], g - RING + 1)
                    dve.tensor_tensor(L[:, g % RING, 0:w], E[:, g % RING, 0:w], raw(H[:, g % RING, 0:w]), ALU.subtract
                                      ).then_inc(S["l_done"], 1)


def mix_out(nc, t, dr, keep, l, h_hi, h_lo):
    NT = TT if l < DEPTH - 1 else TX
    with ExitStack() as outer:
        w = Scope(nc, outer, f"mw{l}")
        wo_hi, wo_lo = w.sb("wo_hi", [P, KT, D], F32R), w.sb("wo_lo", [P, KT, D], F32R)
        with ExitStack() as ctx:
            s = Scope(nc, ctx, f"mo{l}")
            WRING = 4
            wring = s.sb("wring", [P, WRING, D])
            mix = s.sb("mix", [P, 2, 2, KT, P], F32R)
            x = s.sb("x", [P, 2, D])
            y = s.sb("y", [P, 2, D])
            gate = s.sb("gate", [P, 2, D])
            junk = s.sb("junk", [P, D], BF16)
            ss, ms, rs = s.sb("ss", [P, 2, 2]), s.sb("ms", [P, 2, 2]), s.sb("rs", [P, 2, 2])
            pm = s.ps("pm", [P, 2, 2 * BANK])
            pt = s.ps("pt", [P, 2 * BANK])
            mix_loaded = [s.sem(f"mix_loaded{b}") for b in range(2)]
            x_loaded = [s.sem(f"x_loaded{b}") for b in range(2)]
            w_loaded = [s.sem(f"w_loaded{b}") for b in range(WRING)]
            x_stored = [s.sem(f"x_stored{b}") for b in range(2)]
            names = ("gate_loaded mm_done m_squared m_rms y_done x_done x_squared x_rms normed turned full hi lo "
                     "pool_own w_hi_done w_lo_done")
            S = {n: s.sem(n) for n in names.split()}
            block = ctx.enter_context(nc.Block())

            @block.sync
            def _(sp):
                def load_weights():
                    for k in range(KT):
                        if k >= WRING:
                            sp.wait_ge(S["w_lo_done"], k - WRING + 1)
                        sp.dma_start(wring[:, k % WRING, :], t["w_out"][l, k * P:(k + 1) * P, :]
                                     ).then_inc(w_loaded[k % WRING], 16)

                for c in range(2):
                    sp.dma_start(gate[:, c, :], dr["gate"][l, 0, c].partition_broadcast(P)).then_inc(S["gate_loaded"], 16)
                def store(i):
                    sp.wait_ge(S["x_done"], i + 1)
                    sp.dma_start(dr["x1"][i * P:(i + 1) * P, :], x[:, i % 2, :]).then_inc(x_stored[i % 2], 16)

                for i in range(NT):
                    b = i % 2
                    if i >= 2:
                        sp.wait_ge(S["mm_done"], i - 1)
                    for j in range(2):
                        sp.dma_start(raw(mix[:, b, j]), dr["mix"][j, :, i * P:(i + 1) * P].rearrange("(k p) n -> p k n", p=P)
                                     ).then_inc(mix_loaded[b], 16)
                    if i >= 2:
                        store(i - 2)
                        sp.wait_ge(x_stored[b], 16 * (i // 2))
                        sp.wait_ge(S["normed"], i - 1)
                    if l == 0:
                        src = t["x"][0, i * P:(i + 1) * P, :] if i < TX else t["ctx"][0, (i - TX) * P:(i - TX + 1) * P, :]
                    else:
                        src = dr["x"][i * P:(i + 1) * P, :]
                    sp.dma_start(x[:, b, :], src).then_inc(x_loaded[b], 16)
                    if i == 0:
                        load_weights()
                for i in (NT - 2, NT - 1):
                    store(i)
                for b in range(2):
                    sp.wait_ge(x_stored[b], 16 * ((NT + 1 - b) // 2))

            @block.gpsimd
            def _(pool):
                own = 0
                for i in range(NT):
                    b = i % 2
                    for c, before, after in ((0, "m_squared", "m_rms"), (1, "x_squared", "x_rms")):
                        pool.wait_ge(S[before], i + 1)
                        if i >= 2:
                            pool.wait_ge(S["normed"], i - 1)
                            pool.wait_ge(S["y_done"], i - 1)
                        pool.tensor_scalar(ms[:, b, c:c + 1], ss[:, b, c:c + 1], 1.0 / D, EPS, ALU.mult, ALU.add
                                           ).then_inc(S["pool_own"], 1)
                        own += 1
                        pool.wait_ge(S["pool_own"], own)
                        pool.tensor_tensor(rs[:, b, c:c + 1], ms[:, b, c:c + 1], keep["mhalf"][:, 0:1], ALU.pow
                                           ).then_inc(S[after], 1)

            @block.scalar
            def _(act):
                for k in range(KT):
                    split_hi(act, k, wring[:, k % WRING, :], w_loaded, wo_hi[:, k, :], S["w_hi_done"])
                for i in range(NT + 1):
                    if i < NT:
                        act.wait_ge(S["mm_done"], i + 1)
                        if i >= 2:
                            act.wait_ge(S["m_rms"], i - 1)
                        act.activation(junk[:], pm[:, i % 2, :], ACT.Square, accum_out=ss[:, i % 2, 0:1]
                                       ).then_inc(S["m_squared"], 1)
                        act.wait_ge(S["x_done"], i + 1)
                        if i >= 2:
                            act.wait_ge(S["x_rms"], i - 1)
                        act.activation(junk[:], x[:, i % 2, :], ACT.Square, accum_out=ss[:, i % 2, 1:2]
                                       ).then_inc(S["x_squared"], 1)
                        act.wait_ge(S["x_rms"], i + 1)
                        act.activation(y[:, i % 2, :], x[:, i % 2, :], ACT.Copy, scale=rs[:, i % 2, 1:2]
                                       ).then_inc(S["normed"], 1)
                    if i >= 1:
                        j = i - 1
                        act.wait_ge(S["full"], j + 1)
                        act.copy(h_hi[:, :, j * P:(j + 1) * P], y[:, j % 2, :].rearrange("p (k n) -> p k n", k=KT)
                                 ).then_inc(S["hi"], 1)

            @block.tensor
            def _(pe):
                def turn(i):
                    pe.wait_ge(S["normed"], i + 1)
                    if i >= 1:
                        pe.wait_ge(S["full"], i)
                    for k in range(KT):
                        mm = pe.transpose(pt[:, k * P:(k + 1) * P], y[:, i % 2, k * P:(k + 1) * P], keep["ident"][:])
                    mm.then_inc(S["turned"], 1)

                for i in range(NT):
                    b = i % 2
                    pe.wait_ge(mix_loaded[b], 32 * (i // 2 + 1))
                    if i >= 2:
                        pe.wait_ge(S["y_done"], i - 1)
                        pe.wait_ge(S["m_squared"], i - 1)
                    for k in range(KT):
                        if i == 0:
                            pe.wait_ge(S["w_lo_done"], k + 1)
                        for n in range(2):
                            c = slice(n * BANK, (n + 1) * BANK)
                            mm = three_pass(pe, pm[:, b, c], mix[:, b, 0, k, :], mix[:, b, 1, k, :],
                                            wo_hi[:, k, c], wo_lo[:, k, c], k == 0, k == KT - 1)
                    mm.then_inc(S["mm_done"], 1)
                    if i >= 1:
                        turn(i - 1)
                turn(NT - 1)

            @block.vector
            def _(dve):
                for k in range(KT):
                    split_lo(dve, k, wring[:, k % WRING, :], w_loaded, wo_hi[:, k, :], wo_lo[:, k, :],
                             S["w_hi_done"], S["w_lo_done"])
                dve.wait_ge(S["gate_loaded"], 32)
                for i in range(NT + 1):
                    if i < NT:
                        b, c = i % 2, 0 if i < TX else 1
                        dve.wait_ge(S["m_rms"], i + 1)
                        if i >= 2:
                            dve.wait_ge(S["hi"], i - 1)
                            dve.wait_ge(S["lo"], i - 1)
                        dve.scalar_tensor_tensor(out=y[:, b, :], in0=pm[:, b, :], scalar=rs[:, b, 0:1],
                                                 in1=gate[:, c, :], op0=ALU.mult, op1=ALU.mult).then_inc(S["y_done"], 1)
                        dve.wait_ge(S["y_done"], i + 1)
                        dve.wait_ge(x_loaded[b], 16 * (i // 2 + 1))
                        dve.tensor_tensor(x[:, b, :], x[:, b, :], y[:, b, :], ALU.add).then_inc(S["x_done"], 1)
                    if i >= 1:
                        j = i - 1
                        c = 0 if j < TX else 1
                        dve.wait_ge(S["turned"], j + 1)
                        for k in range(KT):
                            ins = dve.tensor_scalar(y[:, j % 2, k * P:(k + 1) * P], pt[:, k * P:(k + 1) * P],
                                                    keep["modT"][:, l, 3, k, c:c + 1], keep["modT"][:, l, 2, k, c:c + 1],
                                                    ALU.mult, ALU.add)
                        ins.then_inc(S["full"], 1)
                        dve.wait_ge(S["full"], j + 1)
                        dve.wait_ge(S["hi"], j + 1)
                        sl = slice(j * P, (j + 1) * P)
                        dve.tensor_tensor(h_lo[:, :, sl], y[:, j % 2, :].rearrange("p (k n) -> p k n", k=KT),
                                          raw(h_hi[:, :, sl]), ALU.subtract).then_inc(S["lo"], 1)


def ffn(nc, t, dr, keep, l, h_hi, h_lo, acc, out):
    NT = TT if l < DEPTH - 1 else TX
    CH = [(a, min(a + BANK, NT * P)) for a in range(0, NT * P, BANK)]
    NC = len(CH)
    PAIRS = FT // 2
    with ExitStack() as ctx:
        s = Scope(nc, ctx, f"ff{l}")
        rawp = [s.sb(f"raw{b}", [P, D]) for b in range(3)]
        w_hi = s.sb("w_hi", [P, 2, 2, D], F32R)
        w_lo = s.sb("w_lo", [P, 2, 2, D], F32R)
        d_hi, d_lo = s.sb("d_hi", [P, 2, D], F32R), s.sb("d_lo", [P, 2, D], F32R)
        g_hi, g_lo = s.sb("g_hi", [P, 2, NT * P], F32R), s.sb("g_lo", [P, 2, NT * P], F32R)
        sg = s.sb("sg", [P, 2, BANK])
        pg = s.ps("pg", [P, 2, 2, BANK])
        pd = s.ps("pd", [P, 2, 2 * BANK])
        raw_loaded = [s.sem(f"raw_loaded{b}") for b in range(3)]
        XRING = 4
        x = [raw(h_hi[:, b, 0:D]) for b in range(XRING)]
        gate = [raw(h_lo[:, c, 0:D]) for c in range(2)]
        junk = [h_lo[:, 2 + b, 0:D] for b in range(2)]
        ss, ms, rs = s.sb("ss", [P, NT]), s.sb("ms", [P, NT]), s.sb("rs", [P, NT])
        x_loaded = [s.sem(f"x_loaded{b}") for b in range(XRING)]
        names = ("w_hi_done w_lo_done gu_bank silu_done prod_done g_hi_done g_lo_done d_tile acc_done zeroed "
                 "gate_loaded squared rms pool_own gated x_done stored")
        S = {n: s.sem(n) for n in names.split()}
        CREDIT, D_CREDIT = 2, 1
        block = ctx.enter_context(nc.Block())

        def gate_up(name, f):
            return t[name][l].rearrange("(k p) (f n) -> f p k n", p=P, n=P)[f]

        def down(f):
            return t["w_down"][l].rearrange("(f p) n -> f p n", p=P)[f]

        def count(i, p):
            return 6 * i + p + 4

        @block.sync
        def _(sp):
            def load(q, slot, src, wait):
                if wait is not None:
                    sp.wait_ge(S["w_lo_done"], wait)
                dst = rawp[slot][:]
                if len(src.shape) == 3:
                    dst = dst.rearrange("p (k n) -> p k n", k=KT)
                sp.dma_start(dst, src).then_inc(raw_loaded[slot], 16)

            def turn(i, last):
                for p in range(2 if last else 6):
                    src = down(2 * i + p) if p < 2 else gate_up(("w_gate", "w_up")[p % 2], 2 * (i + 1) + (p - 2) // 2)
                    load(None, (4 + p) % 3, src, 6 * i + p + 2)

            for p in range(4):
                load(None, p % 3, gate_up(("w_gate", "w_up")[p % 2], p // 2), p - 2 if p >= 3 else None)
            with sp.Fori(0, PAIRS - 1) as i:
                turn(i, False)
            turn(PAIRS - 1, True)

            def load_x(j):
                sp.dma_start(x[j % XRING], dr["x1"][j * P:(j + 1) * P, :]).then_inc(x_loaded[j % XRING], 16)

            sp.wait_ge(S["gu_bank"], 2 * NC * PAIRS)
            for c in range(2):
                sp.dma_start(gate[c], dr["gate"][l, 1, c].partition_broadcast(P)).then_inc(S["gate_loaded"], 16)
            for j in range(XRING):
                load_x(j)
            for j in range(NT):
                sp.wait_ge(S["x_done"], j + 1)
                dst = out[0, j * P:(j + 1) * P, :] if l == DEPTH - 1 else dr["x"][j * P:(j + 1) * P, :]
                sp.dma_start(dst, acc[:, j, :]).then_inc(S["stored"], 16)
                if j + XRING < NT:
                    load_x(j + XRING)
            sp.wait_ge(S["stored"], 16 * NT)

        @block.gpsimd
        def _(pool):
            for j in range(NT):
                ins = pool.memset(acc[:, j, :], 0.0)
            ins.then_inc(S["zeroed"], 1)
            for j in range(NT + 1):
                if j < NT:
                    pool.wait_ge(S["squared"], j + 1)
                    pool.tensor_scalar(ms[:, j:j + 1], ss[:, j:j + 1], 1.0 / D, EPS, ALU.mult, ALU.add
                                       ).then_inc(S["pool_own"], 1)
                    pool.wait_ge(S["pool_own"], j + 1)
                    pool.tensor_tensor(rs[:, j:j + 1], ms[:, j:j + 1], keep["mhalf"][:, 0:1], ALU.pow
                                       ).then_inc(S["rms"], 1)
                if j >= 1:
                    b = (j - 1) % XRING
                    pool.wait_ge(S["gated"], j)
                    pool.wait_ge(x_loaded[b], 16 * ((j - 1) // XRING + 1))
                    pool.tensor_tensor(acc[:, j - 1, :], x[b], acc[:, j - 1, :], ALU.add).then_inc(S["x_done"], 1)

        def split(eng, p, i, hi_side):
            if p < 2:
                hi, lo = d_hi[:, p, :], d_lo[:, p, :]
            else:
                hi, lo = w_hi[:, (p - 2) // 2, p % 2, :], w_lo[:, (p - 2) // 2, p % 2, :]
            if i is None:
                q = p - 2
                slot, uses, done = q % 3, q // 3 + 1, q + 1
            else:
                slot, uses, done = (4 + p) % 3, 2 * i + (4 + p) // 3 + 1, count(i, p) + 1
                if p < 2:
                    eng.wait_ge(S["d_tile"], NT * i + D_CREDIT)
                else:
                    eng.wait_ge(S["gu_bank"], NC * (2 * i + (p - 2) // 2 + 1))
            if hi_side:
                eng.wait_ge(raw_loaded[slot], 16 * uses)
                eng.copy(hi, rawp[slot][:]).then_inc(S["w_hi_done"], 1)
            else:
                eng.wait_ge(S["w_hi_done"], done)
                eng.wait_ge(raw_loaded[slot], 16 * uses)
                eng.tensor_tensor(lo, rawp[slot][:], raw(hi), ALU.subtract).then_inc(S["w_lo_done"], 1)

        @block.scalar
        def _(act):
            def turn(i, last):
                for f in range(2):
                    for c, (a, b) in enumerate(CH):
                        e = 2 * NC * i + f * NC + c
                        z = (f * NC + c) % 2
                        act.wait_ge(S["gu_bank"], e + 1)
                        act.wait_ge(S["g_lo_done"], e + 1)
                        act.activation(sg[:, z, 0:b - a], pg[:, z, 0, 0:b - a], ACT.Silu).then_inc(S["silu_done"], 1)
                        if c < 2 and not (last and f == 1):
                            split(act, 2 * f + c, i, True)
                        act.wait_ge(S["prod_done"], e + 1 + CREDIT)
                        act.wait_ge(S["d_tile"], NT * i + D_CREDIT)
                        act.copy(g_hi[:, f, a:b], sg[:, z, 0:b - a]).then_inc(S["g_hi_done"], 1)
                if not last:
                    split(act, 4, i, True)
                    split(act, 5, i, True)

            for p in range(2, 6):
                split(act, p, None, True)
            with act.Fori(0, PAIRS - 1) as i:
                turn(i, False)
            turn(PAIRS - 1, True)
            act.wait_ge(S["gu_bank"], 2 * NC * PAIRS)
            for j in range(NT):
                act.wait_ge(S["acc_done"], NT * (PAIRS - 1) + j + 1 + CREDIT)
                if j >= 2:
                    act.wait_ge(S["squared"], j - 1)
                act.activation(junk[j % 2], acc[:, j, :], ACT.Square, accum_out=ss[:, j:j + 1]
                               ).then_inc(S["squared"], 1)

        @block.tensor
        def _(pe):
            def turn(i):
                for f in range(2):
                    pe.wait_ge(S["w_lo_done"], 6 * i + 2 * f + 2)
                    for c, (a, b) in enumerate(CH):
                        z = (f * NC + c) % 2
                        pe.wait_ge(S["prod_done"], 2 * NC * i + f * NC + c + 1)
                        for x in range(2):
                            for k in range(KT):
                                kk = slice(k * P, (k + 1) * P)
                                mm = three_pass(pe, pg[:, z, x, 0:b - a], w_hi[:, f, x, kk], w_lo[:, f, x, kk],
                                                h_hi[:, k, a:b], h_lo[:, k, a:b], k == 0, k == KT - 1)
                        mm.then_inc(S["gu_bank"], 1)
                pe.wait_ge(S["w_lo_done"], 6 * i + 6)
                for j in range(NT):
                    if j % 4 == 0:
                        pe.wait_ge(S["g_lo_done"], 2 * NC * i + NC + j // 4 + 1 + CREDIT)
                    pe.wait_ge(S["acc_done"], NT * i + j + 1)
                    tok = slice(j * P, (j + 1) * P)
                    for n in range(2):
                        c = slice(n * BANK, (n + 1) * BANK)
                        for f in range(2):
                            mm = three_pass(pe, pd[:, j % 2, c], g_hi[:, f, tok], g_lo[:, f, tok],
                                            d_hi[:, f, c], d_lo[:, f, c], f == 0, f == 1)
                    mm.then_inc(S["d_tile"], 1)

            pe.nop().then_inc(S["d_tile"], D_CREDIT)
            with pe.Fori(0, PAIRS) as i:
                turn(i)

        @block.vector
        def _(dve):
            def turn(i, last):
                for f in range(2):
                    for c, (a, b) in enumerate(CH):
                        e = 2 * NC * i + f * NC + c
                        z = (f * NC + c) % 2
                        dve.wait_ge(S["silu_done"], e + 1)
                        dve.tensor_tensor(sg[:, z, 0:b - a], sg[:, z, 0:b - a], pg[:, z, 1, 0:b - a], ALU.mult
                                          ).then_inc(S["prod_done"], 1)
                        if c < 2 and not (last and f == 1):
                            split(dve, 2 * f + c, i, False)
                        dve.wait_ge(S["g_hi_done"], e + 1)
                        dve.wait_ge(S["prod_done"], e + 1 + CREDIT)
                        dve.wait_ge(S["d_tile"], NT * i + D_CREDIT)
                        dve.tensor_tensor(g_lo[:, f, a:b], sg[:, z, 0:b - a], raw(g_hi[:, f, a:b]), ALU.subtract
                                          ).then_inc(S["g_lo_done"], 1)
                for j in range(NT):
                    if not last and j in (1, 3):
                        split(dve, 4 + j // 2, i, False)
                    dve.wait_ge(S["d_tile"], NT * i + j + 1 + D_CREDIT)
                    dve.tensor_tensor(acc[:, j, :], acc[:, j, :], pd[:, j % 2, :], ALU.add).then_inc(S["acc_done"], 1)
                    if last and j >= 2:
                        gated(j - 2)

            def gated(j):
                if j == 0:
                    dve.wait_ge(S["gate_loaded"], 32)
                dve.wait_ge(S["rms"], j + 1)
                dve.wait_ge(S["squared"], j + 1)
                dve.scalar_tensor_tensor(out=acc[:, j, :], in0=acc[:, j, :], scalar=rs[:, j:j + 1],
                                         in1=gate[0 if j < TX else 1], op0=ALU.mult, op1=ALU.mult
                                         ).then_inc(S["gated"], 1)

            for name in ("prod_done", "g_lo_done", "acc_done"):
                dve.nop().then_inc(S[name], CREDIT)
            dve.wait_ge(S["zeroed"], 1)
            for p in range(2, 6):
                split(dve, p, None, False)
            with dve.Fori(0, PAIRS - 1) as i:
                turn(i, False)
            turn(PAIRS - 1, True)
            gated(NT - 2)
            gated(NT - 1)


def trunk(nc, t, out):
    dr = {
        "T": nc.dram_tensor("rows_T", (2, R_ALL, TOK), F32, kind="Internal").ap(),
        "V": nc.dram_tensor("values", (2, TOK, VW), F32, kind="Internal").ap(),
        "mix": nc.dram_tensor("mix_T", (2, D, TOK), F32, kind="Internal").ap(),
        "x": nc.dram_tensor("residual", (TOK, D), F32, kind="Internal").ap(),
        "x1": nc.dram_tensor("residual_mid", (TOK, D), F32, kind="Internal").ap(),
        "gate": nc.dram_tensor("gates", (DEPTH, 2, 2, D), F32, kind="Internal").ap(),
        "ones": nc.dram_tensor("ones_row", (1, TOK), F32, kind="Internal").ap(),
    }
    with ExitStack() as ctx:
        s = Scope(nc, ctx, "keep")
        keep = {
            "vecs_loaded": s.sem("vecs_loaded"),
            "ident": s.sb("ident", [P, P]), "identb": s.sb("identb", [P, P], BF16),
            "above": s.sb("above", [P, P], BF16), "below": s.sb("below", [P, P], BF16),
            "eps": s.sb("eps", [P, 1]), "mhalf": s.sb("mhalf", [P, 4]),
            "modT": s.sb("modT", [P, DEPTH, 4, KT, 2]), "cnorm": s.sb("cnorm", [P, DEPTH, 3]),
            "neglam": s.sb("neglam", [P, DEPTH]), "dsn": s.sb("dsn", [64, DEPTH]),
            "sink": s.sb("sink", [P, DEPTH, 6]), "sinkdiv": s.sb("sinkdiv", [P, DEPTH, 6]),
        }
        modulation(nc, t, dr, keep)
        for l in range(DEPTH):
            project(nc, t, dr, keep, l)
            attend(nc, t, dr, keep, l)
            NT = TT if l < DEPTH - 1 else TX
            with ExitStack() as ffn_ctx:
                f = Scope(nc, ffn_ctx, f"h{l}")
                h_hi, h_lo = f.sb("hi", [P, KT, NT * P], F32R), f.sb("lo", [P, KT, NT * P], F32R)
                mix_out(nc, t, dr, keep, l, h_hi, h_lo)
                acc = f.sb("acc", [P, NT, D])
                ffn(nc, t, dr, keep, l, h_hi, h_lo, acc, out)


_INS = ["x", "c", "ctx", "c_ctx", "w_ada", "b_ada", "g_pre_mix", "g_post_mix", "w_in", "win_sink",
        "diff_lambda_q1", "diff_lambda_k1", "diff_lambda_q2", "diff_lambda_k2", "diff_sub_norm",
        "mla_q_norm", "mla_w_q_up", "mla_kv_norm", "mla_w_kv_up", "w_out",
        "g_pre_ffn", "g_post_ffn", "w_gate", "w_up", "w_down"]


def rotary_table(dim):
    half = dim // 2
    pos = np.arange(SEQ)
    freqs = (np.float32(10000.0) ** (-np.arange(0, half, 2, dtype=np.float32) / np.float32(half))).astype(np.float32)
    table = np.zeros((2, SEQ, dim), np.float32)
    for a, p in enumerate((pos // GRID_W, pos % GRID_W)):
        ang = p.astype(np.float32)[:, None] * freqs[None, :]
        cos, sin = np.cos(ang), np.sin(ang)
        o = a * half
        table[0, :, o:o + half] = np.concatenate([cos, cos], 1)
        table[1, :, o:o + half] = np.concatenate([-sin, sin], 1)
    return np.ascontiguousarray(table.reshape(2, TX, P, dim).transpose(2, 0, 1, 3))


def kernel(**inputs):
    import concourse.bacc as bacc
    from concourse.bass_utils import run_bass_kernel_spmd

    nc = bacc.Bacc("TRN2", target_bir_lowering=False, num_devices=1)
    arrays, t = {}, {}
    given = {name: np.ascontiguousarray(inputs[name]) for name in _INS}
    given["rot64"], given["rot32"] = rotary_table(64), rotary_table(32)
    for name, a in given.items():
        arrays[f"in_{name}"] = a
        t[name] = nc.dram_tensor(f"in_{name}", a.shape, mybir.dt.from_np(a.dtype), kind="ExternalInput").ap()
    out = nc.dram_tensor("out_x", (1, SEQ, D), F32, kind="ExternalOutput").ap()
    trunk(nc, t, out)
    r = run_bass_kernel_spmd(nc, [arrays], core_ids=[0])
    return r.results[0]["out_x"]
```
